# Optimizing a Trainium2 kernel written in Bass

```python
import math
import jax, jax.numpy as jnp
from jax import lax
import numpy as np

D_MODEL = 1024
BATCH = 1
SEQ = 256
DEPTH = 1

MEM_LEN = 256
EPS = 1e-6
S5_WIDTH = 512
S5_GROUP = 16
S5_GROUPS = S5_WIDTH // S5_GROUP
S5_STATE = 64
SGU_WIDTH = 1024
SGU_HEADS = 8
SGU_HEAD_DIM = SGU_WIDTH // SGU_HEADS
CHUNK = 128
XATTN_HEADS = 4
XATTN_HEAD_DIM = D_MODEL // XATTN_HEADS
D_FF = ((8 * D_MODEL // 3 + 255) // 256) * 256
OFF_U = S5_WIDTH
OFF_V = OFF_U + SGU_WIDTH
OFF_GA = OFF_V + SGU_WIDTH
OFF_GB = OFF_GA + D_MODEL
IN_COLS = OFF_GB + D_MODEL


def rms_norm(x, g):
    xf = x.astype(jnp.float32)
    y = xf * lax.rsqrt(jnp.mean(xf * xf, axis=-1, keepdims=True) + EPS)
    return (y * g.astype(jnp.float32)).astype(x.dtype)

def layer_norm(x, g, b):
    xf = x.astype(jnp.float32)
    mu = jnp.mean(xf, axis=-1, keepdims=True)
    xc = xf - mu
    y = xc * lax.rsqrt(jnp.mean(xc * xc, axis=-1, keepdims=True) + EPS)
    return (y * g.astype(jnp.float32) + b.astype(jnp.float32)).astype(x.dtype)

def _linear_recurrence(e1, e2):
    a1, b1 = e1
    a2, b2 = e2
    return a1 * a2, a2 * b1 + b2

def s5_scan(u, lam_re, lam_im, log_step, b_re, b_im, c_re, c_im, reverse):
    f32 = jnp.float32
    seq = u.shape[0]
    lam = lax.complex(lam_re.astype(f32), lam_im.astype(f32))
    step = jnp.exp(log_step.astype(f32))[:, None]
    lam_bar = jnp.exp(lam * step)
    b = lax.complex(b_re.astype(f32), b_im.astype(f32))
    b_bar = ((lam_bar - 1.0) / lam)[..., None] * b
    bu = jnp.einsum('gpc,lbgc->lbgp', b_bar, u.astype(jnp.complex64))
    a = jnp.broadcast_to(lam_bar[None, None], (seq, 1) + lam_bar.shape)
    _, states = lax.associative_scan(_linear_recurrence, (a, bu), axis=0, reverse=reverse)
    c = lax.complex(c_re.astype(f32), c_im.astype(f32))
    return jnp.einsum('gcp,lbgp->lbgc', c, states).real

def s5_branch(xa, lam_re, lam_im, log_step, b_re, b_im, c_re, c_im, d, w_glu):
    f32 = jnp.float32
    bsz, seq, _ = xa.shape
    u = xa.astype(f32).reshape(bsz, seq, S5_GROUPS, S5_GROUP).transpose(1, 0, 2, 3)
    y = d.astype(f32).reshape(S5_GROUPS, S5_GROUP) * u
    for direction, reverse in ((0, False), (1, True)):
        y = y + s5_scan(u, lam_re[direction], lam_im[direction], log_step[direction],
                        b_re[direction], b_im[direction], c_re[direction], c_im[direction],
                        reverse)
    y = jax.nn.gelu(y.transpose(1, 0, 2, 3).reshape(bsz, seq, S5_WIDTH))
    y = y * jax.nn.sigmoid(y @ w_glu.astype(f32))
    return y.astype(xa.dtype)

def sgu_branch(zu, zv, ln_g, ln_b, w_s, bias):
    bsz, seq, _ = zu.shape
    zu = jax.nn.gelu(zu)
    zv = layer_norm(jax.nn.gelu(zv), ln_g, ln_b)
    zv = zv.reshape(bsz, seq // CHUNK, CHUNK, SGU_HEADS, SGU_HEAD_DIM)
    sv = jnp.einsum('hts,bnshd->bnthd', w_s, zv) + bias.T[None, None, :, :, None]
    return zu * sv.reshape(bsz, seq, SGU_WIDTH)

def memory_cross_attention(hn, memn, w_q, w_k, w_v, w_o):
    bsz, seq, _ = hn.shape
    q = (hn @ w_q).reshape(bsz, seq, XATTN_HEADS, XATTN_HEAD_DIM)
    k = (memn @ w_k).reshape(bsz, MEM_LEN, XATTN_HEADS, XATTN_HEAD_DIM)
    v = (memn @ w_v).reshape(bsz, MEM_LEN, XATTN_HEADS, XATTN_HEAD_DIM)
    s = jnp.einsum('blhd,bmhd->bhlm', q, k).astype(jnp.float32) * (XATTN_HEAD_DIM ** -0.5)
    p = jax.nn.softmax(s, axis=-1).astype(v.dtype)
    o = jnp.einsum('bhlm,bmhd->blhd', p, v).reshape(bsz, seq, D_MODEL)
    return o @ w_o

def swiglu(hn, w_gate, w_up, w_down):
    return (jax.nn.silu(hn @ w_gate) * (hn @ w_up)) @ w_down

def first_inputs(seed: int = 0) -> dict:
    key = jax.random.key(seed)
    ks = iter(jax.random.split(key, 40))
    f32 = jnp.float32

    def nrm(shape, scale):
        return jax.random.normal(next(ks), shape, f32) * scale

    def gain(shape):
        return 1.0 + nrm(shape, 0.02)

    L, G, P, C, H = DEPTH, S5_GROUPS, S5_STATE, S5_GROUP, SGU_HEADS
    n_idx = jnp.arange(P, dtype=f32)
    lam_re = -0.5 + nrm((L, 2, G, P), 0.01)
    lam_im = math.pi * n_idx + nrm((L, 2, G, P), 0.01)
    log_step = jax.random.uniform(next(ks), (L, 2, G), f32, math.log(1e-3), math.log(1e-1))
    return {
        "x": nrm((BATCH, SEQ, D_MODEL), 1.0),
        "mem": nrm((BATCH, MEM_LEN, D_MODEL), 1.0),
        "mix_norm_g": gain((L, D_MODEL)),
        "w_in": nrm((L, D_MODEL, IN_COLS), D_MODEL ** -0.5),
        "s5_lam_re": lam_re,
        "s5_lam_im": lam_im,
        "s5_log_step": log_step,
        "s5_b_re": nrm((L, 2, G, P, C), (2 * C) ** -0.5),
        "s5_b_im": nrm((L, 2, G, P, C), (2 * C) ** -0.5),
        "s5_c_re": nrm((L, 2, G, C, P), (2 * P) ** -0.5),
        "s5_c_im": nrm((L, 2, G, C, P), (2 * P) ** -0.5),
        "s5_d": nrm((L, S5_WIDTH), 1.0),
        "s5_w_glu": nrm((L, S5_WIDTH, S5_WIDTH), S5_WIDTH ** -0.5),
        "sgu_ln_g": gain((L, SGU_WIDTH)),
        "sgu_ln_b": nrm((L, SGU_WIDTH), 0.02),
        "sgu_w": nrm((L, H, CHUNK, CHUNK), 0.5 * CHUNK ** -0.5),
        "sgu_bias": 1.0 + nrm((L, H, CHUNK), 0.02),
        "w_proj_a": nrm((L, S5_WIDTH, D_MODEL), S5_WIDTH ** -0.5),
        "w_proj_b": nrm((L, SGU_WIDTH, D_MODEL), SGU_WIDTH ** -0.5),
        "w_out": nrm((L, D_MODEL, D_MODEL), D_MODEL ** -0.5),
        "xattn_norm_g": gain((L, D_MODEL)),
        "mem_norm_g": gain((D_MODEL,)),
        "w_q": nrm((L, D_MODEL, D_MODEL), D_MODEL ** -0.5),
        "w_k": nrm((L, D_MODEL, D_MODEL), D_MODEL ** -0.5),
        "w_v": nrm((L, D_MODEL, D_MODEL), D_MODEL ** -0.5),
        "w_xo": nrm((L, D_MODEL, D_MODEL), D_MODEL ** -0.5),
        "ffn_norm_g": gain((L, D_MODEL)),
        "w_gate": nrm((L, D_MODEL, D_FF), D_MODEL ** -0.5),
        "w_up": nrm((L, D_MODEL, D_FF), D_MODEL ** -0.5),
        "w_down": nrm((L, D_FF, D_MODEL), D_FF ** -0.5),
        "final_norm_g": gain((D_MODEL,)),
    }

def first_block(x, mem, mix_norm_g, w_in, s5_lam_re, s5_lam_im, s5_log_step, s5_b_re, s5_b_im,
              s5_c_re, s5_c_im, s5_d, s5_w_glu, sgu_ln_g, sgu_ln_b, sgu_w, sgu_bias,
              w_proj_a, w_proj_b, w_out, xattn_norm_g, mem_norm_g, w_q, w_k, w_v, w_xo,
              ffn_norm_g, w_gate, w_up, w_down, final_norm_g):
    memn = rms_norm(mem, mem_norm_g)
    h = x
    for i in range(DEPTH):
        n = rms_norm(h, mix_norm_g[i])
        proj = n @ w_in[i]
        xa = proj[..., :OFF_U]
        zu = proj[..., OFF_U:OFF_V]
        zv = proj[..., OFF_V:OFF_GA]
        gate_a = jax.nn.sigmoid(proj[..., OFF_GA:OFF_GB])
        gate_b = jax.nn.sigmoid(proj[..., OFF_GB:])
        ya = s5_branch(xa, s5_lam_re[i], s5_lam_im[i], s5_log_step[i], s5_b_re[i], s5_b_im[i],
                       s5_c_re[i], s5_c_im[i], s5_d[i], s5_w_glu[i])
        yb = sgu_branch(zu, zv, sgu_ln_g[i], sgu_ln_b[i], sgu_w[i], sgu_bias[i])
        merged = gate_a * (ya @ w_proj_a[i]) + gate_b * (yb @ w_proj_b[i])
        h = h + merged @ w_out[i]
        h = h + memory_cross_attention(rms_norm(h, xattn_norm_g[i]), memn,
                                       w_q[i], w_k[i], w_v[i], w_xo[i])
        h = h + swiglu(rms_norm(h, ffn_norm_g[i]), w_gate[i], w_up[i], w_down[i])
    return rms_norm(h, final_norm_g)


DEPTH_2 = 2

GRID_W = 64
CTX_LEN = 256
HEAD_DIM = 64
BRANCH_WIDTH = D_MODEL // 2
FOURIER_GROUP_DIM = 64
FOURIER_GROUPS = BRANCH_WIDTH // FOURIER_GROUP_DIM
CONV_WIDTH = BRANCH_WIDTH
CONV_KERNEL = 31
GQA_Q_HEADS = BRANCH_WIDTH // HEAD_DIM
GQA_GROUP = 4
GQA_KV_HEADS = GQA_Q_HEADS // GQA_GROUP
DIFF_QK_DIM = HEAD_DIM
DIFF_V_DIM = 2 * HEAD_DIM
DIFF_HEADS = BRANCH_WIDTH // DIFF_V_DIM
N_BRANCH = 4
FFN_HIDDEN = -(-8 * D_MODEL // (3 * 256)) * 256
ROPE_BASE = 10000.0
AXIS_ROT_DIM = HEAD_DIM // 2
Q_BLOCK = 128
LN_EPS = 1e-5

_IN_SIZES = (BRANCH_WIDTH,
             2 * CONV_WIDTH,
             GQA_Q_HEADS * HEAD_DIM,
             GQA_KV_HEADS * HEAD_DIM,
             GQA_KV_HEADS * HEAD_DIM,
             DIFF_HEADS * 2 * DIFF_QK_DIM,
             DIFF_HEADS * 2 * DIFF_QK_DIM,
             DIFF_HEADS * DIFF_V_DIM,
             N_BRANCH * D_MODEL)
IN_COLS_2 = sum(_IN_SIZES)
SPLIT_IDX = tuple(int(v) for v in np.cumsum(_IN_SIZES)[:-1])


def rms_norm_2(x, g):
    x32 = x.astype(jnp.float32)
    y = x32 * lax.rsqrt(jnp.mean(x32 * x32, axis=-1, keepdims=True) + EPS)
    return (y * g.astype(jnp.float32)).astype(x.dtype)

def layer_norm_2(x, g, b):
    x32 = x.astype(jnp.float32)
    mu = jnp.mean(x32, axis=-1, keepdims=True)
    var = jnp.mean(jnp.square(x32 - mu), axis=-1, keepdims=True)
    y = (x32 - mu) * lax.rsqrt(var + LN_EPS)
    return (y * g.astype(jnp.float32) + b.astype(jnp.float32)).astype(x.dtype)

def modulate(h, shift, scale):
    return h * (1.0 + scale) + shift

def axial_rope_tables(n_rows):
    row = jnp.repeat(jnp.arange(n_rows, dtype=jnp.float32), GRID_W)
    col = jnp.tile(jnp.arange(GRID_W, dtype=jnp.float32), n_rows)
    inv = ROPE_BASE ** (-jnp.arange(0, AXIS_ROT_DIM, 2, dtype=jnp.float32) / AXIS_ROT_DIM)
    ang = jnp.concatenate([row[:, None] * inv, col[:, None] * inv], axis=-1)
    return jnp.cos(ang), jnp.sin(ang)

def rope(x, cos, sin):
    half = x.shape[-1] // 2
    x32 = x.astype(jnp.float32)
    x1, x2 = x32[..., :half], x32[..., half:]
    return jnp.concatenate([x1 * cos - x2 * sin, x2 * cos + x1 * sin], axis=-1).astype(x.dtype)

def fourier_mix(z):
    b, l, _ = z.shape
    zg = z.reshape(b, l, FOURIER_GROUPS, FOURIER_GROUP_DIM).astype(jnp.float32)
    f = jnp.fft.fft2(zg, axes=(1, 3), norm="ortho").real
    return f.reshape(b, l, BRANCH_WIDTH).astype(z.dtype)

def conformer_conv(z, w, bias, ln_g, ln_b):
    a, g = jnp.split(z, 2, axis=-1)
    u = a * jax.nn.sigmoid(g)
    pad = CONV_KERNEL // 2
    y = lax.conv_general_dilated(u, w[:, None, :].astype(u.dtype), window_strides=(1,),
                                 padding=[(pad, pad)], dimension_numbers=("NWC", "WIO", "NWC"),
                                 feature_group_count=CONV_WIDTH) + bias
    return jax.nn.silu(layer_norm_2(y, ln_g, ln_b))

def gqa_q(zq, g, cos, sin):
    b, l, _ = zq.shape
    q = rms_norm_2(zq.reshape(b, l, GQA_Q_HEADS, HEAD_DIM), g).transpose(0, 2, 1, 3)
    if cos is not None:
        q = rope(q, cos, sin)
    return q.reshape(b, GQA_KV_HEADS, GQA_GROUP, l, HEAD_DIM)

def gqa_kv(zk, zv, g, cos, sin):
    b, l, _ = zk.shape
    k = rms_norm_2(zk.reshape(b, l, GQA_KV_HEADS, HEAD_DIM), g).transpose(0, 2, 1, 3)
    v = zv.reshape(b, l, GQA_KV_HEADS, HEAD_DIM).transpose(0, 2, 1, 3)
    if cos is not None:
        k = rope(k, cos, sin)
    return k, v

def diff_q(zq, cos, sin):
    b, l, _ = zq.shape
    q = zq.reshape(b, l, DIFF_HEADS, 2, DIFF_QK_DIM).transpose(0, 2, 3, 1, 4)
    if cos is not None:
        q = rope(q, cos, sin)
    return q

def diff_kv(zk, zv, cos, sin):
    b, l, _ = zk.shape
    k = zk.reshape(b, l, DIFF_HEADS, 2, DIFF_QK_DIM).transpose(0, 2, 3, 1, 4)
    v = zv.reshape(b, l, DIFF_HEADS, DIFF_V_DIM).transpose(0, 2, 1, 3)
    if cos is not None:
        k = rope(k, cos, sin)
    return k, v

def gqa_attend(q, k, v):
    s = jnp.einsum("bhgqd,bhkd->bhgqk", q, k).astype(jnp.float32) * (HEAD_DIM ** -0.5)
    p = jax.nn.softmax(s, axis=-1).astype(v.dtype)
    return jnp.einsum("bhgqk,bhkd->bhgqd", p, v)

def diff_attend(q, k, v, lam):
    s = jnp.einsum("bhmqd,bhmkd->bhmqk", q, k).astype(jnp.float32) * (DIFF_QK_DIM ** -0.5)
    p = jax.nn.softmax(s, axis=-1)
    w = (p[:, :, 0] - lam * p[:, :, 1]).astype(v.dtype)
    return jnp.einsum("bhqk,bhkd->bhqd", w, v)

def sweep_query_blocks(fn, q):
    *lead, s, d = q.shape
    nb = s // Q_BLOCK
    qb = jnp.moveaxis(q.reshape(*lead, nb, Q_BLOCK, d), -3, 0)
    out = jnp.moveaxis(lax.map(fn, qb), 0, -3)
    return out.reshape(*out.shape[:-3], s, out.shape[-1])

def gqa_merge(o):
    b, _, _, l, d = o.shape
    return o.reshape(b, GQA_Q_HEADS, l, d).transpose(0, 2, 1, 3).reshape(b, l, GQA_Q_HEADS * d)

def diff_merge(o, g, lam_init):
    b, h, l, dv = o.shape
    o = rms_norm_2(o, g) * (1.0 - lam_init)
    return o.transpose(0, 2, 1, 3).reshape(b, l, h * dv)

def context_keys_values(pc, lp):
    k, v = gqa_kv(pc[3], pc[4], lp["k_norm"], None, None)
    kd, vd = diff_kv(pc[6], pc[7], None, None)
    return (k, v, kd, vd)

def mixer_stream(parts, lp, cos, sin, ctx_kv, lam, lam_init):
    zf, zconv, zgq, zgk, zgv, zdq, zdk, zdv, zgate = parts
    y_four = fourier_mix(zf) @ lp["w_four"]
    y_conv = conformer_conv(zconv, lp["conv_w"], lp["conv_b"], lp["conv_ln_g"], lp["conv_ln_b"]) @ lp["w_conv"]
    q = gqa_q(zgq, lp["q_norm"], cos, sin)
    k, v = gqa_kv(zgk, zgv, lp["k_norm"], cos, sin)
    qd = diff_q(zdq, cos, sin)
    kd, vd = diff_kv(zdk, zdv, cos, sin)
    if ctx_kv is None:
        o_gqa = gqa_attend(q, k, v)
        o_diff = diff_attend(qd, kd, vd, lam)
    else:
        kc, vc, kdc, vdc = ctx_kv
        k_all = jnp.concatenate([k, kc], axis=2)
        v_all = jnp.concatenate([v, vc], axis=2)
        kd_all = jnp.concatenate([kd, kdc], axis=3)
        vd_all = jnp.concatenate([vd, vdc], axis=2)
        o_gqa = sweep_query_blocks(lambda qb: gqa_attend(qb, k_all, v_all), q)
        o_diff = sweep_query_blocks(lambda qb: diff_attend(qb, kd_all, vd_all, lam), qd)
    y_gqa = gqa_merge(o_gqa) @ lp["w_gqa"]
    y_diff = diff_merge(o_diff, lp["diff_norm"], lam_init) @ lp["w_diff"]
    b, l, _ = zgate.shape
    gates = jax.nn.sigmoid(zgate.reshape(b, l, N_BRANCH, D_MODEL))
    ys = jnp.stack([y_four, y_conv, y_gqa, y_diff], axis=2)
    return jnp.sum(gates * ys, axis=2) @ lp["w_out"]

def swiglu_2(h, w1, w3, w2):
    return (jax.nn.silu(h @ w1) * (h @ w3)) @ w2

def second_inputs(seed: int = 0) -> dict:
    key = jax.random.key(seed)
    ks = iter(jax.random.split(key, 40))

    def nrm(shape, scale):
        return scale * jax.random.normal(next(ks), shape, jnp.float32)

    def gain(shape):
        return 1.0 + nrm(shape, 0.02)

    L = DEPTH_2
    return {
        "x": nrm((BATCH, SEQ, D_MODEL), 1.0),
        "c": nrm((BATCH, D_MODEL), 1.0),
        "ctx": nrm((BATCH, CTX_LEN, D_MODEL), 1.0),
        "c_ctx": nrm((D_MODEL,), 1.0),
        "w_ada": nrm((L, D_MODEL, 6 * D_MODEL), 0.5 * D_MODEL ** -0.5),
        "b_ada": nrm((L, 6 * D_MODEL), 0.02),
        "norm_mix": gain((L, D_MODEL)),
        "w_in": nrm((L, D_MODEL, IN_COLS_2), D_MODEL ** -0.5),
        "w_four": nrm((L, BRANCH_WIDTH, D_MODEL), BRANCH_WIDTH ** -0.5),
        "conv_w": nrm((L, CONV_KERNEL, CONV_WIDTH), CONV_KERNEL ** -0.5),
        "conv_b": nrm((L, CONV_WIDTH), 0.02),
        "conv_ln_g": gain((L, CONV_WIDTH)),
        "conv_ln_b": nrm((L, CONV_WIDTH), 0.02),
        "w_conv": nrm((L, CONV_WIDTH, D_MODEL), CONV_WIDTH ** -0.5),
        "q_norm": gain((L, HEAD_DIM)),
        "k_norm": gain((L, HEAD_DIM)),
        "w_gqa": nrm((L, GQA_Q_HEADS * HEAD_DIM, D_MODEL), (GQA_Q_HEADS * HEAD_DIM) ** -0.5),
        "lam_q1": nrm((L, DIFF_QK_DIM), 0.1),
        "lam_k1": nrm((L, DIFF_QK_DIM), 0.1),
        "lam_q2": nrm((L, DIFF_QK_DIM), 0.1),
        "lam_k2": nrm((L, DIFF_QK_DIM), 0.1),
        "diff_norm": gain((L, DIFF_V_DIM)),
        "w_diff": nrm((L, DIFF_HEADS * DIFF_V_DIM, D_MODEL), (DIFF_HEADS * DIFF_V_DIM) ** -0.5),
        "w_out": nrm((L, D_MODEL, D_MODEL), D_MODEL ** -0.5),
        "norm_ffn": gain((L, D_MODEL)),
        "w_ffn1": nrm((L, D_MODEL, FFN_HIDDEN), D_MODEL ** -0.5),
        "w_ffn3": nrm((L, D_MODEL, FFN_HIDDEN), D_MODEL ** -0.5),
        "w_ffn2": nrm((L, FFN_HIDDEN, D_MODEL), FFN_HIDDEN ** -0.5),
        "final_norm": gain((D_MODEL,)),
    }

def second_block(x, c, ctx, c_ctx, w_ada, b_ada, norm_mix, w_in, w_four, conv_w, conv_b, conv_ln_g,
              conv_ln_b, w_conv, q_norm, k_norm, w_gqa, lam_q1, lam_k1, lam_q2, lam_k2, diff_norm,
              w_diff, w_out, norm_ffn, w_ffn1, w_ffn3, w_ffn2, final_norm):
    n_rows = x.shape[1] // GRID_W
    cos, sin = axial_rope_tables(n_rows)
    silu_c = jax.nn.silu(c)
    silu_cc = jax.nn.silu(c_ctx)
    for l in range(DEPTH_2):
        last = l == DEPTH_2 - 1
        lam_init = 0.8 - 0.6 * math.exp(-0.3 * l)
        lp = dict(w_four=w_four[l], conv_w=conv_w[l], conv_b=conv_b[l], conv_ln_g=conv_ln_g[l],
                  conv_ln_b=conv_ln_b[l], w_conv=w_conv[l], q_norm=q_norm[l], k_norm=k_norm[l],
                  w_gqa=w_gqa[l], diff_norm=diff_norm[l], w_diff=w_diff[l], w_out=w_out[l])
        mod_x = (silu_c @ w_ada[l] + b_ada[l])[:, None, :]
        sh_m, sc_m, g_m, sh_f, sc_f, g_f = jnp.split(mod_x, 6, axis=-1)
        mod_c = silu_cc @ w_ada[l] + b_ada[l]
        csh_m, csc_m, cg_m, csh_f, csc_f, cg_f = jnp.split(mod_c, 6, axis=-1)
        lam = (jnp.exp(jnp.sum(lam_q1[l].astype(jnp.float32) * lam_k1[l].astype(jnp.float32)))
               - jnp.exp(jnp.sum(lam_q2[l].astype(jnp.float32) * lam_k2[l].astype(jnp.float32)))
               + lam_init)
        hx = modulate(rms_norm_2(x, norm_mix[l]), sh_m, sc_m)
        hc = modulate(rms_norm_2(ctx, norm_mix[l]), csh_m, csc_m)
        px = jnp.split(hx @ w_in[l], SPLIT_IDX, axis=-1)
        pc = jnp.split(hc @ w_in[l], SPLIT_IDX, axis=-1)
        ctx_kv = context_keys_values(pc, lp)
        x = x + g_m * mixer_stream(px, lp, cos, sin, ctx_kv, lam, lam_init)
        if not last:
            ctx = ctx + cg_m * mixer_stream(pc, lp, None, None, None, lam, lam_init)
            ctx = ctx + cg_f * swiglu_2(modulate(rms_norm_2(ctx, norm_ffn[l]), csh_f, csc_f),
                                      w_ffn1[l], w_ffn3[l], w_ffn2[l])
        x = x + g_f * swiglu_2(modulate(rms_norm_2(x, norm_ffn[l]), sh_f, sc_f),
                             w_ffn1[l], w_ffn3[l], w_ffn2[l])
    return rms_norm_2(x, final_norm)


def setup_inputs(seed=0):
    out = dict(first_inputs(seed))
    for name, value in second_inputs(seed + 1).items():
        if name != "x":
            out[name + "_2"] = value
    return out


def reference(
    x, mem, mix_norm_g, w_in, s5_lam_re, s5_lam_im, s5_log_step, s5_b_re, s5_b_im, s5_c_re,
    s5_c_im, s5_d, s5_w_glu, sgu_ln_g, sgu_ln_b, sgu_w, sgu_bias, w_proj_a, w_proj_b, w_out,
    xattn_norm_g, mem_norm_g, w_q, w_k, w_v, w_xo, ffn_norm_g, w_gate, w_up, w_down,
    final_norm_g, c_2, ctx_2, c_ctx_2, w_ada_2, b_ada_2, norm_mix_2, w_in_2, w_four_2, conv_w_2,
    conv_b_2, conv_ln_g_2, conv_ln_b_2, w_conv_2, q_norm_2, k_norm_2, w_gqa_2, lam_q1_2,
    lam_k1_2, lam_q2_2, lam_k2_2, diff_norm_2, w_diff_2, w_out_2, norm_ffn_2, w_ffn1_2,
    w_ffn3_2, w_ffn2_2, final_norm_2,
):
    x = first_block(
        x, mem, mix_norm_g, w_in, s5_lam_re, s5_lam_im, s5_log_step, s5_b_re, s5_b_im, s5_c_re,
        s5_c_im, s5_d, s5_w_glu, sgu_ln_g, sgu_ln_b, sgu_w, sgu_bias, w_proj_a, w_proj_b, w_out,
        xattn_norm_g, mem_norm_g, w_q, w_k, w_v, w_xo, ffn_norm_g, w_gate, w_up, w_down,
        final_norm_g,
    )
    return second_block(
        x, c_2, ctx_2, c_ctx_2, w_ada_2, b_ada_2, norm_mix_2, w_in_2, w_four_2, conv_w_2,
        conv_b_2, conv_ln_g_2, conv_ln_b_2, w_conv_2, q_norm_2, k_norm_2, w_gqa_2, lam_q1_2,
        lam_k1_2, lam_q2_2, lam_k2_2, diff_norm_2, w_diff_2, w_out_2, norm_ffn_2, w_ffn1_2,
        w_ffn3_2, w_ffn2_2, final_norm_2,
    )


_drawn_inputs = setup_inputs


def setup_inputs(seed=0):
    import zlib

    import numpy as np

    out = dict(_drawn_inputs(seed))
    spreads = {}
    factors = {'mix_norm_g': 4.762,
     's5_lam_re': 8.0,
     's5_lam_im': 3.506,
     's5_log_step': 3.547,
     's5_b_re': 4.925,
     's5_b_im': 4.935,
     's5_c_re': 4.946,
     's5_c_im': 4.872,
     'sgu_ln_g': 8.0,
     'sgu_ln_b': 8.0,
     'sgu_bias': 7.574,
     'xattn_norm_g': 8.0,
     'mem_norm_g': 8.0,
     'ffn_norm_g': 3.892,
     'norm_mix_2': 8.0,
     'conv_b_2': 8.0,
     'conv_ln_g_2': 8.0,
     'conv_ln_b_2': 8.0,
     'q_norm_2': 8.0,
     'k_norm_2': 8.0,
     'lam_q1_2': 4.222,
     'lam_k1_2': 3.076,
     'lam_q2_2': 3.802,
     'lam_k2_2': 5.47,
     'diff_norm_2': 8.0,
     'norm_ffn_2': 6.851,
     'final_norm_2': 2.904}
    for name, (base, spread) in spreads.items():
        noise = np.random.default_rng([zlib.crc32(name.encode()), seed]).standard_normal(out[name].shape)
        drawn = base * np.exp(spread * noise) if base else spread * noise
        out[name] = __import__('jax').numpy.asarray(drawn.astype(out[name].dtype))
    for name, factor in factors.items():
        out[name] = (out[name] * factor).astype(out[name].dtype)
    return out
```

```python
from contextlib import ExitStack

import concourse.bass as bass
from concourse import mybir
import numpy as np

F32 = mybir.dt.float32
F32R = mybir.dt.float32r
ALU = mybir.AluOpType
ACT = mybir.ActivationFunctionType
AX = mybir.AxisListType

P = 128
T = 256
D = 1024
DC = D // P
HALF = 512
HC = HALF // P
F = 2816
FC = F // P
GROUPS, STATE, CH = 32, 64, 16
TILES = 2 * GROUPS // 2
SGU_HEADS = 8
CHUNK = 128
MEM_HEADS = 4
TAPS = 31
PAD = TAPS // 2
HEAD = 64
DIFF_HEADS = 4
LAYERS = 2
EPS = 1e-6
LN_EPS = 1e-5
UNIT = 2048
RAW = 4
REST = 2
LAM_INIT = [0.8 - 0.6 * float(np.exp(-0.3 * l)) for l in range(LAYERS)]
ADA_GROUPS = 6

COLS = {}


def _place_columns():
    at = 0
    for name, rows in (("mix_norm_g", 8), ("mem_norm_g", 8), ("xattn_norm_g", 8), ("ffn_norm_g", 8),
                       ("final_norm_g", 8), ("norm_mix_2", 16), ("norm_ffn_2", 16), ("final_norm_2", 8),
                       ("c_2", 8), ("c_ctx_2", 8), ("s5_d", 4), ("conv_b_2", 8), ("conv_ln_g_2", 8),
                       ("conv_ln_b_2", 8)):
        COLS[name] = at
        at += rows
    return at


NVEC = _place_columns()


def schedule():
    s = [("mem_k", 4), ("mem_v", 4), ("xa", 2), ("ADA", 0),
         ("zv", 4), ("zu", 4), ("gate_a", 4), ("glu", 1), ("proj_a", 2), ("gate_b", 4), ("proj_b", 4),
         ("out", 4), ("mem_q", 4), ("mem_o", 4), ("ffn_up", 22), ("ffn_down", 11)]
    for p in ("c0", "x0", "c1", "x1"):
        if p == "c1":
            s += [(p + k, n) for k, n in (("kv", 1), ("dk", 2), ("dv", 2))]
        else:
            s += [(p + k, n) for k, n in (
                ("four", 2), ("conv_u", 2), ("conv_g", 2), ("q", 2), ("kv", 1), ("dq", 2), ("dk", 2), ("dv", 2),
                ("gate0", 4), ("proj0", 2), ("gate1", 4), ("proj1", 2), ("gate2", 4), ("proj2", 2),
                ("gate3", 4), ("proj3", 2), ("out", 4), ("ffn_up", 22), ("ffn_down", 11))]
    return s


ROW_KIND = ("proj_a", "proj0", "proj1", "proj2", "proj3", "ffn_down")


def row_kind(name):
    return name in ROW_KIND or name[2:] in ROW_KIND


FIRST, COUNT, BANK_USES = {}, {}, {}


def _number_units():
    at, uses = 0, [0] * 4
    for name, n in schedule():
        if name == "ADA":
            continue
        FIRST[name], COUNT[name], BANK_USES[name] = at, n, list(uses)
        at += n
        if row_kind(name):
            uses = [x + 1 for x in uses]
        elif name == "glu":
            uses = [uses[0] + 1, uses[1] + 1, uses[2], uses[3]]
        else:
            uses = [x + (n - b + 3) // 4 for b, x in enumerate(uses)]
    return at


UNITS = _number_units()
BEFORE_ADA = FIRST["zv"]
ADA_UNITS = LAYERS * 3 * DC


class Unit:

    def __init__(self, first, turn=0):
        self.first, self.turn = first, turn

    def plus(self, k):
        return Unit(self.first + k, self.turn)

    def count(self, k=0):
        return self.first + 4 * self.turn + k

    def quarter(self):
        at = self.first + (ADA_UNITS if self.first >= BEFORE_ADA else 0)
        return at // 4 + 1 + self.turn


def build(nc, t, out, consts):
    ctx = ExitStack()
    with ctx:
        def sb(name, shape, dt=F32):
            return ctx.enter_context(nc.sbuf_tensor(name, shape, dt))

        def sem(name):
            return ctx.enter_context(nc.semaphore(name))

        raw = sb("raw", [P, RAW, UNIT])
        w_high = sb("w_high", [P, RAW, UNIT], F32R)
        w_rest = sb("w_rest", [P, REST, UNIT], F32R)
        n_high = sb("n_high", [P, DC, T], F32R)
        n_rest = sb("n_rest", [P, DC, T], F32R)
        hx = sb("hx", [P, DC, T])
        hc = sb("hc", [P, DC, T])
        kv = sb("kv", [P, 5632])
        ident = sb("ident", [P, P])
        dft64 = sb("dft64", [P, 2 * P])
        rope = sb("rope", [P, 2, T])
        ada_rows = sb("ada_rows", [96, LAYERS, P])
        b_ada = sb("b_ada", [P, LAYERS, 48])
        swap = sb("swap", [P, P])
        dup = sb("dup", [P, 2, P])
        pair_ones = sb("pair_ones", [P, P])
        ones = sb("ones", [P, P])
        one_row = sb("one_row", [1, P])
        masks = sb("masks", [P, 4])
        cols = sb("cols", [P, NVEC])
        cols2 = sb("cols2", [P, 6])
        tapc = sb("tapc", [P, LAYERS, TAPS * HC])
        mod = sb("mod", [P, LAYERS, 96])
        modg = sb("modg", [P, LAYERS, 2, 2, DC])
        silu_c = sb("silu_c", [P, DC, 2])
        flat = sb("flat", [P, 2])
        lam = sb("lam", [P, LAYERS, 8])
        stats = sb("stats", [P, 2, 8])
        soft = sb("soft", [P, 4, 4])
        rstd = sb("rstd", [P, T])
        m = sb("m", [P, DC, T])
        gate = sb("gate", [P, DC, T])

        over = ExitStack()
        with over:
            hid_high = over.enter_context(nc.sbuf_tensor("hid_high", [P, FC, T], F32R))
            hid_rest = over.enter_context(nc.sbuf_tensor("hid_rest", [P, FC, T], F32R))
        over = ExitStack()
        with over:
            b_high = over.enter_context(nc.sbuf_tensor("b_high", [P, HC, T], F32R))
            b_rest = over.enter_context(nc.sbuf_tensor("b_rest", [P, HC, T], F32R))
            work = over.enter_context(nc.sbuf_tensor("work", [P, 9216], F32))
        over = ExitStack()
        with over:
            s5w = over.enter_context(nc.sbuf_tensor("s5w", [P, 11264], F32))

        conv_in = work[:, 0:HC * (T + 2 * PAD)].rearrange("p (c t) -> p c t", c=HC)
        acc = work[:, 1152:2176].rearrange("p (c t) -> p c t", c=HC)
        qk = work[:, 2176:3456].rearrange("p (c t) -> p c t", c=HC + 1)
        dq = work[:, 3456:4480].rearrange("p (c t) -> p c t", c=HC)
        t1 = work[:, 4480:5760].rearrange("p (c t) -> p c t", c=HC + 1)
        t2 = work[:, 5760:7040].rearrange("p (c t) -> p c t", c=HC + 1)
        oT = work[:, 7040:8064].rearrange("p (c t) -> p c t", c=HC)
        dft256 = work[:, 8064:9088].rearrange("p (s l k) -> p s l k", s=2, l=2)
        zu = work[:, 0:2048].rearrange("p (c t) -> p c t", c=DC)
        zv = work[:, 2048:4096].rearrange("p (a n) -> p a n", a=2)
        o_mem = work[:, 2048:4096].rearrange("p (c t) -> p c t", c=DC)
        sgu_wt = work[:, 7040:8064].rearrange("p (h t) -> p h t", h=SGU_HEADS)
        sgu_raw = work[:, 4480:5504].rearrange("p (h t) -> p h t", h=SGU_HEADS)
        sgu_b = work[0:1, 8064:9088]
        mem_kT = kv[:, 0:2048].rearrange("p (c t) -> p c t", c=DC)
        mem_v = kv[:, 2048:4096].rearrange("p (a n) -> p a n", a=2)
        kdup = kv[:, 0:1024].rearrange("p (h t) -> p h t", h=2)
        vrow = kv[:, 1024:1536].rearrange("p (a n) -> p a n", a=4)
        kdT = kv[:, 1536:3584].rearrange("p (h t) -> p h t", h=HC)
        vdrow = kv[:, 3584:5632].rearrange("p (a n) -> p a n", a=4)
        ex = work[:, 4480:5504].rearrange("p (a n) -> p a n", a=2)
        exT = work[:, 5760:6784].rearrange("p (a n) -> p a n", a=4)

        def s5a(i):
            return s5w[:, 1024 * i:1024 * (i + 1)]
        q4 = "p (r t) -> p r t"
        tab_c = [s5a(0).rearrange(q4, r=4), s5a(2).rearrange(q4, r=4)]
        tab_s = [s5a(1).rearrange(q4, r=4), s5a(3).rearrange(q4, r=4)]
        z1, z2, z3, z4 = (m[:, 0:4, :], m[:, 4:8, :], gate[:, 0:4, :], gate[:, 4:8, :])
        z5, z6 = s5a(4).rearrange(q4, r=4), s5a(5).rearrange(q4, r=4)
        BT = s5w[:, 6144:8192].rearrange("p (i n k) -> p i n k", i=2, n=8)
        CT = s5w[:, 8192:10240].rearrange("p (i n k) -> p i n k", i=2, n=8)
        hi_c = s5w[:, 10240:10752].rearrange("p (n k) -> p n k", n=TILES)
        hi_s = s5w[:, 10752:11264].rearrange("p (n k) -> p n k", n=TILES)
        lo_c = kv[:, 4096:4608].rearrange("p (n k) -> p n k", n=TILES)
        lo_s = kv[:, 4608:5120].rearrange("p (n k) -> p n k", n=TILES)
        s5c = kv[:, 5120:5280].rearrange("p (i n) -> p i n", i=5)
        pw = kv[:, 5280:5472].rearrange("p (i n) -> p i n", i=6)
        xaT, xaR, yT = hc[:, 0:4, :], hc[:, 4:8, :], hc[:, 4:8, :]
        braw = s5w[:, 0:1024].rearrange("p (i n c) -> p i n c", i=2, n=TILES)
        bbar = s5w[:, 1024:2048].rearrange("p (i n c) -> p i n c", i=2, n=TILES)
        btmp = s5w[:, 2048:2560].rearrange("p (n c) -> p n c", n=TILES)
        craw = s5w[:, 3072:4096].rearrange("p (i n k) -> p i n k", i=2, n=8)
        bblk = m[:, :, :].rearrange("p a t -> p (a t)").rearrange("p (i n g c) -> p i n g c", i=2, n=TILES, g=2)
        cblk = gate[:, :, :].rearrange("p a t -> p (a t)").rearrange("p (i n g k) -> p i n g k", i=2, n=8, g=2)
        rows = s5w[0:TILES, 4096:4096 + 16 * P].rearrange("p (i k) -> p i k", i=16)

        L = ctx.enter_context(nc.psum_tensor("L", [P, 4, 512], F32))
        M = ctx.enter_context(nc.psum_tensor("M", [P, 4, 512], F32))

        landed = [sem(f"landed{i}") for i in range(RAW)]
        high_ready, rest_ready, unit_done, ada_done = sem("high_ready"), sem("rest_ready"), sem("unit_done"), sem("ada_done")
        bank_free = [sem(f"bank_free{i}") for i in range(4)]
        consts_in, params_in, s5_in, tokens_in = sem("consts_in"), sem("params_in"), sem("s5_in"), sem("tokens_in")
        rows_in, sgu_in, dft_in, lam_in = sem("rows_in"), sem("sgu_in"), sem("dft_in"), sem("lam_in")
        flats_set, dve_step, act_step, pool_step = sem("flats_set"), sem("dve_step"), sem("act_step"), sem("pool_step")
        turned, turned_out = sem("turned"), sem("turned_out")
        sq_ready, sum_ready, ms_ready, root_ready, scaled, n_high_ready, n_ready = [
            sem(x) for x in ("sq_ready", "sum_ready", "ms_ready", "root_ready", "scaled", "n_high_ready", "n_ready")]
        ada_row, ada_rows_in, mod_ready = sem("ada_row"), sem("ada_rows_in"), sem("mod_ready")
        silu_ready = sem("silu_ready")
        s5_act_in, s5_act, s5_coef_rows, s5_coef, s5_blk, s5_pow, s5_tab = [
            sem(x) for x in ("s5_act_in", "s5_act", "s5_coef_rows", "s5_coef", "s5_blk", "s5_pow", "s5_tab")]
        s5_bt, s5_bu, s5_rot, s5_sum, s5_w, s5_y, s5_yout, xa_ready = [
            sem(x) for x in ("s5_bt", "s5_bu", "s5_rot", "s5_sum", "s5_w", "s5_y", "s5_yout", "xa_ready")]
        gelu_y, branch_ready, glu_sig, gate_ready, merged = [
            sem(x) for x in ("gelu_y", "branch_ready", "glu_sig", "gate_ready", "merged")]
        zv_ready, zu_ready, ln_sum, ln_sq, ln_root, ln_ready, sgu_mm, sgu_out, m_split = [
            sem(x) for x in ("zv_ready", "zu_ready", "ln_sum", "ln_sq", "ln_root", "ln_ready", "sgu_mm", "sgu_out", "m_split")]
        h_ready, q_ready, k_ready, v_ready, scores, neg_max, expd, probs, probs_T, probs_Tc, attended, o_ready = [
            sem(x) for x in ("h_ready", "q_ready", "k_ready", "v_ready", "scores", "neg_max", "expd", "probs",
                             "probs_T", "probs_Tc", "attended", "o_ready")]
        up_act, hid_ready = sem("up_act"), sem("hid_ready")
        z_ready, four1, four1c, four2 = sem("z_ready"), sem("four1"), sem("four1c"), sem("four2")
        conv_a, conv_sig, conv_step, conv_st, conv_stc, conv_root, conv_n = [
            sem(x) for x in ("conv_a", "conv_sig", "conv_step", "conv_st", "conv_stc", "conv_root", "conv_n")]
        qk_raw, qk_sq, qk_sum, qk_ms, qk_root, qk_n, qk_rot, dq_raw, d_rot, kd_dup, kd_dupc = [
            sem(x) for x in ("qk_raw", "qk_sq", "qk_sum", "qk_ms", "qk_root", "qk_n", "qk_rot", "dq_raw", "d_rot",
                             "kd_dup", "kd_dupc")]
        on_sq, on_sum, on_ms, on_root = sem("on_sq"), sem("on_sum"), sem("on_ms"), sem("on_root")
        lam_dot, lam_exp = sem("lam_dot"), sem("lam_exp")
        stored = sem("stored")

        block = ctx.enter_context(nc.Block())

        def col(name, c, n=1):
            return cols[:, COLS[name] + c:COLS[name] + c + n]

        def each_unit(eng, name, body, start=0):
            first, n = FIRST[name] + start, COUNT[name] - start
            turns = n // 4
            if turns > 1:
                with eng.Fori(0, turns) as i:
                    for k in range(4):
                        body(Unit(first + k, i), start + 4 * i + k, k)
            else:
                turns = 0
            for k in range(4 * turns, n):
                body(Unit(first + k), start + k, k)

        def uses(name, k, turn=0):
            return BANK_USES[name][k % 4] + k // 4 + turn

        def split_high(act, u):
            act.wait_ge(landed[u.first % 4 if u.first < BEFORE_ADA else (u.first + ADA_UNITS) % 4], 16 * u.quarter())
            if u.first >= 4:
                act.wait_ge(unit_done, u.count(-3))
            nc.scalar.activation(w_high[:, u.first % 4, :], raw[:, u.first % 4, :], ACT.Copy).then_inc(high_ready, 1)

        def split_rest(dve, u):
            dve.wait_ge(high_ready, u.count(1))
            if u.first >= 2:
                dve.wait_ge(unit_done, u.count(-1))
            nc.vector.tensor_tensor(w_rest[:, u.first % 2, :], raw[:, u.first % 4, :],
                                    w_high[:, u.first % 4, :].bitcast(F32), ALU.subtract).then_inc(rest_ready, 1)

        def ahead_high(act, u, last):
            if u.first + 3 < last:
                split_high(act, u.plus(3))

        def ahead_rest(dve, u, last):
            if u.first + 1 < last:
                split_rest(dve, u.plus(1))

        def last_of(name):
            return BEFORE_ADA if FIRST[name] < BEFORE_ADA else UNITS


        @block.sync
        def _(sp):
            for k, (name, dst) in enumerate((("ident", ident), ("dft64", dft64), ("swap", swap),
                                             ("pair_ones", pair_ones), ("masks", masks))):
                sp.dma_start(dst[:, :], consts[name]).then_inc(consts_in, 16)
            sp.dma_start(dup[:, :, :], consts["dup"].rearrange("p (a k) -> p a k", a=2)).then_inc(consts_in, 16)
            sp.dma_start(gate[:, :, :].rearrange("p a t -> p (a t)").rearrange("p (a n) -> p a n", a=2),
                         t["mem"][0].rearrange("(a p) n -> p a n", p=P)).then_inc(tokens_in, 16)

            def rows_of(ap):
                return ap.rearrange("l (r k) -> (l r) k", k=P) if len(ap.shape) == 2 else ap.rearrange("(r k) -> r k", k=P)
            at = 0
            flat_m = m[:, :, :].rearrange("p a t -> p (a t)")
            for name in COLS:
                src = rows_of(t[name])
                sp.dma_start(flat_m[at:at + src.shape[0], 0:P], src).then_inc(params_in, 16)
                at += src.shape[0]
            sp.dma_start(flat_m[0:2, P:2 * P], t["diff_norm_2"]).then_inc(params_in, 16)
            for k, name in enumerate(("q_norm_2", "k_norm_2")):
                for h in range(2):
                    sp.dma_start(flat_m[2 + 2 * k:4 + 2 * k, P + h * HEAD:P + (h + 1) * HEAD], t[name]).then_inc(params_in, 16)
            for l in range(LAYERS):
                sp.dma_start(flat_m[0:TAPS * HC, (2 + l) * P:(3 + l) * P],
                             t["conv_w_2"][l].rearrange("k (c n) -> (k c) n", n=P)).then_inc(params_in, 16)
                sp.dma_start(flat_m[0:48, 1024 + l * P:1024 + (l + 1) * P],
                             t["b_ada_2"][l].rearrange("(r k) -> r k", k=P)).then_inc(params_in, 16)
            for k, name in enumerate(("lam_q1_2", "lam_k1_2", "lam_q2_2", "lam_k2_2")):
                for l in range(LAYERS):
                    sp.dma_start(flat_m[:, 512 + (4 * l + k) * HEAD:512 + (4 * l + k + 1) * HEAD],
                                 t[name][l:l + 1, :].partition_broadcast(P)).then_inc(lam_in, 16)

            def load(u, src, dst=None):
                slot = u.first % 4
                if u.first >= 4:
                    if BEFORE_ADA <= u.first < BEFORE_ADA + 4:
                        sp.wait_ge(ada_done, ADA_UNITS - 4 + u.first - BEFORE_ADA + 1)
                    else:
                        sp.wait_ge(rest_ready, u.count(-3))
                sp.dma_start(raw[:, slot, :] if dst is None else dst, src).then_inc(landed[slot], 16)

            def load_cols(name, w, at, step=256):
                wv = w.rearrange("(k p) n -> p k n", p=P)
                k = wv.shape[1]
                each_unit(sp, name, lambda u, j, _: load(
                    u, wv[:, :, bass.ds(at + step * j, step)],
                    raw[:, u.first % 4, :].rearrange("p (k n) -> p k n", k=k)))

            def load_rows(name, w):
                wv = w.rearrange("(k p) n -> p k n", p=P)
                each_unit(sp, name, lambda u, j, _: load(
                    u, wv[:, bass.ds(2 * j, 2), :], raw[:, u.first % 4, :].rearrange("p (k n) -> p k n", k=2)), start=0)

            def load_ffn(name, gate_w, up_w, down_w):
                gv, uv = (w.rearrange("(k p) n -> p k n", p=P) for w in (gate_w, up_w))

                def one(u, j, k):
                    half = (j - (k % 2)) * 128 if isinstance(j, int) else (u.turn * 512 + (k // 2) * 256)
                    load(u, (gv if k % 2 == 0 else uv)[:, :, bass.ds(half, 256)],
                         raw[:, u.first % 4, :].rearrange("p (k n) -> p k n", k=DC))
                each_unit(sp, name + "up", one)
                load_rows(name + "down", down_w)

            load_cols("mem_k", t["w_k"][0], 0)
            load_cols("mem_v", t["w_v"][0], 0)
            w_in = t["w_in"][0]
            load_cols("xa", w_in, 0)
            sp.wait_ge(h_ready, 1)
            sp.dma_start(gate[:, :, :].rearrange("p a t -> p (a t)").rearrange("p (a n) -> p a n", a=2),
                         t["x"][0].rearrange("(a p) n -> p a n", p=P)).then_inc(tokens_in, 16)
            for a in range(ADA_UNITS):
                v = BEFORE_ADA + a
                if a < 4:
                    sp.wait_ge(rest_ready, v - 3)
                else:
                    sp.wait_ge(ada_done, a - 3)
                l, g, k = a // 24, a // 8 % 3, a % 8
                sp.dma_start(raw[:, v % 4, :], t["w_ada_2"][l, k * P:(k + 1) * P, g * UNIT:(g + 1) * UNIT]).then_inc(landed[v % 4], 16)

            load_cols("zv", w_in, HALF + D)
            load_cols("zu", w_in, HALF)
            load_cols("gate_a", w_in, HALF + 2 * D)
            load(Unit(FIRST["glu"]), t["s5_w_glu"][0].rearrange("(k p) n -> p k n", p=P),
                 raw[:, FIRST["glu"] % 4, :].rearrange("p (k n) -> p k n", k=HC))
            load_rows("proj_a", t["w_proj_a"][0])
            load_cols("gate_b", w_in, HALF + 3 * D)
            load_cols("proj_b", t["w_proj_b"][0], 0)
            load_cols("out", t["w_out"][0], 0)
            load_cols("mem_q", t["w_q"][0], 0)
            load_cols("mem_o", t["w_xo"][0], 0)
            load_ffn("ffn_", t["w_gate"][0], t["w_up"][0], t["w_down"][0])
            for p, l in (("c0", 0), ("x0", 0), ("c1", 1), ("x1", 1)):
                w = t["w_in_2"][l]
                if p != "c1":
                    load_cols(p + "four", w, 0)
                    load_cols(p + "conv_u", w, 512)
                    load_cols(p + "conv_g", w, 1024)
                    load_cols(p + "q", w, 1536)
                load_cols(p + "kv", w, 2048)
                if p != "c1":
                    load_cols(p + "dq", w, 2304)
                load_cols(p + "dk", w, 2816)
                load_cols(p + "dv", w, 3328)
                if p == "c1":
                    continue
                for b, wb in enumerate(("w_four_2", "w_conv_2", "w_gqa_2", "w_diff_2")):
                    load_cols(p + f"gate{b}", w, 3840 + b * D)
                    load_rows(p + f"proj{b}", t[wb][l])
                load_cols(p + "out", t["w_out_2"][l], 0)
                load_ffn(p + "ffn_", t["w_ffn1_2"][l], t["w_ffn3_2"][l], t["w_ffn2_2"][l])

        PASSES = (("c0", 0, 1), ("x0", 0, 0), ("c1", 1, 1), ("x1", 1, 0))
        NORM_H = [1, 2, 3, 4, 5, 7, 8, 9, 10, 11, 11, 12, 13]
        NORM_OF = {"c0": 5, "x0": 7, "c1": 9, "x1": 10}
        FULL_OF = {"c0": 0, "x0": 1, "x1": 2}
        ROPE_OF = {"x0": 0, "x1": 1}
        HID_OF = {"": 0, "c0": 1, "x0": 2, "x1": 3}
        CONV_BASE = {p: TAPS * HC * i for p, i in FULL_OF.items()}
        SCALED = [DC * k for k in range(13)]
        NREADY = [1, 2, 3, 4, None, 5, 6, 7, 8, 9, 10, 11]
        NHIGH, NHIGH_EVENTS = {}, {}
        count = 0
        for x in (0, 1, "yb", "merged", 2, "o_mem", 3, 5, "c0", 6, 7, "x0", 8, 9, 10, "x1", 11):
            if isinstance(x, int):
                NHIGH[x] = count
                count += DC
            else:
                count += 1
                NHIGH_EVENTS[x] = count
        y1 = work[:, 4480:6528].rearrange("p (c a k) -> p c a k", c=HC, a=2)

        def after(name, b):
            n = COUNT[name]
            if row_kind(name):
                return BANK_USES[name][b] + 1
            if name == "glu":
                return BANK_USES[name][b] + (b < 2)
            return BANK_USES[name][b] + (n - b + 3) // 4

        def evacuated(eng, name):
            for b in range(4):
                eng.wait_ge(bank_free[b], after(name, b))

        def multiplied(eng, name):
            eng.wait_ge(unit_done, FIRST[name] + COUNT[name])

        TASKS = {}

        def _tasks():
            g = group = head = 0
            for key, heads, maps in [("mem", MEM_HEADS, 1)] + [(p + k, h, n) for p in ("c0", "x0", "x1")
                                                              for k, h, n in (("gqa", 8, 1), ("diff", DIFF_HEADS, 2))]:
                tasks = []
                for h in range(heads):
                    for qt in range(2):
                        for mp in range(maps):
                            tasks.append(dict(g=g, group=group, head=head, h=h, qt=qt, map=mp,
                                              whole=mp == maps - 1, end=mp == maps - 1 and qt == 1))
                            g += 1
                        group += 1
                    head += 1
                TASKS[key] = tasks
        _tasks()
        GROUP = [x["group"] for v in TASKS.values() for x in v]
        NHEADS = {k: v[-1]["head"] + 1 for k, v in TASKS.items()}
        ATT_SCALE = {"mem": float(D // MEM_HEADS) ** -0.5}

        def keys_of(key):
            return (0, T) if key == "mem" else (T, T) if key[0] == "c" else (0, 2 * T)

        def s5_tile(b):
            return 4 * (b % 4) + (16 if b < 4 else 0)

        @block.gpsimd
        def _(pool):
            n = [0]

            def link(ins):
                n[0] += 1
                ins.then_inc(pool_step, 1)
                pool.wait_ge(pool_step, n[0])

            def s5rows(name):
                return t[name].rearrange("o d (n g) p -> (o d n) (g p)", g=2)
            nc.gpsimd.memset(ones[:, :], 1.0).then_inc(flats_set, 1)
            nc.gpsimd.memset(one_row[:, :], 1.0).then_inc(flats_set, 1)
            nc.gpsimd.memset(flat[:, 0:1], 0.0).then_inc(flats_set, 1)
            nc.gpsimd.memset(flat[:, 1:2], 1.0).then_inc(flats_set, 1)
            pool.dma_start(rows[:, 0, :], s5rows("s5_lam_re")).then_inc(s5_in, 16)
            pool.dma_start(rows[:, 1, :], s5rows("s5_lam_im")).then_inc(s5_in, 16)
            pool.dma_start(rows[:, 2, 0:2], t["s5_log_step"].rearrange("o d (n g) -> (o d n) g", g=2)).then_inc(s5_in, 16)
            for i, (b, c) in enumerate((("s5_b_re", "s5_c_re"), ("s5_b_im", "s5_c_im"))):
                pool.dma_start(braw[:, i, :, :], t[b].rearrange("o d (n g) p c -> (g p) (o d n) c", g=2)).then_inc(s5_in, 16)
                pool.dma_start(craw[:, i, :, :], t[c].rearrange("o d (n g) c p -> (g c) (o d n) p", g=8)).then_inc(s5_in, 16)
            pool.wait_ge(s5_coef, 1)
            link(nc.gpsimd.tensor_copy(pw[:, 0, :], s5c[:, 1, :]))
            link(nc.gpsimd.tensor_copy(pw[:, 1, :], s5c[:, 2, :]))
            scr = s5w[:, 4096:5120]
            for tc_, ts_ in ((lo_c, lo_s), (hi_c, hi_s)):
                link(nc.gpsimd.memset(tc_[:, :, 0:1], 1.0))
                link(nc.gpsimd.memset(ts_[:, :, 0:1], 0.0))
                for k in range(4):
                    w = 1 << k
                    pc = pw[:, 0, :].unsqueeze(2).to_broadcast((P, TILES, w))
                    ps = pw[:, 1, :].unsqueeze(2).to_broadcast((P, TILES, w))
                    s1 = scr[:, 0:TILES * w].rearrange("p (n k) -> p n k", n=TILES)
                    s2 = scr[:, 512:512 + TILES * w].rearrange("p (n k) -> p n k", n=TILES)
                    link(nc.gpsimd.tensor_tensor(s1, tc_[:, :, 0:w], pc, ALU.mult))
                    link(nc.gpsimd.tensor_tensor(s2, ts_[:, :, 0:w], ps, ALU.mult))
                    link(nc.gpsimd.tensor_tensor(tc_[:, :, w:2 * w], s1, s2, ALU.subtract))
                    link(nc.gpsimd.tensor_tensor(s1, tc_[:, :, 0:w], ps, ALU.mult))
                    link(nc.gpsimd.tensor_tensor(s2, ts_[:, :, 0:w], pc, ALU.mult))
                    link(nc.gpsimd.tensor_tensor(ts_[:, :, w:2 * w], s1, s2, ALU.add))
                    link(nc.gpsimd.tensor_tensor(pw[:, 2, :], pw[:, 0, :], pw[:, 1, :], ALU.add))
                    link(nc.gpsimd.tensor_tensor(pw[:, 3, :], pw[:, 0, :], pw[:, 1, :], ALU.subtract))
                    link(nc.gpsimd.tensor_tensor(pw[:, 4, :], pw[:, 0, :], pw[:, 1, :], ALU.mult))
                    link(nc.gpsimd.tensor_tensor(pw[:, 0, :], pw[:, 2, :], pw[:, 3, :], ALU.mult))
                    link(nc.gpsimd.tensor_tensor(pw[:, 1, :], pw[:, 4, :], pw[:, 4, :], ALU.add))
            pool.wait_ge(s5_blk, 8)

            def make_table(b):
                if b >= 2:
                    pool.wait_ge(s5_w, b - 1)
                tile = s5_tile(b)
                hc_, hs_, lc_, ls_ = (x[:, tile:tile + 4, :] for x in (hi_c, hi_s, lo_c, lo_s))

                def up(x):
                    return x.unsqueeze(3).to_broadcast((P, 4, 16, 16))

                def low(x):
                    return x.unsqueeze(2).to_broadcast((P, 4, 16, 16))
                c4, s4 = (x[b % 2].rearrange("p r (a t) -> p r a t", a=16) for x in (tab_c, tab_s))
                one = rstd[:, :].rearrange("p (a t) -> p a t", a=16)
                link(nc.gpsimd.tensor_tensor(c4, up(hc_), low(lc_), ALU.mult))
                link(nc.gpsimd.tensor_tensor(s4, up(hs_), low(ls_), ALU.mult))
                link(nc.gpsimd.tensor_tensor(c4, c4, s4, ALU.subtract))
                link(nc.gpsimd.tensor_tensor(s4, up(hs_), low(lc_), ALU.mult))
                for r in range(4):
                    link(nc.gpsimd.tensor_tensor(one, hc_[:, r, :].unsqueeze(2).to_broadcast((P, 16, 16)),
                                                 ls_[:, r, :].unsqueeze(1).to_broadcast((P, 16, 16)), ALU.mult))
                    link(nc.gpsimd.tensor_tensor(s4[:, r], s4[:, r], one, ALU.add))
                pool.sem_inc(s5_tab, 1)

            make_table(0)
            for b in range(8):
                if b + 1 < 8:
                    make_table(b + 1)
                pool.wait_ge(s5_rot, b + 1)
                nc.gpsimd.tensor_tensor(z1, z1, z2, ALU.add).then_inc(s5_sum, 1)
                nc.gpsimd.tensor_tensor(z3, z3, z4, ALU.subtract).then_inc(s5_sum, 1)

        @block.tensor
        def _(pe):
            mm = nc.tensor.matmul

            def begin(u, banks):
                pe.wait_ge(rest_ready, u.count(1))
                for b, n in banks:
                    if not isinstance(n, int) or n > 0:
                        pe.wait_ge(bank_free[b], n)

            def parts(u, shape):
                return [w[:, u.first % n, :].rearrange("p (k n) -> p k n", k=shape)
                        for w, n in ((w_high, RAW), (w_rest, REST))]

            def product(dst, wh, wr, xh, xr, first, last, skip=False, weights_move=False):
                ops = ((wh, xh), (wh, xr), (wr, xh)) if not weights_move else ((wh, xh), (wr, xh), (wh, xr))
                for i, (w, x) in enumerate(ops):
                    a, b = (x, w) if weights_move else (w, x)
                    ins = mm(dst, a, b, start=first and i == 0, stop=last and i == 2, skip_group_check=skip)
                return ins

            def cols_unit(u, k, name, xh, xr, kc=DC):
                begin(u, [(k % 4, uses(name, k, u.turn))])
                wh, wr = parts(u, kc)
                for o in range(2):
                    for c in range(kc):
                        ins = product(L[:, k % 4, o * T:(o + 1) * T], wh[:, c, o * P:(o + 1) * P], wr[:, c, o * P:(o + 1) * P],
                                      xh[:, c, :], xr[:, c, :], c == 0, c == kc - 1)
                ins.then_inc(unit_done, 1)

            def cols_linear(name, xh=n_high, xr=n_rest):
                each_unit(pe, name, lambda u, j, k: cols_unit(u, k, name, xh, xr))

            def rows_linear(name):
                def one(u, j, k):
                    begin(u, [(k % 4, uses(name, k, u.turn))])
                    wh, wr = parts(u, DC)
                    for a in range(2):
                        for c in range(DC):
                            ins = product(L[:, k % 4, a * T:(a + 1) * T], wh[:, c, :], wr[:, c, :],
                                          n_high[:, c, a * P:(a + 1) * P], n_rest[:, c, a * P:(a + 1) * P],
                                          c == 0, c == DC - 1, weights_move=True)
                    ins.then_inc(unit_done, 1)
                each_unit(pe, name, one)

            def acc_unit(u, xh, xr, at, first, last):
                wh, wr = parts(u, 2)
                for c in range(2):
                    for o in range(DC):
                        ins = product(L[:, o // 2, o % 2 * T:(o % 2 + 1) * T], wh[:, c, o * P:(o + 1) * P],
                                      wr[:, c, o * P:(o + 1) * P], xh[:, at + c, :] if isinstance(at, int) else xh[:, bass.ds(at + c, 1), :].rearrange("p a t -> p (a t)"),
                                      xr[:, at + c, :] if isinstance(at, int) else xr[:, bass.ds(at + c, 1), :].rearrange("p a t -> p (a t)"),
                                      first and c == 0 and o % 2 == 0, last and c == 1, skip=True)
                ins.then_inc(unit_done, 1)

            def acc_linear(name, xh, xr):
                first, n = FIRST[name], COUNT[name]
                begin(Unit(first), [(b, BANK_USES[name][b]) for b in range(4)])
                acc_unit(Unit(first), xh, xr, 0, True, n == 1)

                turns = (n - 2) // 4
                if turns > 1:
                    with pe.Fori(0, turns) as i:
                        for k in range(1, 5):
                            u = Unit(first + k, i)
                            begin(u, [])
                            acc_unit(u, xh, xr, 8 * i + 2 * k, False, False)
                else:
                    turns = 0
                for k in range(1 + 4 * turns, n):
                    begin(Unit(first + k), [])
                    acc_unit(Unit(first + k), xh, xr, 2 * k, False, k == n - 1)

            def turn_tokens(k, rows_ap):
                pe.wait_ge(tokens_in, 16 * (k + 1))
                for b in range(4):
                    for c in range(2):
                        for a in range(2):
                            ins = nc.tensor.transpose(M[:, b, c * T + a * P:c * T + (a + 1) * P],
                                                      rows_ap[:, a, (2 * b + c) * P:(2 * b + c + 1) * P], ident[:, :])
                    ins.then_inc(turned, 1)

            rows2 = gate[:, :, :].rearrange("p a t -> p (a t)").rearrange("p (a n) -> p a n", a=2)

            def norm(k):
                pe.wait_ge(sq_ready, k + 1)
                for c in range(DC):
                    ins = mm(M[:, 0, 0:T], ones[:, :], m[:, c, :], start=c == 0, stop=c == DC - 1)
                ins.then_inc(sum_ready, 1)

            def attention(key, heads):
                score_of, values_of = heads
                tasks = TASKS[key]
                k0, nk = keys_of(key)

                def score(x):
                    if x["g"] >= 2:
                        pe.wait_ge(expd, x["g"] - 1)
                    pairs = score_of(x["h"], x["map"], x["qt"])
                    for i, (q, kk) in enumerate(pairs):
                        ins = mm(M[:, x["g"] % 2, 0:nk], q, kk, start=i == 0, stop=i == len(pairs) - 1)
                    ins.then_inc(scores, 1)
                score(tasks[0])
                for i, x in enumerate(tasks):
                    if i + 1 < len(tasks):
                        score(tasks[i + 1])
                    if not x["whole"]:
                        continue
                    pe.wait_ge(probs, x["group"] + 1)
                    if x["group"]:
                        pe.wait_ge(probs_Tc, x["group"])
                    src = ex[:, (x["g"] - x["map"]) % 2, :]
                    for c in range(nk // P):
                        ins = nc.tensor.transpose(M[:, 2, c * P:(c + 1) * P], src[:, c * P:(c + 1) * P], ident[:, :])
                    ins.then_inc(probs_T, 1)
                    if x["end"]:
                        pe.wait_ge(probs_Tc, x["group"] + 1)
                        if x["head"]:
                            pe.wait_ge(o_ready, x["head"])
                        for dst, vals in values_of(x["h"]):
                            for c, v in enumerate(vals):
                                ins = mm(dst, v, exT[:, c, :], start=c == 0, stop=c == len(vals) - 1)
                        ins.then_inc(attended, 1)

            pe.wait_ge(consts_in, 16 * 6)
            pe.wait_ge(params_in, 16 * (len(COLS) + 1 + 4 + 2 * LAYERS))
            flat_m = m[:, :, :].rearrange("p a t -> p (a t)")
            nc.tensor.transpose(M[:, 0, 0:NVEC], flat_m[0:NVEC, 0:P], ident[0:NVEC, 0:NVEC])
            nc.tensor.transpose(M[:, 0, P:P + 6], flat_m[0:6, P:2 * P], ident[0:6, 0:6])
            for l in range(LAYERS):
                nc.tensor.transpose(M[:, 1, l * P:l * P + TAPS * HC], flat_m[0:TAPS * HC, (2 + l) * P:(3 + l) * P],
                                    ident[0:TAPS * HC, 0:TAPS * HC])
                ins = nc.tensor.transpose(M[:, 1, 256 + l * 48:256 + (l + 1) * 48], flat_m[0:48, 1024 + l * P:1024 + (l + 1) * P],
                                          ident[0:48, 0:48])
            ins.then_inc(turned, 1)
            pe.wait_ge(turned_out, 4)
            turn_tokens(0, rows2)
            norm(0)
            pe.wait_ge(n_ready, 1)
            cols_linear("mem_k")
            rows_linear("mem_v")
            turn_tokens(1, rows2)
            norm(1)
            pe.wait_ge(n_ready, 2)
            cols_linear("xa")

            def modulation(half):
                grp = half // 2
                if half == 0:
                    pe.wait_ge(silu_ready, 1)
                    pe.wait_ge(bank_free[0], after("xa", 0))
                    pe.wait_ge(bank_free[1], after("xa", 1))
                if half % 2 == 0 and grp >= 2:
                    pe.wait_ge(ada_row, grp - 1)
                for a in range(4 * half, 4 * half + 4):
                    v, kc = BEFORE_ADA + a, a % 8
                    pe.wait_ge(landed[v % 4], 16 * (v // 4 + 1))
                    for q in range(4):
                        ins = mm(L[32 * q:32 * q + 2, grp % 2, :], silu_c[:, kc, :], raw[:, v % 4, q * 512:(q + 1) * 512],
                                 start=kc == 0, stop=kc == 7, skip_group_check=True)
                    ins.then_inc(ada_done, 1)

            modulation(0)
            modulation(1)
            pe.wait_ge(s5_coef_rows, 1)
            for i in range(5):
                ins = nc.tensor.transpose(M[:, 0, i * TILES:(i + 1) * TILES], rows[:, 11 + i, :], ident[0:TILES, 0:TILES])
            ins.then_inc(s5_bt, 1)
            modulation(2)
            modulation(3)
            pe.wait_ge(s5_blk, 8)
            for q in range(8):
                if q >= 4:
                    pe.wait_ge(turned_out, 4 + q - 4 + 1)
                else:
                    pe.wait_ge(s5_coef, 1)
                for k in range(4):
                    i, nblk = (4 * q + k) % 16 // 8, (4 * q + k) % 8
                    if q < 4:
                        src = bblk[:, i, 4 * nblk:4 * nblk + 4, :, :].rearrange("p n g c -> p (n g c)")
                    else:
                        src = cblk[:, i, nblk, :, :].rearrange("p g k -> p (g k)")
                    ins = nc.tensor.transpose(M[:, q % 4, k * P:(k + 1) * P], src, ident[:, :])
                ins.then_inc(turned, 1)

            def s5_in_product(b):
                d, c = (1 if b < 4 else 0), b % 4
                pe.wait_ge(xa_ready, 1)
                if b == 0:
                    pe.wait_ge(turned_out, 4 + 8)
                else:
                    pe.wait_ge(s5_rot, b)
                for r in range(4):
                    x = (xaR if d else xaT)[32 * r:32 * r + 32, c, :]
                    for i in range(2):
                        ins = mm(M[:, r, i * T:(i + 1) * T], BT[32 * r:32 * r + 32, i, 4 * d + c, :], x, start=True, stop=True)
                ins.then_inc(s5_bu, 1)

            def s5_out_product(b):
                d, c = (1 if b < 4 else 0), b % 4
                pe.wait_ge(s5_w, b + 1)
                if b == 0:
                    evacuated(pe, "xa")
                if b >= 2:
                    pe.wait_ge(s5_yout, b - 1)
                for r in range(4):
                    for k, (i, z) in enumerate(((0, z1), (0, z3), (1, z5), (1, z6))):
                        ins = mm(L[32 * r:32 * r + 32, 2 + b % 2, 0:T], CT[:, i, 4 * d + c, 32 * r:32 * r + 32], z[:, r, :],
                                 start=k == 0, stop=k == 3, skip_group_check=True)
                ins.then_inc(s5_y, 1)

            for b in range(8):
                s5_in_product(b)
                modulation(4 + b)
                s5_out_product(b)
            pe.wait_ge(ada_rows_in, 16 * 8 * ADA_GROUPS)
            for l in range(LAYERS):
                ins = nc.tensor.transpose(M[:, 0, l * P:l * P + 96], ada_rows[:, l, :], ident[0:96, 0:96])
            ins.then_inc(turned, 1)

            pe.wait_ge(s5_yout, 8)
            pe.wait_ge(ada_row, ADA_GROUPS)
            rows_linear("zv")
            cols_linear("zu")
            pe.wait_ge(sgu_in, 16 * 4)
            pe.wait_ge(mod_ready, 1)
            for h in range(SGU_HEADS):
                ins = nc.tensor.transpose(M[:, 2 + h // 4, h % 4 * P:(h % 4 + 1) * P], sgu_raw[:, h, :], ident[:, :])
            ins.then_inc(turned, 1)
            pe.wait_ge(ln_ready, 2)
            pe.wait_ge(turned_out, 4 + 8 + 1)
            for h in range(SGU_HEADS):
                for a in range(2):
                    dst = M[:, h // 2, h % 2 * T + a * P:h % 2 * T + (a + 1) * P]
                    mm(dst, zv[:, a, h * P:(h + 1) * P], sgu_wt[:, h, :], start=True, stop=False)
                    ins = mm(dst, one_row[0:1, :], sgu_b[0:1, h * P:(h + 1) * P], start=False, stop=True)
            ins.then_inc(sgu_mm, 1)
            cols_linear("gate_a")

            name = "glu"
            pe.wait_ge(branch_ready, 1)
            u = Unit(FIRST[name])
            begin(u, [(0, BANK_USES[name][0]), (1, BANK_USES[name][1])])
            wh, wr = parts(u, HC)
            for o in range(HC):
                for c in range(HC):
                    ins = product(L[:, o // 2, o % 2 * T:(o % 2 + 1) * T], wh[:, c, o * P:(o + 1) * P], wr[:, c, o * P:(o + 1) * P],
                                  b_high[:, c, :], b_rest[:, c, :], c == 0, c == HC - 1)
            ins.then_inc(unit_done, 1)
            pe.wait_ge(branch_ready, 2)
            acc_linear("proj_a", b_high, b_rest)
            cols_linear("gate_b")
            pe.wait_ge(m_split, 1)
            cols_linear("proj_b")
            pe.wait_ge(m_split, 2)
            cols_linear("out")
            norm(2)
            pe.wait_ge(n_ready, 3)
            cols_linear("mem_q")
            evacuated(pe, "mem_q")

            def mem_scores(h, mp, qt):
                return [(zu[:, 2 * h + c, qt * P:(qt + 1) * P], mem_kT[:, 2 * h + c, :]) for c in range(2)]

            def mem_values(h):
                return [(M[:, 3, d * T:(d + 1) * T], [mem_v[:, a, (2 * h + d) * P:(2 * h + d + 1) * P] for a in range(2)])
                        for d in range(2)]
            attention("mem", (mem_scores, mem_values))
            pe.wait_ge(m_split, 3)
            cols_linear("mem_o")

            def feed_forward(pre, k):
                norm(k)
                pe.wait_ge(n_ready, NREADY[k])
                cols_linear(pre + "ffn_up")
                pe.wait_ge(hid_ready, FC // 2 * (HID_OF[pre] + 1))
                acc_linear(pre + "ffn_down", hid_high, hid_rest)

            feed_forward("", 3)
            norm(4)
            for num, (p, l, s) in enumerate(PASSES):
                own = 0 if s == 0 else 2
                if p == "c0":
                    turn_tokens(2, rows2)
                norm(NORM_OF[p])
                pe.wait_ge(n_ready, NREADY[NORM_OF[p]])
                full = p != "c1"
                nf = FULL_OF.get(p)
                if full:
                    cols_linear(p + "four")
                    evacuated(pe, p + "four")
                    pe.wait_ge(dft_in, 16 * (nf + 1))
                    for c in range(HC):
                        for a in range(2):
                            ins = mm(M[:, c, a * T:(a + 1) * T], acc[:, c, a * P:(a + 1) * P], dft64[:, :], start=True, stop=True)
                    ins.then_inc(four1, 1)
                    pe.wait_ge(four1c, 4 * (nf + 1))
                    for c in range(HC):
                        for i, (a, k) in enumerate(((0, 0), (0, 1), (1, 0), (1, 1))):
                            ins = mm(M[:, c // 2, c % 2 * T:(c % 2 + 1) * T], y1[:, c, a, k * P:(k + 1) * P], dft256[:, k, a, :],
                                     start=i == 0, stop=i == 3)
                    ins.then_inc(four2, 1)
                    cols_linear(p + "conv_u")
                    cols_linear(p + "conv_g")
                    cols_linear(p + "q")
                cols_linear(p + "kv")
                evacuated(pe, p + "kv")
                if full:
                    pe.wait_ge(branch_ready, 2 + 4 * nf + 1)
                for a in range(2):
                    ins = nc.tensor.transpose(M[:, 3, a * P:(a + 1) * P], oT[:, 0, a * P:(a + 1) * P], ident[:, :])
                ins.then_inc(k_ready, 1)
                if full:
                    cols_linear(p + "dq")
                cols_linear(p + "dk")
                rows_linear(p + "dv")
                chunks = range(HC + 1) if full else range(HC, HC + 1)
                pe.wait_ge(qk_sq, num + 1)
                for c in chunks:
                    ins = mm(M[:, c // 2, c % 2 * T:(c % 2 + 1) * T], pair_ones[:, :], t2[:, c, :], start=True, stop=True)
                ins.then_inc(qk_sum, 1)
                rx = ROPE_OF.get(p)
                if rx is not None:
                    pe.wait_ge(qk_n, num + 1)
                    for c in chunks:
                        ins = mm(M[:, c // 2, c % 2 * T:(c % 2 + 1) * T], swap[:, :], qk[:, c, :], start=True, stop=True)
                    ins.then_inc(qk_rot, 1)
                    pe.wait_ge(d_rot, 3 * rx + 1)
                    evacuated(pe, p + "dv")
                    for c in range(8):
                        ins = mm(M[:, c // 2, c % 2 * T:(c % 2 + 1) * T], swap[:, :], dq[:, c, :] if c < 4 else t1[:, c - 4, :],
                                 start=True, stop=True)
                    ins.then_inc(qk_rot, 1)
                    pe.wait_ge(d_rot, 3 * rx + 3)
                else:
                    pe.wait_ge(qk_n, num + 1)
                for h in range(2):
                    ins = mm(M[:, 0, h * T:(h + 1) * T], dup[:, h, :], qk[:, HC, :], start=True, stop=True)
                ins.then_inc(kd_dup, 1)
                pe.wait_ge(kd_dupc, num + 1)
                if not full:
                    continue

                def branch(i):
                    cols_linear(p + f"gate{i}")
                    pe.wait_ge(branch_ready, 2 + 4 * nf + i + 1)
                    acc_linear(p + f"proj{i}", b_high, b_rest)

                branch(0)
                pe.wait_ge(conv_st, 2 * nf + 1)
                for c in range(HC):
                    ins = mm(M[:, 0, 0:T], ones[:, :], acc[:, c, :], start=c == 0, stop=c == HC - 1)
                ins.then_inc(conv_stc, 1)
                pe.wait_ge(conv_st, 2 * nf + 2)
                for c in range(HC):
                    ins = mm(M[:, 1, 0:T], ones[:, :], t2[:, c, :], start=c == 0, stop=c == HC - 1)
                ins.then_inc(conv_stc, 1)
                branch(1)

                k0, nk = keys_of(p)

                def gqa_scores(h, mp, qt):
                    a = HEAD * (h % 2)
                    return [(qk[a:a + HEAD, h // 2, qt * P:(qt + 1) * P], kdup[a:a + HEAD, h // 4, k0:k0 + nk])]

                def gqa_values(h):
                    a = HEAD * (h % 2)
                    return [(M[a:a + HEAD, 3, 0:T], [vrow[:, k0 // P + c, h // 4 * HEAD:(h // 4 + 1) * HEAD] for c in range(nk // P)])]

                def diff_scores(h, mp, qt):
                    a = HEAD * mp
                    return [(dq[a:a + HEAD, h, qt * P:(qt + 1) * P], kdT[a:a + HEAD, h, k0:k0 + nk])]

                def diff_values(h):
                    return [(M[:, 3, 0:T], [vdrow[:, k0 // P + c, h * P:(h + 1) * P] for c in range(nk // P)])]

                pe.wait_ge(branch_ready, 2 + 4 * nf + 2)
                attention(p + "gqa", (gqa_scores, gqa_values))
                branch(2)
                attention(p + "diff", (diff_scores, diff_values))
                pe.wait_ge(on_sq, nf + 1)
                for c in range(HC):
                    ins = mm(M[:, c // 2, c % 2 * T:(c % 2 + 1) * T], ones[:, :], t1[:, c, :], start=True, stop=True)
                ins.then_inc(on_sum, 1)
                branch(3)
                pe.wait_ge(m_split, 3 + nf + 1)
                cols_linear(p + "out")
                feed_forward(p, NORM_OF[p] + 1)
            norm(12)
            pe.wait_ge(scaled, SCALED[12] + DC)
            for b in range(4):
                a, half = b // 2, b % 2
                for c in range(4):
                    ins = nc.tensor.transpose(M[:, b, c * P:(c + 1) * P], m[:, 4 * half + c, a * P:(a + 1) * P], ident[:, :])
                ins.then_inc(turned, 1)

        @block.scalar
        def _(act):
            A = nc.scalar.activation
            rows2 = gate[:, :, :].rearrange("p a t -> p (a t)").rearrange("p (a n) -> p a n", a=2)

            def start_units(first):
                for k in range(3):
                    split_high(act, Unit(first + k))

            def linear(name, one):
                def step(u, j, k):
                    ahead_high(act, u, last_of(name))
                    if one is not None:
                        act.wait_ge(unit_done, u.count(1))
                        ins = one(j, k, u)
                        if ins is not None:
                            ins.then_inc(bank_free[k % 4], 1)
                each_unit(act, name, step)

            def out_to(name, dst, func=ACT.Copy):
                linear(name, lambda j, k, u: A(dst[:, 2 * j:2 * j + 2, :].rearrange("p a t -> p (a t)"), L[:, k % 4, :], func))

            def rows_to(name, dst, func=ACT.Copy):
                linear(name, lambda j, k, u: A(dst[:, :, j * T:(j + 1) * T], L[:, k % 4, :].rearrange("p (a n) -> p a n", a=2), func))

            def norm(k, h, shift, split=True):
                act.wait_ge(h_ready, NORM_H[k])
                if split and k >= 5:
                    act.wait_ge(mod_ready, 1)
                A(m[:, :, :], h[:, :, :], ACT.Square).then_inc(sq_ready, 1)
                act.wait_ge(ms_ready, k + 1)
                A(rstd[:, :], rstd[:, :], ACT.Sqrt).then_inc(root_ready, 1)
                if split:
                    for c in range(DC):
                        act.wait_ge(scaled, SCALED[k] + c + 1)
                        A(n_high[:, c, :], m[:, c, :], ACT.Identity, bias=shift(c)).then_inc(n_high_ready, 1)

            def attention(key, scale):
                k0, nk = keys_of(key)

                def turned_probs(x):
                    act.wait_ge(probs_T, x["group"] + 1)
                    if x["qt"] == 0 and x["head"]:
                        act.wait_ge(attended, x["head"])
                    A(exT[:, 0:nk // P, x["qt"] * P:(x["qt"] + 1) * P],
                      M[:, 2, 0:nk].rearrange("p (c q) -> p c q", q=P), ACT.Copy).then_inc(probs_Tc, 1)
                late = None
                for x in TASKS[key]:
                    act.wait_ge(neg_max, x["g"] + 1)
                    if x["g"] >= 2:
                        act.wait_ge(probs_T, GROUP[x["g"] - 2] + 1)
                    A(ex[:, x["g"] % 2, 0:nk], M[:, x["g"] % 2, 0:nk], ACT.Exp, bias=soft[:, x["g"] % 2, 1:2], scale=scale,
                      accum_out=soft[:, x["g"] % 2, 2:3]).then_inc(expd, 1)
                    if late is not None:
                        turned_probs(late)
                        late = None
                    if x["whole"]:
                        late = x
                turned_probs(late)

            act.wait_ge(flats_set, 4)
            act.wait_ge(turned_out, 4)
            for i, name in enumerate(("c_2", "c_ctx_2")):
                ins = A(silu_c[:, :, i], col(name, 0, DC), ACT.Silu)
            ins.then_inc(silu_ready, 1)
            act.wait_ge(lam_dot, 2 * LAYERS)
            for l in range(LAYERS):
                ins = A(lam[:, l, 2:4], lam[:, l, 0:2], ACT.Exp)
            ins.then_inc(lam_exp, 1)
            start_units(0)
            norm(0, hc, lambda c: flat[:, 0:1])
            out_to("mem_k", mem_kT)
            rows_to("mem_v", mem_v)
            norm(1, hx, lambda c: flat[:, 0:1])
            out_to("xa", xaT)
            act.wait_ge(s5_in, 16 * 7)
            A(rows[:, 2, 0:2], rows[:, 2, 0:2], ACT.Exp).then_inc(s5_act, 1)
            act.wait_ge(s5_act_in, 1)
            A(rows[:, 8, :], rows[:, 7, :], ACT.Sin).then_inc(s5_act, 1)
            A(rows[:, 9, :], rows[:, 7, :], ACT.Sin, scale=0.5).then_inc(s5_act, 1)
            A(rows[:, 10, :], rows[:, 3, :], ACT.Tanh, scale=0.5).then_inc(s5_act, 1)
            flatB = s5w[:, 6144:10240].rearrange("p (q k) -> p q k", q=8)

            def turned_block(q):
                act.wait_ge(turned, 1 + 8 + q + 1)
                A(flatB[:, q, :], M[:, q % 4, :], ACT.Copy).then_inc(turned_out, 1)

            def ada_out(grp):
                l, g = grp // 3, grp % 3
                act.wait_ge(ada_done, 8 * (grp + 1))
                if grp:
                    act.wait_ge(ada_rows_in, 16 * 8 * grp)
                flat_rope = rope[:, :, :].rearrange("p a t -> p (a t)")
                for q in range(4):
                    ins = A(flat_rope[32 * q:32 * q + 2, :], L[32 * q:32 * q + 2, grp % 2, :], ACT.Copy)
                    ins.then_inc(act_step, 1)
                act.wait_ge(act_step, 4 * (grp + 1))
                act.sem_inc(ada_row, 1)
                for q in range(4):
                    for s in range(2):
                        at = s * 48 + g * 16 + q * 4
                        act.dma_start(ada_rows[at:at + 4, l, :], flat_rope[32 * q + s:32 * q + s + 1, :]).then_inc(ada_rows_in, 16)
            ada_out(0)
            ada_out(1)
            for q in range(8):
                turned_block(q)
            for grp in range(2, ADA_GROUPS):
                ada_out(grp)
            act.wait_ge(ada_rows_in, 16 * 8 * ADA_GROUPS)
            act.dma_start(rope[:, :, :], consts["rope"].rearrange("p (a t) -> p a t", a=2)).then_inc(consts_in, 16)
            start_units(BEFORE_ADA)
            act.wait_ge(s5_yout, 8)
            act.dma_start(sgu_raw, t["sgu_w"][0].rearrange("h t s -> t h s")).then_inc(sgu_in, 16)
            act.dma_start(sgu_b, t["sgu_bias"][0].rearrange("(o h) t -> o (h t)", o=1)).then_inc(sgu_in, 16)
            lnv = m[:, :, :].rearrange("p a t -> p (a t)").rearrange("p (a n) -> p a n", a=2)
            act.dma_start(lnv[:, 0, :], t["sgu_ln_g"].partition_broadcast(P)).then_inc(sgu_in, 16)
            act.dma_start(lnv[:, 1, :], t["sgu_ln_b"].partition_broadcast(P)).then_inc(sgu_in, 16)
            act.wait_ge(s5_yout, 8)
            A(yT, yT, ACT.Gelu_apprx_tanh).then_inc(gelu_y, 1)
            rows_to("zv", zv, ACT.Gelu_apprx_tanh)
            out_to("zu", zu, ACT.Gelu_apprx_tanh)
            act.wait_ge(turned, 1 + 4 * 2 + 8 + 1 + 1)
            A(sgu_wt.rearrange("p h t -> p (h t)"), M[:, 2:4, :].rearrange("p a n -> p (a n)"), ACT.Copy).then_inc(turned_out, 1)
            for a in range(2):
                act.wait_ge(ln_sum, a + 1)
                A(work[:, 5760:6784], zv[:, a, :], ACT.Square, accum_out=stats[:, a, 2:3]).then_inc(ln_sq, 1)
                act.wait_ge(ln_sq, a + 1)
            act.wait_ge(ln_sum, 3)
            A(stats[:, :, 4], stats[:, :, 3], ACT.Sqrt).then_inc(ln_root, 1)
            out_to("gate_a", gate, ACT.Sigmoid)
            act.wait_ge(gelu_y, 1)
            A(b_high[:, :, :], yT, ACT.Copy).then_inc(glu_sig, 1)

            def glu_out(j, k, u):
                for b in range(2):
                    A(work[:, 5760 + 512 * b:5760 + 512 * (b + 1)], L[:, b, :], ACT.Sigmoid).then_inc(bank_free[b], 1)
            linear("glu", glu_out)
            act.wait_ge(glu_sig, 2)
            A(b_high[:, :, :], yT, ACT.Copy).then_inc(glu_sig, 1)
            linear("proj_a", None)
            act.wait_ge(merged, 4)
            out_to("gate_b", gate, ACT.Sigmoid)
            multiplied(act, "gate_b")
            act.wait_ge(sgu_out, 4)
            A(n_high[:, :, :], zu, ACT.Copy).then_inc(n_high_ready, 1)
            linear("proj_b", None)
            act.wait_ge(merged, 8)
            multiplied(act, "proj_b")
            A(n_high[:, :, :], m[:, :, :], ACT.Copy).then_inc(n_high_ready, 1)
            linear("out", None)
            norm(2, hx, lambda c: flat[:, 0:1])
            out_to("mem_q", zu)
            attention("mem", ATT_SCALE["mem"])
            multiplied(act, "mem_q")
            act.wait_ge(o_ready, NHEADS["mem"])
            A(n_high[:, :, :], o_mem, ACT.Copy).then_inc(n_high_ready, 1)
            linear("mem_o", None)

            def feed_forward(pre, k, h, shift):
                norm(k, h, shift)
                base = FC // 2 * HID_OF[pre]

                def one(j, k2, u):
                    if k2 % 2:
                        return None
                    pair = u.turn * 2 + k2 // 2 if not isinstance(u.turn, int) else j // 2
                    buf = (k2 // 2) % 2
                    if isinstance(pair, int):
                        if pair >= 2:
                            act.wait_ge(hid_ready, base + pair - 1)
                    else:
                        act.wait_ge(hid_ready, base + pair - 1)
                    A(gate[:, 4 * buf:4 * buf + 2, :].rearrange("p a t -> p (a t)"), L[:, k2 % 4, :], ACT.Silu).then_inc(up_act, 1)
                    return None
                first, n = FIRST[pre + "ffn_up"], COUNT[pre + "ffn_up"]

                def step(u, j, k2):
                    ahead_high(act, u, UNITS)
                    if k2 % 2 == 0:
                        act.wait_ge(unit_done, u.count(1))
                        one(j, k2, u)
                for j in range(4):
                    step(Unit(first + j), j, j)
                with act.Fori(0, n // 4 - 1) as i:
                    for k2 in range(4):
                        ahead_high(act, Unit(first + 4 + k2, i), UNITS)
                        if k2 % 2 == 0:
                            act.wait_ge(unit_done, Unit(first + 4 + k2, i).count(1))
                            act.wait_ge(hid_ready, base + 2 * i + 2 + k2 // 2 - 1)
                            A(gate[:, 2 * k2:2 * k2 + 2, :].rearrange("p a t -> p (a t)"), L[:, k2, :],
                              ACT.Silu).then_inc(up_act, 1)
                for j in range(n // 4 * 4, n):
                    step(Unit(first + j), j, j % 4)
                linear(pre + "ffn_down", None)

            feed_forward("", 3, hx, lambda c: flat[:, 0:1])
            norm(4, hx, None, split=False)
            act.wait_ge(h_ready, 6)
            act.dma_start(rows2, t["ctx_2"][0].rearrange("(a p) n -> p a n", p=P)).then_inc(tokens_in, 16)
            for num, (p, l, s) in enumerate(PASSES):
                h = hc if s else hx
                own = 2 if s else 0
                full, nf, rx = p != "c1", FULL_OF.get(p), ROPE_OF.get(p)
                norm(NORM_OF[p], h, lambda c: mod[:, l, s * 48 + c:s * 48 + c + 1])
                if full:
                    act.dma_start(dft256, consts["dft256"].rearrange("p (s l k) -> p s l k", s=2, l=2)).then_inc(dft_in, 16)
                    out_to(p + "four", acc)
                    act.wait_ge(four1, nf + 1)
                    for c in range(HC):
                        A(y1[:, c, :, :].rearrange("p a k -> p (a k)"), M[:, c, :], ACT.Copy).then_inc(four1c, 1)
                    act.wait_ge(four2, nf + 1)
                    for b in range(2):
                        A(b_high[:, 2 * b:2 * b + 2, :].rearrange("p a t -> p (a t)"), M[:, b, :], ACT.Copy).then_inc(z_ready, 1)
                    conv_mid = conv_in[:, :, PAD:PAD + T]
                    act.wait_ge(conv_a, 2 * nf + 1)
                    linear(p + "conv_u", lambda j, k, u: A(conv_mid[:, 2 * j:2 * j + 2, :],
                                                           L[:, k % 4, :].rearrange("p (a t) -> p a t", a=2), ACT.Copy))
                    act.wait_ge(branch_ready, 2 + 4 * nf + 1)
                    out_to(p + "conv_g", t1, ACT.Sigmoid)
                    out_to(p + "q", qk)

                def kv_out(j, k, u):
                    A(qk[:, HC, :], L[:, k, 0:T], ACT.Copy)
                    return A(oT[:, 0, :], L[:, k, T:2 * T], ACT.Copy)
                linear(p + "kv", kv_out)
                if full:
                    out_to(p + "dq", dq)
                    act.wait_ge(conv_a, 2 * nf + 2)
                kk = T if s else 0
                if s:
                    linear(p + "dk", lambda j, k, u: A(kdT[:, 2 * j:2 * j + 2, kk:kk + T],
                                                       L[:, k % 4, :].rearrange("p (a t) -> p a t", a=2), ACT.Copy))
                else:
                    out_to(p + "dk", t1)
                linear(p + "dv", lambda j, k, u: A(vdrow[:, own:own + 2, j * T:(j + 1) * T],
                                                   L[:, k % 4, :].rearrange("p (a n) -> p a n", a=2), ACT.Copy))
                evacuated(act, p + "dv")
                ch = slice(0, HC + 1) if full else slice(HC, HC + 1)
                A(t2[:, ch, :], qk[:, ch, :], ACT.Square).then_inc(qk_sq, 1)
                act.wait_ge(qk_ms, num + 1)
                A(t2[:, ch, :], t2[:, ch, :], ACT.Sqrt).then_inc(qk_root, 1)
                act.wait_ge(kd_dup, num + 1)
                A(kdup[:, :, kk:kk + T], M[:, 0, :].rearrange("p (h t) -> p h t", h=2), ACT.Copy).then_inc(kd_dupc, 1)
                if not full:
                    continue

                def branch(i):
                    if i or nf >= 0:
                        act.wait_ge(merged, 8 + 16 * nf + 4 * i)
                    out_to(p + f"gate{i}", gate, ACT.Sigmoid)
                    linear(p + f"proj{i}", None)

                branch(0)
                act.wait_ge(conv_n, 3 * nf + 1)
                A(t2[:, 0:HC, :], acc, ACT.Square).then_inc(conv_st, 1)
                act.wait_ge(conv_n, 3 * nf + 2)
                A(rstd[:, :], rstd[:, :], ACT.Sqrt).then_inc(conv_root, 1)
                act.wait_ge(conv_n, 3 * nf + 3)
                multiplied(act, p + "proj0")
                for c in range(HC):
                    A(t1[:, c, :], acc[:, c, :], ACT.Silu, bias=col("conv_ln_b_2", 4 * l + c)).then_inc(conv_sig, 1)
                act.wait_ge(conv_sig, 4 * (nf + 1))
                A(b_high[:, :, :], t1[:, 0:HC, :], ACT.Copy).then_inc(z_ready, 1)
                branch(1)
                attention(p + "gqa", HEAD ** -0.5)
                act.wait_ge(o_ready, NHEADS[p + "gqa"])
                multiplied(act, p + "proj1")
                A(b_high[:, :, :], oT, ACT.Copy).then_inc(z_ready, 1)
                branch(2)
                attention(p + "diff", HEAD ** -0.5)
                act.wait_ge(o_ready, NHEADS[p + "diff"])
                A(t1[:, 0:HC, :], oT, ACT.Square).then_inc(on_sq, 1)
                act.wait_ge(on_ms, nf + 1)
                A(t2[:, 0:HC, :], t2[:, 0:HC, :], ACT.Sqrt).then_inc(on_root, 1)
                act.wait_ge(on_ms, nf + 1)
                act.wait_ge(q_ready, nf + 1)
                multiplied(act, p + "proj2")
                A(b_high[:, :, :], oT, ACT.Copy).then_inc(z_ready, 1)
                branch(3)
                act.wait_ge(merged, 8 + 16 * (nf + 1))
                multiplied(act, p + "gate3")
                A(n_high[:, :, :], m[:, :, :], ACT.Copy).then_inc(n_high_ready, 1)
                linear(p + "out", None)
                feed_forward(p, NORM_OF[p] + 1, h, lambda c: mod[:, l, s * 48 + 24 + c:s * 48 + 25 + c])
            norm(12, hx, None, split=False)
            act.wait_ge(turned_out, 4 + 8 + 1 + 4)
            res = gate[:, :, :].rearrange("p a t -> p (a t)").rearrange("p (a n) -> p a n", a=2)
            act.dma_start(out[0].rearrange("(a p) n -> p a n", p=P), res).then_inc(stored, 16)
            act.wait_ge(stored, 16)

        @block.vector
        def _(dve):
            V = nc.vector
            n = [0]

            def link(ins):
                n[0] += 1
                ins.then_inc(dve_step, 1)
                dve.wait_ge(dve_step, n[0])

            def linear(name, one=None):
                def step(u, j, k):
                    ahead_rest(dve, u, last_of(name))
                    if one is not None:
                        dve.wait_ge(unit_done, u.count(1))
                        one(j, k, u)
                each_unit(dve, name, step)

            def norm(k, h, gain, shift, split=True, dst=None):
                dve.wait_ge(sum_ready, k + 1)
                V.tensor_scalar(rstd[:, :], M[:, 0, 0:T], 1.0 / D, EPS, ALU.mult, ALU.add).then_inc(ms_ready, 1)
                dve.wait_ge(root_ready, k + 1)
                link(V.reciprocal(rstd[:, :], rstd[:, :]))
                for c in range(DC):
                    V.scalar_tensor_tensor(m[:, c, :] if dst is None else dst[:, c, :], h[:, c, :], gain(c), rstd[:, :],
                                           ALU.mult, ALU.mult).then_inc(scaled, 1)
                if split:
                    for c in range(DC):
                        dve.wait_ge(n_high_ready, NHIGH[k] + c + 1)
                        ins = V.scalar_tensor_tensor(n_rest[:, c, :], m[:, c, :], shift(c), n_high[:, c, :].bitcast(F32),
                                                     ALU.add, ALU.subtract)
                    ins.then_inc(n_ready, 1)

            def turn_out(h, base):
                for b in range(4):
                    dve.wait_ge(turned, base + b + 1)
                    ins = V.tensor_copy(h[:, 2 * b:2 * b + 2, :].rearrange("p a t -> p (a t)"), M[:, b, :])
                    n[0] += 1
                    ins.then_inc(dve_step, 1)
                dve.wait_ge(dve_step, n[0])
                dve.sem_inc(h_ready, 1)

            def n_split(src, count):
                dve.wait_ge(n_high_ready, count)
                V.tensor_tensor(n_rest[:, :, :], src, n_high[:, :, :].bitcast(F32), ALU.subtract).then_inc(m_split, 1)

            def add_to_h(name, h, gain):
                def one(j, k, u):
                    for o in range(2):
                        ins = V.scalar_tensor_tensor(h[:, 2 * j + o, :], L[:, k % 4, o * T:(o + 1) * T], gain(2 * j + o),
                                                     h[:, 2 * j + o, :], ALU.mult, ALU.add)
                    ins.then_inc(bank_free[k % 4], 1)
                linear(name, one)
                evacuated(dve, name)
                dve.sem_inc(h_ready, 1)

            def merge_rows(name, first):
                linear(name)
                dve.wait_ge(unit_done, FIRST[name] + COUNT[name])
                for b in range(4):
                    g, mm_ = (x[:, 2 * b:2 * b + 2, :].rearrange("p a t -> p (a t)") for x in (gate, m))
                    if first:
                        V.tensor_tensor(mm_, g, L[:, b, :], ALU.mult).then_inc(bank_free[b], 1)
                    else:
                        V.tensor_tensor(g, g, L[:, b, :], ALU.mult).then_inc(bank_free[b], 1)
                evacuated(dve, name)
                for b in range(4):
                    g, mm_ = (x[:, 2 * b:2 * b + 2, :].rearrange("p a t -> p (a t)") for x in (gate, m))
                    if first:
                        dve.sem_inc(merged, 1)
                    else:
                        V.tensor_tensor(mm_, mm_, g, ALU.add).then_inc(merged, 1)

            def attention(key, scale, out_of, negl=None):
                k0, nk = keys_of(key)

                def neg(x):
                    sl = x["g"] % 2
                    dve.wait_ge(scores, x["g"] + 1)
                    link(V.tensor_reduce(soft[:, sl, 0:1], M[:, sl, 0:nk], AX.X, ALU.max, negate=True))
                    V.tensor_scalar(soft[:, sl, 1:2], soft[:, sl, 0:1], scale, None, ALU.mult).then_inc(neg_max, 1)
                tasks = TASKS[key]
                neg(tasks[0])
                ended = []
                for i, x in enumerate(tasks):
                    sl = x["g"] % 2
                    if i + 1 < len(tasks):
                        if x["g"] >= 1:
                            dve.wait_ge(expd, x["g"])
                        neg(tasks[i + 1])
                    dve.wait_ge(expd, x["g"] + 1)
                    link(V.reciprocal(soft[:, sl, 3:4], soft[:, sl, 2:3]))
                    if negl is None:
                        V.tensor_scalar(ex[:, sl, 0:nk], ex[:, sl, 0:nk], soft[:, sl, 3:4], None, ALU.mult).then_inc(probs, 1)
                    elif x["map"] == 0:
                        link(V.tensor_scalar(ex[:, sl, 0:nk], ex[:, sl, 0:nk], soft[:, sl, 3:4], None, ALU.mult))
                    else:
                        link(V.tensor_scalar(ex[:, sl, 0:nk], ex[:, sl, 0:nk], soft[:, sl, 3:4], negl, ALU.mult, ALU.mult))
                        V.tensor_tensor(ex[:, 1 - sl, 0:nk], ex[:, 1 - sl, 0:nk], ex[:, sl, 0:nk], ALU.add).then_inc(probs, 1)
                    if ended and (x["whole"]):
                        y = ended.pop()
                        dve.wait_ge(attended, y["head"] + 1)
                        out_of(y["h"]).then_inc(o_ready, 1)
                    if x["end"]:
                        ended.append(x)
                y = ended.pop()
                dve.wait_ge(attended, y["head"] + 1)
                out_of(y["h"]).then_inc(o_ready, 1)

            dve.wait_ge(consts_in, 16 * 6)
            dve.wait_ge(turned, 1)
            V.tensor_copy(cols[:, :], M[:, 0, 0:NVEC]).then_inc(turned_out, 1)
            V.tensor_copy(cols2[:, :], M[:, 0, P:P + 6]).then_inc(turned_out, 1)
            V.tensor_copy(tapc[:, :, :], M[:, 1, 0:2 * P].rearrange("p (l k) -> p l k", l=2)[:, :, 0:TAPS * HC]).then_inc(turned_out, 1)
            V.tensor_copy(b_ada[:, :, :], M[:, 1, 256:352].rearrange("p (l k) -> p l k", l=2)).then_inc(turned_out, 1)
            dve.wait_ge(lam_in, 16 * 4 * LAYERS)
            flat_m = m[:, :, :].rearrange("p a t -> p (a t)")
            for l in range(LAYERS):
                for i in range(2):
                    a, b = (flat_m[:, 512 + (4 * l + 2 * i + k) * HEAD:512 + (4 * l + 2 * i + k + 1) * HEAD] for k in range(2))
                    V.tensor_tensor_reduce(a, a, b, 1.0, 0.0, ALU.mult, ALU.add, lam[:, l, i:i + 1]).then_inc(lam_dot, 1)
            dve.wait_ge(lam_exp, 1)
            for l in range(LAYERS):
                link(V.tensor_tensor(lam[:, l, 4:5], lam[:, l, 3:4], lam[:, l, 2:3], ALU.subtract))
                link(V.tensor_scalar(lam[:, l, 5:6], lam[:, l, 4:5], -LAM_INIT[l], None, ALU.add))
                link(V.tensor_scalar(lam[:, l, 6:7], cols2[:, l:l + 1], 1.0 - LAM_INIT[l], None, ALU.mult))
            turn_out(hc, 1)
            split_rest(dve, Unit(0))
            norm(0, hc, lambda c: col("mem_norm_g", c), lambda c: flat[:, 0:1])
            linear("mem_k")
            linear("mem_v")
            turn_out(hx, 5)
            norm(1, hx, lambda c: col("mix_norm_g", c), lambda c: flat[:, 0:1])
            linear("xa")
            evacuated(dve, "xa")
            V.tensor_copy(xaR, xaT[:, :, ::-1]).then_inc(xa_ready, 1)

            R = lambda i: rows[:, i, :]
            dve.wait_ge(s5_act, 1)
            for g in range(2):
                sl = slice(g * STATE, (g + 1) * STATE)
                for i in range(2):
                    link(V.tensor_scalar(rows[:, 3 + i, sl], rows[:, i, sl], rows[:, 2, g:g + 1], None, ALU.mult))
            big = 1.5 * 2.0 ** 23
            C1, C2 = 6.28125, 0.0019350051879882812
            C3 = float(2 * np.pi - C1 - C2)
            link(V.tensor_scalar(R(5), R(4), 1.0 / (2 * np.pi), big, ALU.mult, ALU.add))
            link(V.tensor_scalar(R(5), R(5), -big, None, ALU.add))
            link(V.scalar_tensor_tensor(R(6), R(5), -C1, R(4), ALU.mult, ALU.add))
            link(V.scalar_tensor_tensor(R(7), R(5), -C2, R(6), ALU.mult, ALU.add))
            link(V.scalar_tensor_tensor(R(6), R(5), -C3, R(7), ALU.mult, ALU.add))
            V.tensor_scalar(R(7), R(6), 3.1415925, -3.1415925, ALU.min, ALU.max).then_inc(s5_act_in, 1)
            dve.wait_ge(s5_act, 4)
            link(V.tensor_scalar(R(5), R(10), -1.0, 1.0, ALU.mult, ALU.add))
            link(V.reciprocal(R(5), R(5)))
            link(V.scalar_tensor_tensor(R(6), R(10), 2.0, R(5), ALU.mult, ALU.mult))
            link(V.tensor_scalar(R(11), R(6), 1.0, None, ALU.add))
            link(V.scalar_tensor_tensor(R(7), R(9), -2.0, R(9), ALU.mult, ALU.mult))
            link(V.tensor_scalar(R(12), R(7), 1.0, None, ALU.add))
            link(V.tensor_copy(R(13), R(8)))
            link(V.tensor_tensor(R(5), R(6), R(12), ALU.mult))
            link(V.tensor_tensor(R(5), R(5), R(7), ALU.add))
            link(V.tensor_tensor(R(6), R(11), R(13), ALU.mult))
            link(V.tensor_tensor(R(7), R(0), R(0), ALU.mult))
            link(V.tensor_tensor(R(9), R(1), R(1), ALU.mult))
            link(V.tensor_tensor(R(7), R(7), R(9), ALU.add))
            link(V.reciprocal(R(7), R(7)))
            link(V.tensor_tensor(R(9), R(5), R(0), ALU.mult))
            link(V.tensor_tensor(R(10), R(6), R(1), ALU.mult))
            link(V.tensor_tensor(R(9), R(9), R(10), ALU.add))
            link(V.tensor_tensor(R(14), R(9), R(7), ALU.mult))
            link(V.tensor_tensor(R(9), R(6), R(0), ALU.mult))
            link(V.tensor_tensor(R(10), R(5), R(1), ALU.mult))
            link(V.tensor_tensor(R(9), R(9), R(10), ALU.subtract))
            V.tensor_tensor(R(15), R(9), R(7), ALU.mult).then_inc(s5_coef_rows, 1)
            dve.wait_ge(s5_bt, 1)
            V.tensor_copy(s5c, M[:, 0, 0:5 * TILES].rearrange("p (i n) -> p i n", i=5)).then_inc(s5_coef, 1)
            dve.wait_ge(s5_coef, 1)
            cr, ci = (s5c[:, 3 + i, :].unsqueeze(2).to_broadcast((P, TILES, CH)) for i in range(2))
            for i, (x, y, op) in enumerate((((cr, 0), (ci, 1), ALU.subtract), ((cr, 1), (ci, 0), ALU.add))):
                link(V.tensor_tensor(bbar[:, i], braw[:, x[1]], x[0], ALU.mult))
                link(V.tensor_tensor(btmp, braw[:, y[1]], y[0], ALU.mult))
                link(V.tensor_tensor(bbar[:, i], bbar[:, i], btmp, op))
            dve.wait_ge(n_ready, 2)
            link(V.memset(bblk[0:STATE, :, :, 1, :], 0.0))
            link(V.memset(bblk[STATE:P, :, :, 0, :], 0.0))
            for i in range(2):
                V.tensor_copy(bblk[0:STATE, i, :, 0, :], bbar[0:STATE, i]).then_inc(s5_blk, 1)
                V.tensor_copy(bblk[STATE:P, i, :, 1, :], bbar[STATE:P, i]).then_inc(s5_blk, 1)
                for g in range(2):
                    V.tensor_scalar(cblk[:, i, :, g, :], craw[:, i, :, :], masks[:, 2 * i + g:2 * i + g + 1], None,
                                    ALU.mult).then_inc(s5_blk, 1)
            dve.wait_ge(turned_out, 4 + 8)

            def rotate_in(b):
                dve.wait_ge(s5_tab, b + 1)
                dve.wait_ge(s5_bu, b + 1)
                if b:
                    dve.wait_ge(s5_y, b)
                c_, s_ = tab_c[b % 2], tab_s[b % 2]
                re, im = M[:, :, 0:T], M[:, :, T:2 * T]
                V.tensor_tensor(z1, c_, re, ALU.mult).then_inc(dve_step, 1)
                V.tensor_tensor(z2, s_, im, ALU.mult).then_inc(dve_step, 1)
                V.tensor_tensor(z3, c_, im, ALU.mult).then_inc(dve_step, 1)
                V.tensor_tensor(z4, s_, re, ALU.mult).then_inc(dve_step, 1)
                n[0] += 4
                dve.wait_ge(dve_step, n[0])
                dve.sem_inc(s5_rot, 1)

            for b in range(8):
                d, c, tile = (1 if b < 4 else 0), b % 4, s5_tile(b)
                rotate_in(b)
                for half, (src, dst) in enumerate(((z1, z2), (z3, z4))):
                    dve.wait_ge(s5_sum, 2 * b + 2)
                    for r in range(4):
                        V.tensor_tensor_scan(dst[:, r, :], s5c[:, 0, tile + r:tile + r + 1].to_broadcast((P, T)), src[:, r, :],
                                             0.0, ALU.mult, ALU.add).then_inc(dve_step, 1)
                        n[0] += 1
                dve.wait_ge(dve_step, n[0])
                c_, s_ = tab_c[b % 2], tab_s[b % 2]
                V.tensor_tensor(z1, c_, z2, ALU.mult).then_inc(dve_step, 1)
                V.scalar_tensor_tensor(z3, s_, -1.0, z4, ALU.mult, ALU.mult).then_inc(dve_step, 1)
                V.tensor_tensor(z5, s_, z2, ALU.mult).then_inc(dve_step, 1)
                V.tensor_tensor(z6, c_, z4, ALU.mult).then_inc(dve_step, 1)
                n[0] += 4
                dve.wait_ge(dve_step, n[0])
                dve.sem_inc(s5_w, 1)
                dve.wait_ge(s5_y, b + 1)
                res = L[:, 2 + b % 2, 0:T]
                if d:
                    V.tensor_copy(yT[:, c, :], res[:, ::-1]).then_inc(s5_yout, 1)
                else:
                    link(V.tensor_tensor(yT[:, c, :], yT[:, c, :], res, ALU.add))
                    V.scalar_tensor_tensor(yT[:, c, :], xaT[:, c, :], col("s5_d", c), yT[:, c, :], ALU.mult,
                                           ALU.add).then_inc(s5_yout, 1)
            dve.wait_ge(turned, 1 + 8 + 8 + 1)
            for l in range(LAYERS):
                for s in range(2):
                    link(V.tensor_tensor(mod[:, l, s * 48:(s + 1) * 48], M[:, 0, l * P + s * 48:l * P + (s + 1) * 48], b_ada[:, l, :], ALU.add))
            for l in range(LAYERS):
                for s in range(2):
                    for i, (part, name) in enumerate(((1, "norm_mix_2"), (4, "norm_ffn_2"))):
                        at = s * 48 + part * 8
                        link(V.scalar_tensor_tensor(modg[:, l, s, i, :], mod[:, l, at:at + 8], 1.0, col(name, 8 * l, 8), ALU.add, ALU.mult))
            dve.sem_inc(mod_ready, 1)

            split_rest(dve, Unit(BEFORE_ADA))
            linear("zv")
            linear("zu")
            evacuated(dve, "zv")
            for a in range(2):
                link(V.tensor_reduce(stats[:, a, 0:1], zv[:, a, :], AX.X, ALU.add))
                link(V.tensor_scalar(stats[:, a, 1:2], stats[:, a, 0:1], -1.0 / D, None, ALU.mult))
                V.tensor_scalar(zv[:, a, :], zv[:, a, :], stats[:, a, 1:2], None, ALU.add).then_inc(ln_sum, 1)
            dve.wait_ge(ln_sq, 2)
            V.tensor_scalar(stats[:, :, 3], stats[:, :, 2], 1.0 / D, EPS, ALU.mult, ALU.add).then_inc(ln_sum, 1)
            dve.wait_ge(ln_root, 1)
            link(V.reciprocal(stats[:, :, 5], stats[:, :, 4]))
            dve.wait_ge(sgu_in, 16 * 4)
            lnv = m[:, :, :].rearrange("p a t -> p (a t)").rearrange("p (a n) -> p a n", a=2)
            for a in range(2):
                link(V.scalar_tensor_tensor(zv[:, a, :], zv[:, a, :], stats[:, a, 5:6], lnv[:, 0, :], ALU.mult, ALU.mult))
                V.tensor_tensor(zv[:, a, :], zv[:, a, :], lnv[:, 1, :], ALU.add).then_inc(ln_ready, 1)
            dve.wait_ge(sgu_mm, 1)
            evacuated(dve, "zu")
            for b in range(4):
                x = zu[:, 2 * b:2 * b + 2, :].rearrange("p a t -> p (a t)")
                V.tensor_tensor(x, x, M[:, b, :], ALU.mult).then_inc(sgu_out, 1)
            linear("gate_a")
            dve.wait_ge(glu_sig, 1)
            V.tensor_tensor(b_rest[:, :, :], yT, b_high[:, :, :].bitcast(F32), ALU.subtract).then_inc(branch_ready, 1)
            linear("glu")
            evacuated(dve, "glu")
            V.tensor_tensor(yT, yT, work[:, 5760:6784].rearrange("p (c t) -> p c t", c=HC), ALU.mult).then_inc(glu_sig, 1)
            dve.wait_ge(glu_sig, 3)
            V.tensor_tensor(b_rest[:, :, :], yT, b_high[:, :, :].bitcast(F32), ALU.subtract).then_inc(branch_ready, 1)
            dve.wait_ge(ln_ready, 2)
            evacuated(dve, "gate_a")
            merge_rows("proj_a", True)
            linear("gate_b")
            n_split(zu, NHIGH_EVENTS["yb"])

            def proj_b_out(j, k, u):
                g, mm_ = (x[:, 2 * j:2 * j + 2, :].rearrange("p a t -> p (a t)") for x in (gate, m))
                if j == 0:
                    evacuated(dve, "gate_b")
                V.tensor_tensor(g, g, L[:, k, :], ALU.mult).then_inc(bank_free[k], 1)
                dve.wait_ge(bank_free[k], after("proj_b", k))
                V.tensor_tensor(mm_, mm_, g, ALU.add).then_inc(merged, 1)
            linear("proj_b", proj_b_out)
            n_split(m[:, :, :], NHIGH_EVENTS["merged"])
            one = lambda c: flat[:, 1:2]
            zero = lambda c: flat[:, 0:1]
            add_to_h("out", hx, one)
            norm(2, hx, lambda c: col("xattn_norm_g", c), zero)
            linear("mem_q")
            attention("mem", ATT_SCALE["mem"], lambda h: V.tensor_copy(
                o_mem[:, 2 * h:2 * h + 2, :].rearrange("p a t -> p (a t)"), M[:, 3, :]))
            n_split(o_mem, NHIGH_EVENTS["o_mem"])
            add_to_h("mem_o", hx, one)

            def feed_forward(pre, k, h, gain, shift, out_gain):
                norm(k, h, gain, shift)
                first, cnt = FIRST[pre + "ffn_up"], COUNT[pre + "ffn_up"]
                base = FC // 2 * HID_OF[pre]
                steps = n[0]

                def pair(i, k2, gates, done):
                    sg = gate[:, 2 * k2 - 2:2 * k2, :].rearrange("p a t -> p (a t)")
                    hh = gate[:, 2 * k2:2 * k2 + 2, :].rearrange("p a t -> p (a t)")
                    at = 4 * i + (k2 - 1)
                    if isinstance(at, int):
                        hi_, re_ = (x[:, at:at + 2, :].rearrange("p a t -> p (a t)") for x in (hid_high, hid_rest))
                    else:
                        hi_, re_ = (x[:, bass.ds(at, 2), :].rearrange("p a t -> p (a t)") for x in (hid_high, hid_rest))
                    dve.wait_ge(up_act, gates)
                    V.tensor_tensor(hh, sg, L[:, k2, :], ALU.mult).then_inc(dve_step, 1)
                    dve.wait_ge(dve_step, done + 1)
                    V.tensor_copy(hi_, hh).then_inc(dve_step, 1)
                    dve.wait_ge(dve_step, done + 2)
                    V.tensor_tensor(re_, hh, hi_.bitcast(F32), ALU.subtract).then_inc(hid_ready, 1)
                    dve.sem_inc(bank_free[k2 - 1], 1)
                    dve.sem_inc(bank_free[k2], 1)

                def turn(i):
                    for k2 in range(4):
                        u = Unit(first + k2, i)
                        ahead_rest(dve, u, UNITS)
                        if k2 % 2:
                            dve.wait_ge(unit_done, u.count(1))
                            pair(i, k2, base + 2 * i + k2 // 2 + 1, steps + 4 * i + 2 * (k2 // 2))
                turns = cnt // 4
                with dve.Fori(0, turns) as i:
                    turn(i)
                n[0] += 4 * turns
                for k2 in range(cnt - 4 * turns):
                    u = Unit(first + 4 * turns + k2)
                    ahead_rest(dve, u, UNITS)
                    if k2 % 2:
                        dve.wait_ge(unit_done, u.count(1))
                        pair(turns, k2, base + 2 * turns + k2 // 2 + 1, n[0])
                        n[0] += 2
                name = pre + "ffn_down"
                linear(name)
                dve.wait_ge(unit_done, FIRST[name] + COUNT[name])
                for b in range(4):
                    for o in range(2):
                        ins = V.scalar_tensor_tensor(h[:, 2 * b + o, :], L[:, b, o * T:(o + 1) * T], out_gain(2 * b + o),
                                                     h[:, 2 * b + o, :], ALU.mult, ALU.add)
                    ins.then_inc(bank_free[b], 1)
                evacuated(dve, name)
                dve.sem_inc(h_ready, 1)

            feed_forward("", 3, hx, lambda c: col("ffn_norm_g", c), zero, one)
            norm(4, hx, lambda c: col("final_norm_g", c), None, split=False, dst=hx)
            dve.wait_ge(scaled, SCALED[4] + DC)
            dve.sem_inc(h_ready, 1)
            turn_out(hc, 1 + 8 + 8 + 1 + 1)
            for num, (p, l, s) in enumerate(PASSES):
                h = hc if s else hx
                own, kk = (2, T) if s else (0, 0)
                full, nf, rx = p != "c1", FULL_OF.get(p), ROPE_OF.get(p)
                norm(NORM_OF[p], h, lambda c: modg[:, l, s, 0, c:c + 1], lambda c: mod[:, l, s * 48 + c:s * 48 + c + 1])

                def b_split(src):
                    V.tensor_tensor(b_rest[:, :, :], src, b_high[:, :, :].bitcast(F32), ALU.subtract).then_inc(branch_ready, 1)
                if full:
                    link(V.memset(conv_in[:, :, 0:PAD], 0.0))
                    V.memset(conv_in[:, :, PAD + T:2 * PAD + T], 0.0).then_inc(conv_a, 1)
                    linear(p + "four")
                    dve.wait_ge(z_ready, 5 * nf + 2)
                    b_split(M[:, 0:2, :].rearrange("p b (c t) -> p (b c) t", c=2))
                    linear(p + "conv_u")
                    linear(p + "conv_g")
                    linear(p + "q")
                linear(p + "kv")
                dve.wait_ge(k_ready, num + 1)
                V.tensor_copy(vrow[:, own:own + 2, :], M[:, 3, 0:T].rearrange("p (a n) -> p a n", a=2)).then_inc(v_ready, 1)
                if full:
                    evacuated(dve, p + "conv_g")
                    mid = conv_in[:, :, PAD:PAD + T]
                    dve.wait_ge(four1, nf + 1)
                    V.tensor_tensor(mid, mid, t1[:, 0:HC, :], ALU.mult).then_inc(conv_a, 1)
                    linear(p + "dq")
                linear(p + "dk")
                linear(p + "dv")
                dve.wait_ge(qk_sum, num + 1)
                banks = ((0, 0, 2), (1, 2, 2), (2, 4, 1)) if full else ((2, 4, 1),)
                for b, c0, w in banks:
                    link(V.tensor_scalar(t2[:, c0:c0 + w, :].rearrange("p a t -> p (a t)"), M[:, b, 0:w * T], 1.0 / HEAD, EPS, ALU.mult, ALU.add))
                dve.sem_inc(qk_ms, 1)
                dve.wait_ge(qk_root, num + 1)
                ch = slice(0, HC + 1) if full else slice(HC, HC + 1)
                link(V.reciprocal(t2[:, ch, :], t2[:, ch, :]))
                for c in (range(HC + 1) if full else (HC,)):
                    g = cols2[:, 2 + l:3 + l] if c < HC else cols2[:, 4 + l:5 + l]
                    link(V.scalar_tensor_tensor(qk[:, c, :], qk[:, c, :], g, t2[:, c, :], ALU.mult, ALU.mult))
                dve.sem_inc(qk_n, 1)
                if rx is not None:
                    def bc(i, w):
                        return rope[:, i, :].unsqueeze(1).to_broadcast((P, w, T))
                    dve.wait_ge(consts_in, 16 * 7)
                    dve.wait_ge(qk_rot, 2 * rx + 1)
                    for b, c0, w in banks:
                        link(V.tensor_tensor(t2[:, c0:c0 + w, :], M[:, b, 0:w * T].rearrange("p (a t) -> p a t", a=w), bc(1, w), ALU.mult))
                    dve.sem_inc(d_rot, 1)
                    link(V.tensor_tensor(qk, qk, bc(0, 5), ALU.mult))
                    link(V.tensor_tensor(qk, qk, t2, ALU.add))
                    dve.wait_ge(qk_rot, 2 * rx + 2)
                    for i, (src, dst) in enumerate(((dq, dq), (t1[:, 0:HC, :], kdT[:, :, 0:T]))):
                        rot = M[:, 2 * i:2 * i + 2, :].rearrange("p b (c t) -> p (b c) t", c=2)
                        link(V.tensor_tensor(t2[:, 0:HC, :], rot, bc(1, HC), ALU.mult))
                        link(V.tensor_tensor(src, src, bc(0, HC), ALU.mult))
                        V.tensor_tensor(dst, src, t2[:, 0:HC, :], ALU.add).then_inc(d_rot, 1)
                        dve.wait_ge(d_rot, 3 * rx + 2 + i)
                if not full:
                    continue
                evacuated(dve, p + "dv")
                dve.wait_ge(conv_a, 2 * nf + 2)
                for c in range(HC):
                    V.tensor_scalar(acc[:, c, :], conv_in[:, c, 0:T], tapc[:, l, c:c + 1], col("conv_b_2", 4 * l + c),
                                    ALU.mult, ALU.add).then_inc(conv_step, 1)
                with dve.Fori(1, TAPS) as k:
                    for c in range(HC):
                        dve.wait_ge(conv_step, 4 * k + CONV_BASE[p] + c - 3)
                        V.scalar_tensor_tensor(acc[:, c, :], conv_in[:, c, bass.ds(k, T)], tapc[:, l, bass.ds(4 * k + c, 1)], acc[:, c, :],
                                               ALU.mult, ALU.add).then_inc(conv_step, 1)
                dve.wait_ge(conv_step, CONV_BASE[p] + 4 + 4 * (TAPS - 1))
                dve.sem_inc(conv_st, 1)
                gl = lambda i: (linear(p + f"gate{i}"), evacuated(dve, p + f"gate{i}"), merge_rows(p + f"proj{i}", i == 0))
                gl(0)
                dve.wait_ge(conv_stc, 2 * nf + 1)
                link(V.tensor_scalar(rstd[:, :], M[:, 0, 0:T], -1.0 / HALF, None, ALU.mult))
                link(V.tensor_tensor(acc, acc, rstd[:, :].unsqueeze(1).to_broadcast((P, HC, T)), ALU.add))
                dve.sem_inc(conv_n, 1)
                dve.wait_ge(conv_stc, 2 * nf + 2)
                V.tensor_scalar(rstd[:, :], M[:, 1, 0:T], 1.0 / HALF, LN_EPS, ALU.mult, ALU.add).then_inc(conv_n, 1)
                dve.wait_ge(conv_root, nf + 1)
                link(V.reciprocal(rstd[:, :], rstd[:, :]))
                for c in range(HC):
                    link(V.scalar_tensor_tensor(acc[:, c, :], acc[:, c, :], col("conv_ln_g_2", 4 * l + c), rstd[:, :], ALU.mult, ALU.mult))
                dve.sem_inc(conv_n, 1)
                dve.wait_ge(z_ready, 5 * nf + 3)
                b_split(t1[:, 0:HC, :])
                gl(1)

                def gqa_out(hd):
                    a = HEAD * (hd % 2)
                    return V.tensor_copy(oT[a:a + HEAD, hd // 2, :], M[a:a + HEAD, 3, 0:T])
                attention(p + "gqa", HEAD ** -0.5, gqa_out)
                dve.wait_ge(z_ready, 5 * nf + 4)
                b_split(oT)
                gl(2)
                attention(p + "diff", HEAD ** -0.5, lambda hd: V.tensor_copy(oT[:, hd, :], M[:, 3, 0:T]), negl=lam[:, l, 5:6])
                dve.wait_ge(on_sum, nf + 1)
                for b in range(2):
                    link(V.tensor_scalar(t2[:, 2 * b:2 * b + 2, :].rearrange("p a t -> p (a t)"), M[:, b, :], 1.0 / P, EPS, ALU.mult, ALU.add))
                dve.sem_inc(on_ms, 1)
                dve.wait_ge(on_root, nf + 1)
                link(V.reciprocal(t2[:, 0:HC, :], t2[:, 0:HC, :]))
                link(V.scalar_tensor_tensor(oT, oT, lam[:, l, 6:7], t2[:, 0:HC, :], ALU.mult, ALU.mult))
                dve.sem_inc(q_ready, 1)
                dve.wait_ge(z_ready, 5 * nf + 5)
                b_split(oT)
                gl(3)
                n_split(m[:, :, :], NHIGH_EVENTS[p])
                add_to_h(p + "out", h, lambda c: mod[:, l, s * 48 + 16 + c:s * 48 + 17 + c])
                feed_forward(p, NORM_OF[p] + 1, h, lambda c: modg[:, l, s, 1, c:c + 1],
                             lambda c: mod[:, l, s * 48 + 24 + c:s * 48 + 25 + c],
                             lambda c: mod[:, l, s * 48 + 40 + c:s * 48 + 41 + c])
            norm(12, hx, lambda c: col("final_norm_2", c), None, split=False)
            for b in range(4):
                dve.wait_ge(turned, 1 + 8 + 8 + 1 + 1 + 4 + b + 1)
                V.tensor_copy(gate[:, 2 * b:2 * b + 2, :].rearrange("p a t -> p (a t)"), M[:, b, :]).then_inc(turned_out, 1)


_INS = [
    "x", "mem", "mix_norm_g", "w_in", "s5_lam_re", "s5_lam_im", "s5_log_step", "s5_b_re", "s5_b_im", "s5_c_re",
    "s5_c_im", "s5_d", "s5_w_glu", "sgu_ln_g", "sgu_ln_b", "sgu_w", "sgu_bias", "w_proj_a", "w_proj_b", "w_out",
    "xattn_norm_g", "mem_norm_g", "w_q", "w_k", "w_v", "w_xo", "ffn_norm_g", "w_gate", "w_up", "w_down",
    "final_norm_g", "c_2", "ctx_2", "c_ctx_2", "w_ada_2", "b_ada_2", "norm_mix_2", "w_in_2", "w_four_2", "conv_w_2",
    "conv_b_2", "conv_ln_g_2", "conv_ln_b_2", "w_conv_2", "q_norm_2", "k_norm_2", "w_gqa_2", "lam_q1_2",
    "lam_k1_2", "lam_q2_2", "lam_k2_2", "diff_norm_2", "w_diff_2", "w_out_2", "norm_ffn_2", "w_ffn1_2",
    "w_ffn3_2", "w_ffn2_2", "final_norm_2",
]


def shape_constants():
    f = np.float32
    i, j = np.arange(P)[:, None], np.arange(P)[None, :]
    same64 = i // HEAD == j // HEAD
    ang64 = 2 * np.pi * ((i % HEAD) * (j % HEAD) % HEAD) / HEAD
    dft64 = np.concatenate([np.where(same64, np.cos(ang64), 0), np.where(same64, -np.sin(ang64), 0)], 1) / 8
    l, k = np.arange(T)[:, None], np.arange(T)[None, :]
    ang = 2 * np.pi * (l * k % T) / T
    dft256 = np.stack([np.cos(ang), np.sin(ang)]) / 16
    dft256 = dft256.reshape(2, 2, P, T).transpose(2, 0, 1, 3).reshape(P, -1)
    half = HEAD // 2
    inv = (f(10000.0) ** (-np.arange(0, half, 2, dtype=f) / f(half))).astype(f)
    tok = np.arange(T)
    angles = np.concatenate([(tok // 64).astype(f)[:, None] * inv, (tok % 64).astype(f)[:, None] * inv], 1).astype(f)
    angles = angles.astype(np.float64)[:, np.arange(P) % half].T
    rope = np.concatenate([np.cos(angles), np.sin(angles)], 1)
    a, b = np.arange(P) % HEAD, np.arange(P)
    swap = np.zeros((P, P))
    for c in range(P):
        swap[c + half if a[c] < half else c - half, c] = -1 if a[c] < half else 1
    dup = np.concatenate([(i == j % HEAD) * 1.0, (i == HEAD + j % HEAD) * 1.0], 1)
    even = (np.arange(P) // CH) % 2 == 0
    masks = np.stack([even * 1.0, ~even * 1.0, even * -1.0, ~even * -1.0], 1)
    out = dict(ident=np.eye(P), dft64=dft64, dft256=dft256, rope=rope, swap=swap, dup=dup, pair_ones=same64 * 1.0, masks=masks)
    return {k: np.ascontiguousarray(v).astype(f) for k, v in out.items()}


def kernel(**inputs):
    import concourse.bacc as _bacc
    from concourse.bass_utils import run_bass_kernel_spmd as _run

    nc = _bacc.Bacc("TRN2", target_bir_lowering=False, num_devices=1)
    arrays, t, consts = {}, {}, {}
    for name in _INS:
        a = np.ascontiguousarray(inputs[name])
        arrays[f"in_{name}"] = a
        t[name] = nc.dram_tensor(f"in_{name}", a.shape, mybir.dt.from_np(a.dtype), kind="ExternalInput").ap()
    for name, a in shape_constants().items():
        arrays[f"const_{name}"] = a
        consts[name] = nc.dram_tensor(f"const_{name}", a.shape, mybir.dt.from_np(a.dtype), kind="ExternalInput").ap()
    out = nc.dram_tensor("out_0", (1, T, D), F32, kind="ExternalOutput").ap()
    build(nc, t, out, consts)
    r = _run(nc, [arrays], core_ids=[0])
    return r.results[0]["out_0"]
```

```python
from contextlib import ExitStack

import concourse.bass as bass
from concourse import mybir
import numpy as np

F32 = mybir.dt.float32
F32R = mybir.dt.float32r
ALU = mybir.AluOpType
ACT = mybir.ActivationFunctionType
AX = mybir.AxisListType

P = 128
T = 256
D = 1024
DC = D // P
HALF = 512
HC = HALF // P
F = 2816
FC = F // P
GROUPS, STATE, CH = 32, 64, 16
TILES = 2 * GROUPS // 2
SGU_HEADS = 8
CHUNK = 128
MEM_HEADS = 4
TAPS = 31
PAD = TAPS // 2
HEAD = 64
DIFF_HEADS = 4
LAYERS = 2
EPS = 1e-6
LN_EPS = 1e-5
UNIT = 2048
RAW = 4
REST = 2
LAM_INIT = [0.8 - 0.6 * float(np.exp(-0.3 * l)) for l in range(LAYERS)]
ADA_GROUPS = 6

COLS = {}


def _place_columns():
    at = 0
    for name, rows in (("mix_norm_g", 8), ("mem_norm_g", 8), ("xattn_norm_g", 8), ("ffn_norm_g", 8),
                       ("final_norm_g", 8), ("norm_mix_2", 16), ("norm_ffn_2", 16), ("final_norm_2", 8),
                       ("c_2", 8), ("c_ctx_2", 8), ("s5_d", 4), ("conv_b_2", 8), ("conv_ln_g_2", 8),
                       ("conv_ln_b_2", 8)):
        COLS[name] = at
        at += rows
    return at


NVEC = _place_columns()


def schedule():
    s = [("mem_k", 4), ("mem_v", 4), ("xa", 2), ("ADA", 0),
         ("zv", 4), ("zu", 4), ("gate_a", 4), ("glu", 1), ("proj_a", 2), ("gate_b", 4), ("proj_b", 4),
         ("out", 4), ("mem_q", 4), ("mem_o", 4), ("ffn_up", 22), ("ffn_down", 11)]
    for p in ("c0", "x0", "c1", "x1"):
        if p == "c1":
            s += [(p + k, n) for k, n in (("kv", 1), ("dk", 2), ("dv", 2))]
        else:
            s += [(p + k, n) for k, n in (
                ("conv_u", 2), ("conv_g", 2), ("four", 2), ("q", 2), ("kv", 1), ("dq", 2), ("dk", 2), ("dv", 2),
                ("gate0", 4), ("proj0", 2), ("gate1", 4), ("proj1", 2), ("gate2", 4), ("proj2", 2),
                ("gate3", 4), ("proj3", 2), ("out", 4), ("ffn_up", 22), ("ffn_down", 11))]
    return s


ROW_KIND = ("proj_a", "proj0", "proj1", "proj2", "proj3", "ffn_down")


def row_kind(name):
    return name in ROW_KIND or name[2:] in ROW_KIND


FIRST, COUNT, BANK_USES = {}, {}, {}


def _number_units():
    at, uses = 0, [0] * 4
    for name, n in schedule():
        if name == "ADA":
            continue
        FIRST[name], COUNT[name], BANK_USES[name] = at, n, list(uses)
        at += n
        if row_kind(name):
            uses = [x + 1 for x in uses]
        elif name == "glu":
            uses = [uses[0] + 1, uses[1] + 1, uses[2], uses[3]]
        else:
            uses = [x + (n - b + 3) // 4 for b, x in enumerate(uses)]
    return at


UNITS = _number_units()
BEFORE_ADA = FIRST["zv"]
ADA_UNITS = LAYERS * 3 * DC


class Unit:

    def __init__(self, first, turn=0):
        self.first, self.turn = first, turn

    def plus(self, k):
        return Unit(self.first + k, self.turn)

    def count(self, k=0):
        return self.first + 4 * self.turn + k

    def quarter(self):
        at = self.first + (ADA_UNITS if self.first >= BEFORE_ADA else 0)
        return at // 4 + 1 + self.turn


def build(nc, t, out, consts):
    ctx = ExitStack()
    with ctx:
        def sb(name, shape, dt=F32):
            return ctx.enter_context(nc.sbuf_tensor(name, shape, dt))

        def sem(name):
            return ctx.enter_context(nc.semaphore(name))

        raw = sb("raw", [P, RAW, UNIT])
        w_high = sb("w_high", [P, RAW, UNIT], F32R)
        w_rest = sb("w_rest", [P, REST, UNIT], F32R)
        n_high = sb("n_high", [P, DC, T], F32R)
        n_rest = sb("n_rest", [P, DC, T], F32R)
        hx = sb("hx", [P, DC, T])
        hc = sb("hc", [P, DC, T])
        kv = sb("kv", [P, 5632])
        ident = sb("ident", [P, P])
        dft64 = sb("dft64", [P, 2 * P])
        rope = sb("rope", [P, 2, T])
        ada_rows = sb("ada_rows", [96, LAYERS, P])
        b_ada = sb("b_ada", [P, LAYERS, 48])
        swap = sb("swap", [P, P])
        dup = sb("dup", [P, 2, P])
        pair_ones = sb("pair_ones", [P, P])
        ones = sb("ones", [P, P])
        one_row = sb("one_row", [1, P])
        masks = sb("masks", [P, 4])
        cols = sb("cols", [P, NVEC])
        cols2 = sb("cols2", [P, 6])
        tapc = sb("tapc", [P, LAYERS, TAPS * HC])
        mod = sb("mod", [P, LAYERS, 96])
        modg = sb("modg", [P, LAYERS, 2, 2, DC])
        silu_c = sb("silu_c", [P, DC, 2])
        flat = sb("flat", [P, 2])
        lam = sb("lam", [P, LAYERS, 8])
        stats = sb("stats", [P, 2, 8])
        soft = sb("soft", [P, 4, 4])
        rstd = sb("rstd", [P, T])
        m = sb("m", [P, DC, T])
        gate = sb("gate", [P, DC, T])

        over = ExitStack()
        with over:
            hid_high = over.enter_context(nc.sbuf_tensor("hid_high", [P, FC, T], F32R))
            hid_rest = over.enter_context(nc.sbuf_tensor("hid_rest", [P, FC, T], F32R))
        over = ExitStack()
        with over:
            b_high = over.enter_context(nc.sbuf_tensor("b_high", [P, HC, T], F32R))
            b_rest = over.enter_context(nc.sbuf_tensor("b_rest", [P, HC, T], F32R))
            again = ExitStack()
            with again:
                work = again.enter_context(nc.sbuf_tensor("work", [P, 9216], F32))
            work_r = over.enter_context(nc.sbuf_tensor("work_r", [P, 9216], F32R))
        over = ExitStack()
        with over:
            s5w = over.enter_context(nc.sbuf_tensor("s5w", [P, 11264], F32))

        dft256 = work[:, 0:1024].rearrange("p (s l k) -> p s l k", s=2, l=2)
        conv_in = work[:, 1024:1024 + HC * (T + 2 * PAD)].rearrange("p (c t) -> p c t", c=HC)
        acc = work[:, 2176:3200].rearrange("p (c t) -> p c t", c=HC)
        qk = work[:, 3200:4480].rearrange("p (c t) -> p c t", c=HC + 1)
        dq = work[:, 4480:5504].rearrange("p (c t) -> p c t", c=HC)
        t1 = work[:, 5504:6784].rearrange("p (c t) -> p c t", c=HC + 1)
        t2 = work[:, 6784:8064].rearrange("p (c t) -> p c t", c=HC + 1)
        oT = work[:, 8064:9088].rearrange("p (c t) -> p c t", c=HC)
        zu = work[:, 0:2048].rearrange("p (c t) -> p c t", c=DC)
        zv = work[:, 2048:4096].rearrange("p (a n) -> p a n", a=2)
        o_mem = work[:, 2048:4096].rearrange("p (c t) -> p c t", c=DC)
        sgu_wt = work[:, 7040:8064].rearrange("p (h t) -> p h t", h=SGU_HEADS)
        sgu_raw = work[:, 4480:5504].rearrange("p (h t) -> p h t", h=SGU_HEADS)
        sgu_b = work[0:1, 8064:9088]
        mem_kT = kv[:, 0:2048].rearrange("p (c t) -> p c t", c=DC)
        mem_v = kv[:, 2048:4096].rearrange("p (a n) -> p a n", a=2)
        kdup = kv[:, 0:1024].rearrange("p (h t) -> p h t", h=2)
        vrow = kv[:, 1024:1536].rearrange("p (a n) -> p a n", a=4)
        kdT = kv[:, 1536:3584].rearrange("p (h t) -> p h t", h=HC)
        vdrow = kv[:, 3584:5632].rearrange("p (a n) -> p a n", a=4)
        STORE = {"mem": dict(k=4096, v=5120, q=6144, turned=7168, turned_rest=7680, exp=8192, step=256),
                 "gqa": dict(k=0, v=1024, q=1536, turned_rest=2048, exp=5504, turned=7040, step=512),
                 "diff": dict(k=0, v=2048, q=3072, turned_rest=3328, exp=5504, turned=7040, step=512)}
        SHARE = {"mem": dict(k=1, q=1, v=1), "gqa": dict(k=4, q=2, v=4), "diff": dict(k=1, q=1, v=1)}
        BUFFERS = {"mem": dict(k=1, q=2, v=1), "gqa": dict(k=1, q=2, v=1), "diff": dict(k=2, q=1, v=1)}
        WORDS = {"mem": dict(k=512, q=512, v=512), "gqa": dict(k=512, q=256, v=256), "diff": dict(k=512, q=256, v=512)}

        def kind_of(key):
            return key if key == "mem" else key[2:]

        def store_of(key):
            at = STORE[kind_of(key)]
            exps = [work[:, at["exp"] + i * at["step"]:at["exp"] + (i + 1) * at["step"]] for i in range(3)]
            n = 2 * at["step"]
            return exps, [work_r[:, at[x]:at[x] + n].rearrange("p (c q) -> p c q", q=T) for x in ("turned", "turned_rest")]

        def s5a(i):
            return s5w[:, 1024 * i:1024 * (i + 1)]
        q4 = "p (r t) -> p r t"
        tab_c = [s5a(0).rearrange(q4, r=4), s5a(2).rearrange(q4, r=4)]
        tab_s = [s5a(1).rearrange(q4, r=4), s5a(3).rearrange(q4, r=4)]
        z1, z2, z3, z4 = (m[:, 0:4, :], m[:, 4:8, :], gate[:, 0:4, :], gate[:, 4:8, :])
        z5, z6 = s5a(4).rearrange(q4, r=4), s5a(5).rearrange(q4, r=4)
        BT = s5w[:, 6144:8192].rearrange("p (i n k) -> p i n k", i=2, n=8)
        CT = s5w[:, 8192:10240].rearrange("p (i n k) -> p i n k", i=2, n=8)
        hi_c = s5w[:, 10240:10752].rearrange("p (n k) -> p n k", n=TILES)
        hi_s = s5w[:, 10752:11264].rearrange("p (n k) -> p n k", n=TILES)
        lo_c = kv[:, 4096:4608].rearrange("p (n k) -> p n k", n=TILES)
        lo_s = kv[:, 4608:5120].rearrange("p (n k) -> p n k", n=TILES)
        s5c = kv[:, 5120:5280].rearrange("p (i n) -> p i n", i=5)
        pw = kv[:, 5280:5472].rearrange("p (i n) -> p i n", i=6)
        xaT, xaR, yT = hc[:, 0:4, :], hc[:, 4:8, :], hc[:, 4:8, :]
        braw = s5w[:, 0:1024].rearrange("p (i n c) -> p i n c", i=2, n=TILES)
        bbar = s5w[:, 1024:2048].rearrange("p (i n c) -> p i n c", i=2, n=TILES)
        btmp = s5w[:, 2048:2560].rearrange("p (n c) -> p n c", n=TILES)
        craw = s5w[:, 3072:4096].rearrange("p (i n k) -> p i n k", i=2, n=8)
        bblk = m[:, :, :].rearrange("p a t -> p (a t)").rearrange("p (i n g c) -> p i n g c", i=2, n=TILES, g=2)
        cblk = gate[:, :, :].rearrange("p a t -> p (a t)").rearrange("p (i n g k) -> p i n g k", i=2, n=8, g=2)
        rows = s5w[0:TILES, 4096:4096 + 16 * P].rearrange("p (i k) -> p i k", i=16)

        L = ctx.enter_context(nc.psum_tensor("L", [P, 4, 512], F32))
        M = ctx.enter_context(nc.psum_tensor("M", [P, 4, 512], F32))

        score_bank = (M[:, 0, :], M[:, 1, :], L[:, 0, :])
        turned_bank = (M[:, 2, :], L[:, 1, :])
        head_bank = (L[:, 2, :], M[:, 3, :])

        landed = [sem(f"landed{i}") for i in range(RAW)]
        high_ready, rest_ready, unit_done, ada_done = sem("high_ready"), sem("rest_ready"), sem("unit_done"), sem("ada_done")
        bank_free = [sem(f"bank_free{i}") for i in range(4)]
        consts_in, params_in, s5_in, tokens_in = sem("consts_in"), sem("params_in"), sem("s5_in"), sem("tokens_in")
        rows_in, sgu_in, dft_in, lam_in = sem("rows_in"), sem("sgu_in"), sem("dft_in"), sem("lam_in")
        flats_set, dve_step, act_step, pool_step = sem("flats_set"), sem("dve_step"), sem("act_step"), sem("pool_step")
        turned, turned_out = sem("turned"), sem("turned_out")
        sq_ready, sum_ready, ms_ready, root_ready, scaled, n_high_ready, n_ready = [
            sem(x) for x in ("sq_ready", "sum_ready", "ms_ready", "root_ready", "scaled", "n_high_ready", "n_ready")]
        ada_row, ada_rows_in, mod_ready = sem("ada_row"), sem("ada_rows_in"), sem("mod_ready")
        silu_ready = sem("silu_ready")
        s5_act_in, s5_act, s5_coef_rows, s5_coef, s5_blk, s5_pow, s5_tab = [
            sem(x) for x in ("s5_act_in", "s5_act", "s5_coef_rows", "s5_coef", "s5_blk", "s5_pow", "s5_tab")]
        s5_bt, s5_bu, s5_rot, s5_sum, s5_w, s5_y, s5_yout, xa_ready = [
            sem(x) for x in ("s5_bt", "s5_bu", "s5_rot", "s5_sum", "s5_w", "s5_y", "s5_yout", "xa_ready")]
        gelu_y, branch_ready, glu_sig, gate_ready, merged = [
            sem(x) for x in ("gelu_y", "branch_ready", "glu_sig", "gate_ready", "merged")]
        zv_ready, zu_ready, ln_sum, ln_sq, ln_root, ln_ready, sgu_mm, sgu_out, m_split = [
            sem(x) for x in ("zv_ready", "zu_ready", "ln_sum", "ln_sq", "ln_root", "ln_ready", "sgu_mm", "sgu_out", "m_split")]
        h_ready, q_ready, k_ready, v_ready, scores, neg_max, expd, probs, probs_T, probs_T_high, attended, o_ready = [
            sem(x) for x in ("h_ready", "q_ready", "k_ready", "v_ready", "scores", "neg_max", "expd", "probs",
                             "probs_T", "probs_T_high", "attended", "o_ready")]
        probs_T_rest, op_high, op_rest = sem("probs_T_rest"), sem("op_high"), sem("op_rest")
        up_act, hid_ready = sem("up_act"), sem("hid_ready")
        z_ready, four1, four1c, four2 = sem("z_ready"), sem("four1"), sem("four1c"), sem("four2")
        conv_a, conv_sig, conv_step, conv_st, conv_stc, conv_root, conv_n, conv_pool = [
            sem(x) for x in ("conv_a", "conv_sig", "conv_step", "conv_st", "conv_stc", "conv_root", "conv_n", "conv_pool")]
        qk_raw, qk_sq, qk_sum, qk_ms, qk_root, qk_n, qk_rot, dq_raw, d_rot, kd_dup, kd_dupc = [
            sem(x) for x in ("qk_raw", "qk_sq", "qk_sum", "qk_ms", "qk_root", "qk_n", "qk_rot", "dq_raw", "d_rot",
                             "kd_dup", "kd_dupc")]
        on_sq, on_sum, on_ms, on_root = sem("on_sq"), sem("on_sum"), sem("on_ms"), sem("on_root")
        lam_dot, lam_exp = sem("lam_dot"), sem("lam_exp")
        stored = sem("stored")

        block = ctx.enter_context(nc.Block())

        def col(name, c, n=1):
            return cols[:, COLS[name] + c:COLS[name] + c + n]

        def each_unit(eng, name, body, start=0):
            first, n = FIRST[name] + start, COUNT[name] - start
            turns = n // 4
            if turns > 1:
                with eng.Fori(0, turns) as i:
                    for k in range(4):
                        body(Unit(first + k, i), start + 4 * i + k, k)
            else:
                turns = 0
            for k in range(4 * turns, n):
                body(Unit(first + k), start + k, k)

        def uses(name, k, turn=0):
            return BANK_USES[name][k % 4] + k // 4 + turn

        def split_high(act, u):
            act.wait_ge(landed[u.first % 4 if u.first < BEFORE_ADA else (u.first + ADA_UNITS) % 4], 16 * u.quarter())
            if u.first >= 4:
                act.wait_ge(unit_done, u.count(-3))
            nc.scalar.activation(w_high[:, u.first % 4, :], raw[:, u.first % 4, :], ACT.Copy).then_inc(high_ready, 1)

        def split_rest(dve, u):
            dve.wait_ge(high_ready, u.count(1))
            if u.first >= 2:
                dve.wait_ge(unit_done, u.count(-1))
            nc.vector.tensor_tensor(w_rest[:, u.first % 2, :], raw[:, u.first % 4, :],
                                    w_high[:, u.first % 4, :].bitcast(F32), ALU.subtract).then_inc(rest_ready, 1)

        def ahead_high(act, u, last):
            if u.first + 3 < last:
                split_high(act, u.plus(3))

        def ahead_rest(dve, u, last):
            if u.first + 1 < last:
                split_rest(dve, u.plus(1))

        def last_of(name):
            return BEFORE_ADA if FIRST[name] < BEFORE_ADA else UNITS


        @block.sync
        def _(sp):
            for k, (name, dst) in enumerate((("ident", ident), ("dft64", dft64), ("swap", swap),
                                             ("pair_ones", pair_ones), ("masks", masks))):
                sp.dma_start(dst[:, :], consts[name]).then_inc(consts_in, 16)
            sp.dma_start(dup[:, :, :], consts["dup"].rearrange("p (a k) -> p a k", a=2)).then_inc(consts_in, 16)
            sp.dma_start(gate[:, :, :].rearrange("p a t -> p (a t)").rearrange("p (a n) -> p a n", a=2),
                         t["mem"][0].rearrange("(a p) n -> p a n", p=P)).then_inc(tokens_in, 16)

            def rows_of(ap):
                return ap.rearrange("l (r k) -> (l r) k", k=P) if len(ap.shape) == 2 else ap.rearrange("(r k) -> r k", k=P)
            at = 0
            flat_m = m[:, :, :].rearrange("p a t -> p (a t)")
            for name in COLS:
                src = rows_of(t[name])
                sp.dma_start(flat_m[at:at + src.shape[0], 0:P], src).then_inc(params_in, 16)
                at += src.shape[0]
            sp.dma_start(flat_m[0:2, P:2 * P], t["diff_norm_2"]).then_inc(params_in, 16)
            for k, name in enumerate(("q_norm_2", "k_norm_2")):
                for h in range(2):
                    sp.dma_start(flat_m[2 + 2 * k:4 + 2 * k, P + h * HEAD:P + (h + 1) * HEAD], t[name]).then_inc(params_in, 16)
            for l in range(LAYERS):
                sp.dma_start(flat_m[0:TAPS * HC, (2 + l) * P:(3 + l) * P],
                             t["conv_w_2"][l].rearrange("k (c n) -> (k c) n", n=P)).then_inc(params_in, 16)
                sp.dma_start(flat_m[0:48, 1024 + l * P:1024 + (l + 1) * P],
                             t["b_ada_2"][l].rearrange("(r k) -> r k", k=P)).then_inc(params_in, 16)
            for k, name in enumerate(("lam_q1_2", "lam_k1_2", "lam_q2_2", "lam_k2_2")):
                for l in range(LAYERS):
                    sp.dma_start(flat_m[:, 512 + (4 * l + k) * HEAD:512 + (4 * l + k + 1) * HEAD],
                                 t[name][l:l + 1, :].partition_broadcast(P)).then_inc(lam_in, 16)

            def load(u, src, dst=None):
                slot = u.first % 4
                if u.first >= 4:
                    if BEFORE_ADA <= u.first < BEFORE_ADA + 4:
                        sp.wait_ge(ada_done, ADA_UNITS - 4 + u.first - BEFORE_ADA + 1)
                    else:
                        sp.wait_ge(rest_ready, u.count(-3))
                sp.dma_start(raw[:, slot, :] if dst is None else dst, src).then_inc(landed[slot], 16)

            def load_cols(name, w, at, step=256):
                wv = w.rearrange("(k p) n -> p k n", p=P)
                k = wv.shape[1]
                each_unit(sp, name, lambda u, j, _: load(
                    u, wv[:, :, bass.ds(at + step * j, step)],
                    raw[:, u.first % 4, :].rearrange("p (k n) -> p k n", k=k)))

            def load_rows(name, w):
                wv = w.rearrange("(k p) n -> p k n", p=P)
                each_unit(sp, name, lambda u, j, _: load(
                    u, wv[:, bass.ds(2 * j, 2), :], raw[:, u.first % 4, :].rearrange("p (k n) -> p k n", k=2)), start=0)

            def load_ffn(name, gate_w, up_w, down_w):
                gv, uv = (w.rearrange("(k p) n -> p k n", p=P) for w in (gate_w, up_w))

                def one(u, j, k):
                    half = (j - (k % 2)) * 128 if isinstance(j, int) else (u.turn * 512 + (k // 2) * 256)
                    load(u, (gv if k % 2 == 0 else uv)[:, :, bass.ds(half, 256)],
                         raw[:, u.first % 4, :].rearrange("p (k n) -> p k n", k=DC))
                each_unit(sp, name + "up", one)
                load_rows(name + "down", down_w)

            load_cols("mem_k", t["w_k"][0], 0)
            load_cols("mem_v", t["w_v"][0], 0)
            w_in = t["w_in"][0]
            load_cols("xa", w_in, 0)
            sp.wait_ge(h_ready, 1)
            sp.dma_start(gate[:, :, :].rearrange("p a t -> p (a t)").rearrange("p (a n) -> p a n", a=2),
                         t["x"][0].rearrange("(a p) n -> p a n", p=P)).then_inc(tokens_in, 16)
            for a in range(ADA_UNITS):
                v = BEFORE_ADA + a
                if a < 4:
                    sp.wait_ge(rest_ready, v - 3)
                else:
                    sp.wait_ge(ada_done, a - 3)
                l, g, k = a // 24, a // 8 % 3, a % 8
                sp.dma_start(raw[:, v % 4, :], t["w_ada_2"][l, k * P:(k + 1) * P, g * UNIT:(g + 1) * UNIT]).then_inc(landed[v % 4], 16)

            load_cols("zv", w_in, HALF + D)
            load_cols("zu", w_in, HALF)
            load_cols("gate_a", w_in, HALF + 2 * D)
            load(Unit(FIRST["glu"]), t["s5_w_glu"][0].rearrange("(k p) n -> p k n", p=P),
                 raw[:, FIRST["glu"] % 4, :].rearrange("p (k n) -> p k n", k=HC))
            load_rows("proj_a", t["w_proj_a"][0])
            load_cols("gate_b", w_in, HALF + 3 * D)
            load_cols("proj_b", t["w_proj_b"][0], 0)
            load_cols("out", t["w_out"][0], 0)
            load_cols("mem_q", t["w_q"][0], 0)
            load_cols("mem_o", t["w_xo"][0], 0)
            load_ffn("ffn_", t["w_gate"][0], t["w_up"][0], t["w_down"][0])
            for p, l in (("c0", 0), ("x0", 0), ("c1", 1), ("x1", 1)):
                w = t["w_in_2"][l]
                if p != "c1":
                    load_cols(p + "conv_u", w, 512)
                    load_cols(p + "conv_g", w, 1024)
                    load_cols(p + "four", w, 0)
                    load_cols(p + "q", w, 1536)
                load_cols(p + "kv", w, 2048)
                if p != "c1":
                    load_cols(p + "dq", w, 2304)
                load_cols(p + "dk", w, 2816)
                load_cols(p + "dv", w, 3328)
                if p == "c1":
                    continue
                for b, wb in enumerate(("w_four_2", "w_conv_2", "w_gqa_2", "w_diff_2")):
                    load_cols(p + f"gate{b}", w, 3840 + b * D)
                    load_rows(p + f"proj{b}", t[wb][l])
                load_cols(p + "out", t["w_out_2"][l], 0)
                load_ffn(p + "ffn_", t["w_ffn1_2"][l], t["w_ffn3_2"][l], t["w_ffn2_2"][l])

        PASSES = (("c0", 0, 1), ("x0", 0, 0), ("c1", 1, 1), ("x1", 1, 0))
        NORM_H = [1, 2, 3, 4, 5, 7, 8, 9, 10, 11, 11, 12, 13]
        NORM_OF = {"c0": 5, "x0": 7, "c1": 9, "x1": 10}
        FULL_OF = {"c0": 0, "x0": 1, "x1": 2}
        ROPE_OF = {"x0": 0, "x1": 1}
        HID_OF = {"": 0, "c0": 1, "x0": 2, "x1": 3}
        DVE_CHUNKS = 2
        CONV_STEPS = HC + DVE_CHUNKS * (TAPS - 1)
        SCALED = [DC * k for k in range(13)]
        NREADY = [1, 2, 3, 4, None, 5, 6, 7, 8, 9, 10, 11]
        NHIGH, NHIGH_EVENTS = {}, {}
        count = 0
        for x in (0, 1, "yb", "merged", 2, "o_mem", 3, 5, "c0", 6, 7, "x0", 8, 9, 10, "x1", 11):
            if isinstance(x, int):
                NHIGH[x] = count
                count += DC
            else:
                count += 1
                NHIGH_EVENTS[x] = count
        y1 = work[:, 5504:7552].rearrange("p (c a k) -> p c a k", c=HC, a=2)

        def after(name, b):
            n = COUNT[name]
            if row_kind(name):
                return BANK_USES[name][b] + 1
            if name == "glu":
                return BANK_USES[name][b] + (b < 2)
            return BANK_USES[name][b] + (n - b + 3) // 4

        def evacuated(eng, name):
            for b in range(4):
                eng.wait_ge(bank_free[b], after(name, b))

        def multiplied(eng, name):
            eng.wait_ge(unit_done, FIRST[name] + COUNT[name])

        TASKS = {}

        def _tasks():
            g = group = head = 0
            for key, heads, maps in [("mem", MEM_HEADS, 1)] + [(p + k, h, n) for p in ("c0", "x0", "x1")
                                                              for k, h, n in (("gqa", 8, 1), ("diff", DIFF_HEADS, 2))]:
                tasks = []
                for h in range(heads):
                    for qt in range(2):
                        for mp in range(maps):
                            tasks.append(dict(g=g, group=group, head=head, h=h, qt=qt, map=mp,
                                              whole=mp == maps - 1, end=mp == maps - 1 and qt == 1))
                            g += 1
                        group += 1
                    head += 1
                TASKS[key] = tasks
        _tasks()
        GROUP = [x["group"] for v in TASKS.values() for x in v]
        NHEADS = {k: v[-1]["head"] + 1 for k, v in TASKS.items()}
        END_OF = {}
        for key_, v_ in TASKS.items():
            for i_, x_ in enumerate(v_):
                if x_["end"]:
                    END_OF[key_, i_] = x_

        def keys_of(key):
            return (0, T) if key == "mem" else (T, T) if key[0] == "c" else (0, 2 * T)

        def operand(key, what, h):
            k0, nk = keys_of(key)
            kc = slice(k0 // P, (k0 + nk) // P)
            if key == "mem":
                return {"k": mem_kT[:, 2 * h:2 * h + 2, :], "q": zu[:, 2 * h:2 * h + 2, :],
                        "v": mem_v[:, :, 2 * h * P:2 * (h + 1) * P]}[what]
            if kind_of(key) == "gqa":
                return {"k": kdup[:, h // 4, k0:k0 + nk], "q": qk[:, h // 2, :],
                        "v": vrow[:, kc, h // 4 * HEAD:(h // 4 + 1) * HEAD]}[what]
            return {"k": kdT[:, h, k0:k0 + nk], "q": dq[:, h, :], "v": vdrow[:, kc, h * P:(h + 1) * P]}[what]

        def shaped(buf, like):
            if len(like.shape) == 2:
                return buf[:, 0:like.shape[1]]
            return buf[:, 0:like.shape[1] * like.shape[2]].rearrange("p (a n) -> p a n", a=like.shape[1])

        Q_AT = {"mem": (0, 512), "gqa": (3200, 256), "diff": (4480, 256)}

        def split_of(key, what, h):
            kind, like = kind_of(key), operand(key, what, h)
            n, w, at = h // SHARE[kind][what], WORDS[kind][what], STORE[kind][what]
            slot = n % BUFFERS[kind][what]
            if what == "q":
                q0, qw = Q_AT[kind]
                return shaped(work_r[:, at + slot * w:at + (slot + 1) * w], like), shaped(work_r[:, q0 + n * qw:q0 + (n + 1) * qw], like)
            return [shaped(work_r[:, at + (2 * slot + i) * w:at + (2 * slot + i + 1) * w], like) for i in range(2)]

        SPLITS, NEED = {}, {}

        def _splits():
            done = 0
            for key, tasks in TASKS.items():
                firsts = {x["h"]: i for i, x in reversed(list(enumerate(tasks)))}
                kind = kind_of(key)
                for at in range(-1, len(tasks)):
                    events = []
                    for what in "kqv":
                        share, held = SHARE[kind][what], BUFFERS[kind][what]
                        for h in range(0, len(firsts), share):
                            free = h - (held - 1) * share
                            when = firsts[free] + (1 if what == "v" else -2) if free > 0 else -1
                            if when == at:
                                done += 1
                                events.append((what, h, tasks[firsts[max(free, 0)]], done))
                                for i in range(share):
                                    NEED[key, what, h + i] = done
                    SPLITS[key, at] = events
        _splits()

        def s5_tile(b):
            return 4 * (b % 4) + (16 if b < 4 else 0)

        @block.gpsimd
        def _(pool):
            n = [0]

            def link(ins):
                n[0] += 1
                ins.then_inc(pool_step, 1)
                pool.wait_ge(pool_step, n[0])

            def s5rows(name):
                return t[name].rearrange("o d (n g) p -> (o d n) (g p)", g=2)
            nc.gpsimd.memset(ones[:, :], 1.0).then_inc(flats_set, 1)
            nc.gpsimd.memset(one_row[:, :], 1.0).then_inc(flats_set, 1)
            nc.gpsimd.memset(flat[:, 0:1], 0.0).then_inc(flats_set, 1)
            nc.gpsimd.memset(flat[:, 1:2], 1.0).then_inc(flats_set, 1)
            pool.dma_start(rows[:, 0, :], s5rows("s5_lam_re")).then_inc(s5_in, 16)
            pool.dma_start(rows[:, 1, :], s5rows("s5_lam_im")).then_inc(s5_in, 16)
            pool.dma_start(rows[:, 2, 0:2], t["s5_log_step"].rearrange("o d (n g) -> (o d n) g", g=2)).then_inc(s5_in, 16)
            for i, (b, c) in enumerate((("s5_b_re", "s5_c_re"), ("s5_b_im", "s5_c_im"))):
                pool.dma_start(braw[:, i, :, :], t[b].rearrange("o d (n g) p c -> (g p) (o d n) c", g=2)).then_inc(s5_in, 16)
                pool.dma_start(craw[:, i, :, :], t[c].rearrange("o d (n g) c p -> (g c) (o d n) p", g=8)).then_inc(s5_in, 16)
            pool.wait_ge(s5_coef, 1)
            link(nc.gpsimd.tensor_copy(pw[:, 0, :], s5c[:, 1, :]))
            link(nc.gpsimd.tensor_copy(pw[:, 1, :], s5c[:, 2, :]))
            scr = s5w[:, 4096:5120]
            for tc_, ts_ in ((lo_c, lo_s), (hi_c, hi_s)):
                link(nc.gpsimd.memset(tc_[:, :, 0:1], 1.0))
                link(nc.gpsimd.memset(ts_[:, :, 0:1], 0.0))
                for k in range(4):
                    w = 1 << k
                    pc = pw[:, 0, :].unsqueeze(2).to_broadcast((P, TILES, w))
                    ps = pw[:, 1, :].unsqueeze(2).to_broadcast((P, TILES, w))
                    s1 = scr[:, 0:TILES * w].rearrange("p (n k) -> p n k", n=TILES)
                    s2 = scr[:, 512:512 + TILES * w].rearrange("p (n k) -> p n k", n=TILES)
                    link(nc.gpsimd.tensor_tensor(s1, tc_[:, :, 0:w], pc, ALU.mult))
                    link(nc.gpsimd.tensor_tensor(s2, ts_[:, :, 0:w], ps, ALU.mult))
                    link(nc.gpsimd.tensor_tensor(tc_[:, :, w:2 * w], s1, s2, ALU.subtract))
                    link(nc.gpsimd.tensor_tensor(s1, tc_[:, :, 0:w], ps, ALU.mult))
                    link(nc.gpsimd.tensor_tensor(s2, ts_[:, :, 0:w], pc, ALU.mult))
                    link(nc.gpsimd.tensor_tensor(ts_[:, :, w:2 * w], s1, s2, ALU.add))
                    link(nc.gpsimd.tensor_tensor(pw[:, 2, :], pw[:, 0, :], pw[:, 1, :], ALU.add))
                    link(nc.gpsimd.tensor_tensor(pw[:, 3, :], pw[:, 0, :], pw[:, 1, :], ALU.subtract))
                    link(nc.gpsimd.tensor_tensor(pw[:, 4, :], pw[:, 0, :], pw[:, 1, :], ALU.mult))
                    link(nc.gpsimd.tensor_tensor(pw[:, 0, :], pw[:, 2, :], pw[:, 3, :], ALU.mult))
                    link(nc.gpsimd.tensor_tensor(pw[:, 1, :], pw[:, 4, :], pw[:, 4, :], ALU.add))
            pool.wait_ge(s5_blk, 8)

            def make_table(b):
                if b >= 2:
                    pool.wait_ge(s5_w, b - 1)
                tile = s5_tile(b)
                hc_, hs_, lc_, ls_ = (x[:, tile:tile + 4, :] for x in (hi_c, hi_s, lo_c, lo_s))

                def up(x):
                    return x.unsqueeze(3).to_broadcast((P, 4, 16, 16))

                def low(x):
                    return x.unsqueeze(2).to_broadcast((P, 4, 16, 16))
                c4, s4 = (x[b % 2].rearrange("p r (a t) -> p r a t", a=16) for x in (tab_c, tab_s))
                one = rstd[:, :].rearrange("p (a t) -> p a t", a=16)
                link(nc.gpsimd.tensor_tensor(c4, up(hc_), low(lc_), ALU.mult))
                link(nc.gpsimd.tensor_tensor(s4, up(hs_), low(ls_), ALU.mult))
                link(nc.gpsimd.tensor_tensor(c4, c4, s4, ALU.subtract))
                link(nc.gpsimd.tensor_tensor(s4, up(hs_), low(lc_), ALU.mult))
                for r in range(4):
                    link(nc.gpsimd.tensor_tensor(one, hc_[:, r, :].unsqueeze(2).to_broadcast((P, 16, 16)),
                                                 ls_[:, r, :].unsqueeze(1).to_broadcast((P, 16, 16)), ALU.mult))
                    link(nc.gpsimd.tensor_tensor(s4[:, r], s4[:, r], one, ALU.add))
                pool.sem_inc(s5_tab, 1)

            make_table(0)
            for b in range(8):
                if b + 1 < 8:
                    make_table(b + 1)
                pool.wait_ge(s5_rot, b + 1)
                nc.gpsimd.tensor_tensor(z1, z1, z2, ALU.add).then_inc(s5_sum, 1)
                nc.gpsimd.tensor_tensor(z3, z3, z4, ALU.subtract).then_inc(s5_sum, 1)

            def taps(nf, l):
                mine, tmp = HC - DVE_CHUNKS, rstd[:, :]
                base = nf * (TAPS - 1) * mine * 2 + 1
                pool.wait_ge(conv_step, CONV_STEPS * nf + HC)
                if nf == 0:
                    pool.sem_inc(conv_pool, 1)
                with pool.Fori(1, TAPS) as k:
                    for i in range(mine):
                        c, at = DVE_CHUNKS + i, base + (k - 1) * mine * 2 + 2 * i
                        pool.wait_ge(conv_pool, at)
                        nc.gpsimd.tensor_tensor(tmp, conv_in[:, c, bass.ds(k, T)],
                                                tapc[:, l, bass.ds(4 * k + c, 1)].to_broadcast((P, T)), ALU.mult).then_inc(conv_pool, 1)
                        pool.wait_ge(conv_pool, at + 1)
                        nc.gpsimd.tensor_tensor(acc[:, c, :], acc[:, c, :], tmp, ALU.add).then_inc(conv_pool, 1)

            for key in TASKS:
                if kind_of(key) == "gqa":
                    taps(FULL_OF[key[:2]], 0 if key[1] == "0" else 1)
                for at in range(-1, len(TASKS[key])):
                    for what, h, _, done in SPLITS[key, at]:
                        src = operand(key, what, h)
                        high, rest = split_of(key, what, h)
                        pool.wait_ge(op_high, done)
                        nc.gpsimd.tensor_tensor(rest, src, high.bitcast(F32), ALU.subtract).then_inc(op_rest, 1)

        @block.tensor
        def _(pe):
            mm = nc.tensor.matmul

            def begin(u, banks):
                pe.wait_ge(rest_ready, u.count(1))
                for b, n in banks:
                    if not isinstance(n, int) or n > 0:
                        pe.wait_ge(bank_free[b], n)

            def parts(u, shape):
                return [w[:, u.first % n, :].rearrange("p (k n) -> p k n", k=shape)
                        for w, n in ((w_high, RAW), (w_rest, REST))]

            def product(dst, wh, wr, xh, xr, first, last, skip=False, weights_move=False):
                ops = ((wh, xh), (wh, xr), (wr, xh)) if not weights_move else ((wh, xh), (wr, xh), (wh, xr))
                for i, (w, x) in enumerate(ops):
                    a, b = (x, w) if weights_move else (w, x)
                    ins = mm(dst, a, b, start=first and i == 0, stop=last and i == 2, skip_group_check=skip)
                return ins

            def cols_unit(u, k, name, xh, xr, kc=DC):
                begin(u, [(k % 4, uses(name, k, u.turn))])
                wh, wr = parts(u, kc)
                for o in range(2):
                    for c in range(kc):
                        ins = product(L[:, k % 4, o * T:(o + 1) * T], wh[:, c, o * P:(o + 1) * P], wr[:, c, o * P:(o + 1) * P],
                                      xh[:, c, :], xr[:, c, :], c == 0, c == kc - 1)
                ins.then_inc(unit_done, 1)

            def cols_linear(name, before={}):
                def one(u, j, k):
                    if isinstance(j, int) and j in before:
                        before[j]()
                    cols_unit(u, k, name, n_high, n_rest)
                each_unit(pe, name, one)

            def rows_linear(name):
                def one(u, j, k):
                    begin(u, [(k % 4, uses(name, k, u.turn))])
                    wh, wr = parts(u, DC)
                    for a in range(2):
                        for c in range(DC):
                            ins = product(L[:, k % 4, a * T:(a + 1) * T], wh[:, c, :], wr[:, c, :],
                                          n_high[:, c, a * P:(a + 1) * P], n_rest[:, c, a * P:(a + 1) * P],
                                          c == 0, c == DC - 1, weights_move=True)
                    ins.then_inc(unit_done, 1)
                each_unit(pe, name, one)

            def acc_unit(u, xh, xr, at, first, last):
                wh, wr = parts(u, 2)
                for c in range(2):
                    for o in range(DC):
                        ins = product(L[:, o // 2, o % 2 * T:(o % 2 + 1) * T], wh[:, c, o * P:(o + 1) * P],
                                      wr[:, c, o * P:(o + 1) * P], xh[:, at + c, :] if isinstance(at, int) else xh[:, bass.ds(at + c, 1), :].rearrange("p a t -> p (a t)"),
                                      xr[:, at + c, :] if isinstance(at, int) else xr[:, bass.ds(at + c, 1), :].rearrange("p a t -> p (a t)"),
                                      first and c == 0 and o % 2 == 0, last and c == 1, skip=True)
                ins.then_inc(unit_done, 1)

            def acc_linear(name, xh, xr, before={}):
                first, n = FIRST[name], COUNT[name]
                if 0 in before:
                    before[0]()
                begin(Unit(first), [(b, BANK_USES[name][b]) for b in range(4)])
                acc_unit(Unit(first), xh, xr, 0, True, n == 1)

                turns = (n - 2) // 4
                if turns > 1:
                    with pe.Fori(0, turns) as i:
                        for k in range(1, 5):
                            u = Unit(first + k, i)
                            begin(u, [])
                            acc_unit(u, xh, xr, 8 * i + 2 * k, False, False)
                else:
                    turns = 0
                for k in range(1 + 4 * turns, n):
                    if k in before:
                        before[k]()
                    begin(Unit(first + k), [])
                    acc_unit(Unit(first + k), xh, xr, 2 * k, False, k == n - 1)

            def turn_tokens(k, rows_ap):
                pe.wait_ge(tokens_in, 16 * (k + 1))
                for b in range(4):
                    for c in range(2):
                        for a in range(2):
                            ins = nc.tensor.transpose(M[:, b, c * T + a * P:c * T + (a + 1) * P],
                                                      rows_ap[:, a, (2 * b + c) * P:(2 * b + c + 1) * P], ident[:, :])
                    ins.then_inc(turned, 1)

            rows2 = gate[:, :, :].rearrange("p a t -> p (a t)").rearrange("p (a n) -> p a n", a=2)

            def norm(k):
                pe.wait_ge(sq_ready, k + 1)
                for c in range(DC):
                    ins = mm(M[:, 0, 0:T], ones[:, :], m[:, c, :], start=c == 0, stop=c == DC - 1)
                ins.then_inc(sum_ready, 1)

            def attention(key, before, parts_of, values_of):
                tasks = TASKS[key]
                nk = keys_of(key)[1]
                exps, (th, tr) = store_of(key)
                evacuated(pe, before)

                def score(x):
                    if x["g"] >= 3:
                        pe.wait_ge(expd, x["g"] - 2)
                    pe.wait_ge(op_rest, max(NEED[key, "k", x["h"]], NEED[key, "q", x["h"]]))
                    pairs = parts_of(x["h"], x["map"], x["qt"])
                    (kh, kr), (qh, qr) = (split_of(key, what, x["h"]) for what in "kq")
                    for i, (q, kk) in enumerate(pairs):
                        ins = product(score_bank[x["g"] % 3][:, 0:nk], qh[q], qr[q], kh[kk], kr[kk], i == 0, i == len(pairs) - 1)
                    ins.then_inc(scores, 1)

                def turn(i, x):
                    pe.wait_ge(probs, x["group"] + 1)
                    if x["group"] >= 2:
                        pe.wait_ge(probs_T_rest, x["group"] - 1)
                    for c in range(nk // P):
                        ins = nc.tensor.transpose(turned_bank[x["group"] % 2][:, c * P:(c + 1) * P],
                                                  exps[(i - x["map"]) % 3][:, c * P:(c + 1) * P], ident[:, :])
                    ins.then_inc(probs_T, 1)

                def values(x):
                    pe.wait_ge(probs_T_rest, x["group"] + 1)
                    pe.wait_ge(op_rest, NEED[key, "v", x["h"]])
                    if x["head"] >= 2:
                        pe.wait_ge(o_ready, x["head"] - 1)
                    vh, vr = split_of(key, "v", x["h"])
                    for dst, sl in values_of(x["h"], head_bank[x["head"] % 2]):
                        for c in range(nk // P):
                            ins = product(dst, vh[:, c, sl], vr[:, c, sl], th[:, c, :], tr[:, c, :], c == 0, c == nk // P - 1)
                    ins.then_inc(attended, 1)
                score(tasks[0])
                score(tasks[1])
                for i, x in enumerate(tasks):
                    if i + 2 < len(tasks):
                        score(tasks[i + 2])
                    if x["whole"]:
                        turn(i, x)
                    if (key, i - 1) in END_OF:
                        values(tasks[i - 1])
                values(tasks[-1])
                pe.wait_ge(expd, tasks[-1]["g"] + 1)
                pe.wait_ge(o_ready, NHEADS[key] - 1)

            pe.wait_ge(consts_in, 16 * 6)
            pe.wait_ge(params_in, 16 * (len(COLS) + 1 + 4 + 2 * LAYERS))
            flat_m = m[:, :, :].rearrange("p a t -> p (a t)")
            nc.tensor.transpose(M[:, 0, 0:NVEC], flat_m[0:NVEC, 0:P], ident[0:NVEC, 0:NVEC])
            nc.tensor.transpose(M[:, 0, P:P + 6], flat_m[0:6, P:2 * P], ident[0:6, 0:6])
            for l in range(LAYERS):
                nc.tensor.transpose(M[:, 1, l * P:l * P + TAPS * HC], flat_m[0:TAPS * HC, (2 + l) * P:(3 + l) * P],
                                    ident[0:TAPS * HC, 0:TAPS * HC])
                ins = nc.tensor.transpose(M[:, 1, 256 + l * 48:256 + (l + 1) * 48], flat_m[0:48, 1024 + l * P:1024 + (l + 1) * P],
                                          ident[0:48, 0:48])
            ins.then_inc(turned, 1)
            pe.wait_ge(turned_out, 4)
            turn_tokens(0, rows2)
            norm(0)
            pe.wait_ge(n_ready, 1)
            cols_linear("mem_k")
            rows_linear("mem_v")
            turn_tokens(1, rows2)
            norm(1)
            pe.wait_ge(n_ready, 2)
            cols_linear("xa")

            def modulation(half):
                grp = half // 2
                if half == 0:
                    pe.wait_ge(silu_ready, 1)
                    pe.wait_ge(bank_free[0], after("xa", 0))
                    pe.wait_ge(bank_free[1], after("xa", 1))
                if half % 2 == 0 and grp >= 2:
                    pe.wait_ge(ada_row, grp - 1)
                for a in range(4 * half, 4 * half + 4):
                    v, kc = BEFORE_ADA + a, a % 8
                    pe.wait_ge(landed[v % 4], 16 * (v // 4 + 1))
                    for q in range(4):
                        ins = mm(L[32 * q:32 * q + 2, grp % 2, :], silu_c[:, kc, :], raw[:, v % 4, q * 512:(q + 1) * 512],
                                 start=kc == 0, stop=kc == 7, skip_group_check=True)
                    ins.then_inc(ada_done, 1)

            modulation(0)
            modulation(1)
            pe.wait_ge(s5_coef_rows, 1)
            for i in range(5):
                ins = nc.tensor.transpose(M[:, 0, i * TILES:(i + 1) * TILES], rows[:, 11 + i, :], ident[0:TILES, 0:TILES])
            ins.then_inc(s5_bt, 1)
            modulation(2)
            modulation(3)
            pe.wait_ge(s5_blk, 8)
            for q in range(8):
                if q >= 4:
                    pe.wait_ge(turned_out, 4 + q - 4 + 1)
                else:
                    pe.wait_ge(s5_coef, 1)
                for k in range(4):
                    i, nblk = (4 * q + k) % 16 // 8, (4 * q + k) % 8
                    if q < 4:
                        src = bblk[:, i, 4 * nblk:4 * nblk + 4, :, :].rearrange("p n g c -> p (n g c)")
                    else:
                        src = cblk[:, i, nblk, :, :].rearrange("p g k -> p (g k)")
                    ins = nc.tensor.transpose(M[:, q % 4, k * P:(k + 1) * P], src, ident[:, :])
                ins.then_inc(turned, 1)

            def s5_in_product(b):
                d, c = (1 if b < 4 else 0), b % 4
                pe.wait_ge(xa_ready, 1)
                if b == 0:
                    pe.wait_ge(turned_out, 4 + 8)
                else:
                    pe.wait_ge(s5_rot, b)
                for r in range(4):
                    x = (xaR if d else xaT)[32 * r:32 * r + 32, c, :]
                    for i in range(2):
                        ins = mm(M[:, r, i * T:(i + 1) * T], BT[32 * r:32 * r + 32, i, 4 * d + c, :], x, start=True, stop=True)
                ins.then_inc(s5_bu, 1)

            def s5_out_product(b):
                d, c = (1 if b < 4 else 0), b % 4
                pe.wait_ge(s5_w, b + 1)
                if b == 0:
                    evacuated(pe, "xa")
                if b >= 2:
                    pe.wait_ge(s5_yout, b - 1)
                for r in range(4):
                    for k, (i, z) in enumerate(((0, z1), (0, z3), (1, z5), (1, z6))):
                        ins = mm(L[32 * r:32 * r + 32, 2 + b % 2, 0:T], CT[:, i, 4 * d + c, 32 * r:32 * r + 32], z[:, r, :],
                                 start=k == 0, stop=k == 3, skip_group_check=True)
                ins.then_inc(s5_y, 1)

            for b in range(8):
                s5_in_product(b)
                modulation(4 + b)
                s5_out_product(b)
            pe.wait_ge(ada_rows_in, 16 * 8 * ADA_GROUPS)
            for l in range(LAYERS):
                ins = nc.tensor.transpose(M[:, 0, l * P:l * P + 96], ada_rows[:, l, :], ident[0:96, 0:96])
            ins.then_inc(turned, 1)

            pe.wait_ge(s5_yout, 8)
            pe.wait_ge(ada_row, ADA_GROUPS)
            rows_linear("zv")
            cols_linear("zu")
            pe.wait_ge(sgu_in, 16 * 4)
            pe.wait_ge(mod_ready, 1)
            for h in range(SGU_HEADS):
                ins = nc.tensor.transpose(M[:, 2 + h // 4, h % 4 * P:(h % 4 + 1) * P], sgu_raw[:, h, :], ident[:, :])
            ins.then_inc(turned, 1)
            pe.wait_ge(ln_ready, 2)
            pe.wait_ge(turned_out, 4 + 8 + 1)
            for h in range(SGU_HEADS):
                for a in range(2):
                    dst = M[:, h // 2, h % 2 * T + a * P:h % 2 * T + (a + 1) * P]
                    mm(dst, zv[:, a, h * P:(h + 1) * P], sgu_wt[:, h, :], start=True, stop=False)
                    ins = mm(dst, one_row[0:1, :], sgu_b[0:1, h * P:(h + 1) * P], start=False, stop=True)
            ins.then_inc(sgu_mm, 1)
            cols_linear("gate_a")

            name = "glu"
            pe.wait_ge(branch_ready, 1)
            u = Unit(FIRST[name])
            begin(u, [(0, BANK_USES[name][0]), (1, BANK_USES[name][1])])
            wh, wr = parts(u, HC)
            for o in range(HC):
                for c in range(HC):
                    ins = product(L[:, o // 2, o % 2 * T:(o % 2 + 1) * T], wh[:, c, o * P:(o + 1) * P], wr[:, c, o * P:(o + 1) * P],
                                  b_high[:, c, :], b_rest[:, c, :], c == 0, c == HC - 1)
            ins.then_inc(unit_done, 1)
            pe.wait_ge(branch_ready, 2)
            acc_linear("proj_a", b_high, b_rest)
            cols_linear("gate_b")
            pe.wait_ge(m_split, 1)
            cols_linear("proj_b")
            pe.wait_ge(m_split, 2)
            cols_linear("out")
            norm(2)
            pe.wait_ge(n_ready, 3)
            cols_linear("mem_q")
            evacuated(pe, "mem_q")

            attention("mem", "mem_q",
                      lambda h, mp, qt: [((slice(None), c, slice(qt * P, (qt + 1) * P)), (slice(None), c)) for c in range(2)],
                      lambda h, bank: [(bank[:, d * T:(d + 1) * T], slice(d * P, (d + 1) * P)) for d in range(2)])
            pe.wait_ge(m_split, 3)
            cols_linear("mem_o")

            def feed_forward(pre, k):
                norm(k)
                pe.wait_ge(n_ready, NREADY[k])
                cols_linear(pre + "ffn_up")
                pe.wait_ge(hid_ready, FC // 2 * (HID_OF[pre] + 1))
                acc_linear(pre + "ffn_down", hid_high, hid_rest)

            feed_forward("", 3)
            norm(4)
            for num, (p, l, s) in enumerate(PASSES):
                own = 0 if s == 0 else 2
                if p == "c0":
                    turn_tokens(2, rows2)
                norm(NORM_OF[p])
                pe.wait_ge(n_ready, NREADY[NORM_OF[p]])
                full = p != "c1"
                nf = FULL_OF.get(p)
                rx = ROPE_OF.get(p)

                def fourier_heads():
                    evacuated(pe, p + "four")
                    if nf:
                        pe.wait_ge(kd_dupc, num)
                    for c in range(HC):
                        for a in range(2):
                            ins = mm(M[:, c, a * T:(a + 1) * T], oT[:, c, a * P:(a + 1) * P], dft64[:, :], start=True, stop=True)
                    ins.then_inc(four1, 1)

                def fourier_tokens():
                    pe.wait_ge(dft_in, 16 * (nf + 1))
                    pe.wait_ge(four1c, 4 * (nf + 1))
                    for c in range(HC):
                        for i, (a, k) in enumerate(((0, 0), (0, 1), (1, 0), (1, 1))):
                            ins = mm(M[:, c // 2, c % 2 * T:(c % 2 + 1) * T], y1[:, c, a, k * P:(k + 1) * P], dft256[:, k, a, :],
                                     start=i == 0, stop=i == 3)
                    ins.then_inc(four2, 1)

                def turn_v():
                    evacuated(pe, p + "kv")
                    for a in range(2):
                        ins = nc.tensor.transpose(M[:, 3, a * P:(a + 1) * P], oT[:, 0, a * P:(a + 1) * P], ident[:, :])
                    ins.then_inc(k_ready, 1)

                def square_sums():
                    if full:
                        pe.wait_ge(branch_ready, 2 + 4 * nf + 1)
                    pe.wait_ge(qk_sq, num + 1)
                    for c in (range(HC + 1) if full else (HC,)):
                        ins = mm(M[:, c // 2, c % 2 * T:(c % 2 + 1) * T], pair_ones[:, :], t2[:, c, :], start=True, stop=True)
                    ins.then_inc(qk_sum, 1)

                def swap_halves(src, n, bank):
                    for c in range(n):
                        ins = mm(M[:, bank + c // 2, c % 2 * T:(c % 2 + 1) * T], swap[:, :], src[:, c, :], start=True, stop=True)
                    ins.then_inc(qk_rot, 1)

                def double_k():
                    if rx is not None:
                        pe.wait_ge(d_rot, 3 * rx + 1)
                    pe.wait_ge(qk_n, num + 1)
                    for h in range(2):
                        ins = mm(M[:, 2, h * T:(h + 1) * T], dup[:, h, :], qk[:, HC, :], start=True, stop=True)
                    ins.then_inc(kd_dup, 1)

                def swap_qk():
                    pe.wait_ge(qk_n, num + 1)
                    swap_halves(qk, HC + 1, 0)

                def swap_dq():
                    evacuated(pe, p + "dq")
                    pe.wait_ge(d_rot, 3 * rx + 1)
                    swap_halves(dq, HC, 0)

                def swap_dk():
                    evacuated(pe, p + "dk")
                    pe.wait_ge(kd_dupc, num + 1)
                    swap_halves(t1, HC, 2)

                if full:
                    cols_linear(p + "conv_u")
                    cols_linear(p + "conv_g")
                    cols_linear(p + "four")
                    cols_linear(p + "q")
                    fourier_heads()
                    cols_linear(p + "kv")
                    fourier_tokens()
                    cols_linear(p + "dq", before={1: turn_v})
                    cols_linear(p + "dk", before={1: square_sums})
                    rows_linear(p + "dv")
                else:
                    cols_linear(p + "kv")
                    turn_v()
                    cols_linear(p + "dk")
                    rows_linear(p + "dv")
                    square_sums()
                    double_k()
                    continue

                def conv_sums(k, src, at):
                    pe.wait_ge(conv_st, 2 * nf + k)
                    for c in range(HC):
                        ins = mm(M[:, 3, at:at + T], ones[:, :], src[:, c, :], start=c == 0, stop=c == HC - 1)
                    ins.then_inc(conv_stc, 1)

                def sum_acc():
                    pe.wait_ge(conv_pool, (nf + 1) * (TAPS - 1) * (HC - DVE_CHUNKS) * 2 + 1)
                    pe.wait_ge(v_ready, num + 1)
                    conv_sums(1, acc, 0)

                def branch(i, gate_before={}, proj_before={}):
                    cols_linear(p + f"gate{i}", before=gate_before)
                    pe.wait_ge(branch_ready, 2 + 4 * nf + i + 1)
                    acc_linear(p + f"proj{i}", b_high, b_rest, before=proj_before)

                branch(0, proj_before={0: sum_acc, 1: lambda: conv_sums(2, t2, T)})
                if rx is not None:
                    branch(1, gate_before={0: swap_qk, 3: lambda: (double_k(), swap_dq())}, proj_before={1: swap_dk})
                    pe.wait_ge(d_rot, 3 * rx + 3)
                else:
                    branch(1, gate_before={3: double_k})
                pe.wait_ge(kd_dupc, num + 1)

                def head_parts(a, qt):
                    return [((slice(a, a + HEAD), slice(qt * P, (qt + 1) * P)), (slice(a, a + HEAD), slice(None)))]
                attention(p + "gqa", p + "proj1", lambda h, mp, qt: head_parts(HEAD * (h % 2), qt),
                          lambda h, bank: [(bank[0:HEAD, 0:T], slice(0, HEAD))])
                branch(2)
                attention(p + "diff", p + "proj2", lambda h, mp, qt: head_parts(HEAD * mp, qt),
                          lambda h, bank: [(bank[:, 0:T], slice(0, P))])
                pe.wait_ge(on_sq, nf + 1)
                for c in range(HC):
                    ins = mm(M[:, c // 2, c % 2 * T:(c % 2 + 1) * T], ones[:, :], t1[:, c, :], start=True, stop=True)
                ins.then_inc(on_sum, 1)
                branch(3)
                pe.wait_ge(m_split, 3 + nf + 1)
                cols_linear(p + "out")
                feed_forward(p, NORM_OF[p] + 1)
            norm(12)
            pe.wait_ge(scaled, SCALED[12] + DC)
            for b in range(4):
                a, half = b // 2, b % 2
                for c in range(4):
                    ins = nc.tensor.transpose(M[:, b, c * P:(c + 1) * P], m[:, 4 * half + c, a * P:(a + 1) * P], ident[:, :])
                ins.then_inc(turned, 1)

        @block.scalar
        def _(act):
            A = nc.scalar.activation
            rows2 = gate[:, :, :].rearrange("p a t -> p (a t)").rearrange("p (a n) -> p a n", a=2)

            def start_units(first):
                for k in range(3):
                    split_high(act, Unit(first + k))

            def linear(name, one, beside={}):
                def step(u, j, k):
                    ahead_high(act, u, last_of(name))
                    if one is not None:
                        act.wait_ge(unit_done, u.count(1))
                        ins = one(j, k, u)
                        if ins is not None:
                            ins.then_inc(bank_free[k % 4], 1)
                    if isinstance(j, int) and j in beside:
                        beside[j]()
                each_unit(act, name, step)

            def out_to(name, dst, func=ACT.Copy, scale=1.0, beside={}):
                linear(name, lambda j, k, u: A(dst[:, 2 * j:2 * j + 2, :].rearrange("p a t -> p (a t)"), L[:, k % 4, :], func,
                                               scale=scale), beside)

            def rows_to(name, dst, func=ACT.Copy):
                linear(name, lambda j, k, u: A(dst[:, :, j * T:(j + 1) * T], L[:, k % 4, :].rearrange("p (a n) -> p a n", a=2), func))

            def norm(k, h, shift, split=True):
                act.wait_ge(h_ready, NORM_H[k])
                if split and k >= 5:
                    act.wait_ge(mod_ready, 1)
                A(m[:, :, :], h[:, :, :], ACT.Square).then_inc(sq_ready, 1)
                act.wait_ge(ms_ready, k + 1)
                A(rstd[:, :], rstd[:, :], ACT.Sqrt).then_inc(root_ready, 1)
                if split:
                    for c in range(DC):
                        act.wait_ge(scaled, SCALED[k] + c + 1)
                        A(n_high[:, c, :], m[:, c, :], ACT.Identity, bias=shift(c)).then_inc(n_high_ready, 1)

            def attention(key):
                nk = keys_of(key)[1]
                exps, (th, tr) = store_of(key)
                tasks = TASKS[key]

                def split(at):
                    for what, h, x, _ in SPLITS[key, at]:
                        if what != "v" and x["g"]:
                            act.wait_ge(scores, x["g"])
                        if what == "v" and x["head"]:
                            act.wait_ge(attended, x["head"])
                        src = operand(key, what, h)
                        A(split_of(key, what, h)[0], src, ACT.Copy).then_inc(op_high, 1)

                def exponentials(i, x):
                    act.wait_ge(neg_max, x["g"] + 1)
                    if i >= 3:
                        act.wait_ge(probs_T, tasks[i - 3]["group"] + 1)
                    A(exps[i % 3][:, 0:nk], score_bank[x["g"] % 3][:, 0:nk], ACT.Exp, bias=soft[:, x["g"] % 4, 0:1],
                      accum_out=soft[:, x["g"] % 4, 2:3]).then_inc(expd, 1)

                def turned_high(x):
                    act.wait_ge(probs_T, x["group"] + 1)
                    if x["qt"] == 0 and x["head"]:
                        act.wait_ge(attended, x["head"])
                    A(th[:, 0:nk // P, x["qt"] * P:(x["qt"] + 1) * P],
                      turned_bank[x["group"] % 2][:, 0:nk].rearrange("p (c q) -> p c q", q=P), ACT.Copy).then_inc(probs_T_high, 1)
                split(-1)
                exponentials(0, tasks[0])
                for i, x in enumerate(tasks):
                    split(i)
                    if i + 1 < len(tasks):
                        exponentials(i + 1, tasks[i + 1])
                    if i and tasks[i - 1]["whole"]:
                        turned_high(tasks[i - 1])
                turned_high(tasks[-1])

            act.wait_ge(flats_set, 4)
            act.wait_ge(turned_out, 4)
            for i, name in enumerate(("c_2", "c_ctx_2")):
                ins = A(silu_c[:, :, i], col(name, 0, DC), ACT.Silu)
            ins.then_inc(silu_ready, 1)
            act.wait_ge(lam_dot, 2 * LAYERS)
            for l in range(LAYERS):
                ins = A(lam[:, l, 2:4], lam[:, l, 0:2], ACT.Exp)
            ins.then_inc(lam_exp, 1)
            start_units(0)
            norm(0, hc, lambda c: flat[:, 0:1])
            out_to("mem_k", mem_kT)
            rows_to("mem_v", mem_v)
            norm(1, hx, lambda c: flat[:, 0:1])
            out_to("xa", xaT)
            act.wait_ge(s5_in, 16 * 7)
            A(rows[:, 2, 0:2], rows[:, 2, 0:2], ACT.Exp).then_inc(s5_act, 1)
            act.wait_ge(s5_act_in, 1)
            A(rows[:, 8, :], rows[:, 7, :], ACT.Sin).then_inc(s5_act, 1)
            A(rows[:, 9, :], rows[:, 7, :], ACT.Sin, scale=0.5).then_inc(s5_act, 1)
            A(rows[:, 10, :], rows[:, 3, :], ACT.Tanh, scale=0.5).then_inc(s5_act, 1)
            flatB = s5w[:, 6144:10240].rearrange("p (q k) -> p q k", q=8)

            def turned_block(q):
                act.wait_ge(turned, 1 + 8 + q + 1)
                A(flatB[:, q, :], M[:, q % 4, :], ACT.Copy).then_inc(turned_out, 1)

            def ada_out(grp):
                l, g = grp // 3, grp % 3
                act.wait_ge(ada_done, 8 * (grp + 1))
                if grp:
                    act.wait_ge(ada_rows_in, 16 * 8 * grp)
                flat_rope = rope[:, :, :].rearrange("p a t -> p (a t)")
                for q in range(4):
                    ins = A(flat_rope[32 * q:32 * q + 2, :], L[32 * q:32 * q + 2, grp % 2, :], ACT.Copy)
                    ins.then_inc(act_step, 1)
                act.wait_ge(act_step, 4 * (grp + 1))
                act.sem_inc(ada_row, 1)
                for q in range(4):
                    for s in range(2):
                        at = s * 48 + g * 16 + q * 4
                        act.dma_start(ada_rows[at:at + 4, l, :], flat_rope[32 * q + s:32 * q + s + 1, :]).then_inc(ada_rows_in, 16)
            ada_out(0)
            ada_out(1)
            for q in range(8):
                turned_block(q)
            for grp in range(2, ADA_GROUPS):
                ada_out(grp)
            act.wait_ge(ada_rows_in, 16 * 8 * ADA_GROUPS)
            act.dma_start(rope[:, :, :], consts["rope"].rearrange("p (a t) -> p a t", a=2)).then_inc(consts_in, 16)
            start_units(BEFORE_ADA)
            act.wait_ge(s5_yout, 8)
            act.dma_start(sgu_raw, t["sgu_w"][0].rearrange("h t s -> t h s")).then_inc(sgu_in, 16)
            act.dma_start(sgu_b, t["sgu_bias"][0].rearrange("(o h) t -> o (h t)", o=1)).then_inc(sgu_in, 16)
            lnv = m[:, :, :].rearrange("p a t -> p (a t)").rearrange("p (a n) -> p a n", a=2)
            act.dma_start(lnv[:, 0, :], t["sgu_ln_g"].partition_broadcast(P)).then_inc(sgu_in, 16)
            act.dma_start(lnv[:, 1, :], t["sgu_ln_b"].partition_broadcast(P)).then_inc(sgu_in, 16)
            act.wait_ge(s5_yout, 8)
            A(yT, yT, ACT.Gelu_apprx_tanh).then_inc(gelu_y, 1)
            rows_to("zv", zv, ACT.Gelu_apprx_tanh)
            out_to("zu", zu, ACT.Gelu_apprx_tanh)
            act.wait_ge(turned, 1 + 4 * 2 + 8 + 1 + 1)
            A(sgu_wt.rearrange("p h t -> p (h t)"), M[:, 2:4, :].rearrange("p a n -> p (a n)"), ACT.Copy).then_inc(turned_out, 1)
            for a in range(2):
                act.wait_ge(ln_sum, a + 1)
                A(work[:, 5760:6784], zv[:, a, :], ACT.Square, accum_out=stats[:, a, 2:3]).then_inc(ln_sq, 1)
                act.wait_ge(ln_sq, a + 1)
            act.wait_ge(ln_sum, 3)
            A(stats[:, :, 4], stats[:, :, 3], ACT.Sqrt).then_inc(ln_root, 1)
            out_to("gate_a", gate, ACT.Sigmoid)
            act.wait_ge(gelu_y, 1)
            A(b_high[:, :, :], yT, ACT.Copy).then_inc(glu_sig, 1)

            def glu_out(j, k, u):
                for b in range(2):
                    A(work[:, 5760 + 512 * b:5760 + 512 * (b + 1)], L[:, b, :], ACT.Sigmoid).then_inc(bank_free[b], 1)
            linear("glu", glu_out)
            act.wait_ge(glu_sig, 2)
            A(b_high[:, :, :], yT, ACT.Copy).then_inc(glu_sig, 1)
            linear("proj_a", None)
            act.wait_ge(merged, 4)
            out_to("gate_b", gate, ACT.Sigmoid)
            multiplied(act, "gate_b")
            act.wait_ge(sgu_out, 4)
            A(n_high[:, :, :], zu, ACT.Copy).then_inc(n_high_ready, 1)
            linear("proj_b", None)
            act.wait_ge(merged, 8)
            multiplied(act, "proj_b")
            A(n_high[:, :, :], m[:, :, :], ACT.Copy).then_inc(n_high_ready, 1)
            linear("out", None)
            norm(2, hx, lambda c: flat[:, 0:1])
            out_to("mem_q", zu, scale=float(D // MEM_HEADS) ** -0.5)
            evacuated(act, "mem_q")
            attention("mem")
            multiplied(act, "mem_q")
            act.wait_ge(o_ready, NHEADS["mem"])
            A(n_high[:, :, :], o_mem, ACT.Copy).then_inc(n_high_ready, 1)
            linear("mem_o", None)

            def feed_forward(pre, k, h, shift):
                norm(k, h, shift)
                base = FC // 2 * HID_OF[pre]

                def one(j, k2, u):
                    if k2 % 2:
                        return None
                    pair = u.turn * 2 + k2 // 2 if not isinstance(u.turn, int) else j // 2
                    buf = (k2 // 2) % 2
                    if isinstance(pair, int):
                        if pair >= 2:
                            act.wait_ge(hid_ready, base + pair - 1)
                    else:
                        act.wait_ge(hid_ready, base + pair - 1)
                    A(gate[:, 4 * buf:4 * buf + 2, :].rearrange("p a t -> p (a t)"), L[:, k2 % 4, :], ACT.Silu).then_inc(up_act, 1)
                    return None
                first, n = FIRST[pre + "ffn_up"], COUNT[pre + "ffn_up"]

                def step(u, j, k2):
                    ahead_high(act, u, UNITS)
                    if k2 % 2 == 0:
                        act.wait_ge(unit_done, u.count(1))
                        one(j, k2, u)
                for j in range(4):
                    step(Unit(first + j), j, j)
                with act.Fori(0, n // 4 - 1) as i:
                    for k2 in range(4):
                        ahead_high(act, Unit(first + 4 + k2, i), UNITS)
                        if k2 % 2 == 0:
                            act.wait_ge(unit_done, Unit(first + 4 + k2, i).count(1))
                            act.wait_ge(hid_ready, base + 2 * i + 2 + k2 // 2 - 1)
                            A(gate[:, 2 * k2:2 * k2 + 2, :].rearrange("p a t -> p (a t)"), L[:, k2, :],
                              ACT.Silu).then_inc(up_act, 1)
                for j in range(n // 4 * 4, n):
                    step(Unit(first + j), j, j % 4)
                linear(pre + "ffn_down", None)

            feed_forward("", 3, hx, lambda c: flat[:, 0:1])
            norm(4, hx, None, split=False)
            act.wait_ge(h_ready, 6)
            act.dma_start(rows2, t["ctx_2"][0].rearrange("(a p) n -> p a n", p=P)).then_inc(tokens_in, 16)
            for num, (p, l, s) in enumerate(PASSES):
                h = hc if s else hx
                own = 2 if s else 0
                full, nf, rx = p != "c1", FULL_OF.get(p), ROPE_OF.get(p)
                norm(NORM_OF[p], h, lambda c: mod[:, l, s * 48 + c:s * 48 + c + 1])
                kk = T if s else 0
                ch = slice(0, HC + 1) if full else slice(HC, HC + 1)
                if full:
                    act.dma_start(dft256, consts["dft256"].rearrange("p (s l k) -> p s l k", s=2, l=2)).then_inc(dft_in, 16)
                    conv_mid = conv_in[:, :, PAD:PAD + T]
                    act.wait_ge(conv_a, 2 * nf + 1)
                    linear(p + "conv_u", lambda j, k, u: A(conv_mid[:, 2 * j:2 * j + 2, :],
                                                           L[:, k % 4, :].rearrange("p (a t) -> p a t", a=2), ACT.Copy))
                    out_to(p + "conv_g", t1, ACT.Sigmoid)
                    out_to(p + "four", oT)
                    out_to(p + "q", qk)
                    act.wait_ge(four1, nf + 1)
                    act.wait_ge(conv_a, 2 * nf + 2)
                    for c in range(HC):
                        A(y1[:, c, :, :].rearrange("p a k -> p (a k)"), M[:, c, :], ACT.Copy).then_inc(four1c, 1)

                def kv_out(j, k, u):
                    A(qk[:, HC, :], L[:, k, 0:T], ACT.Copy)
                    return A(oT[:, 0, :], L[:, k, T:2 * T], ACT.Copy)
                linear(p + "kv", kv_out)

                def fourier_out():
                    act.wait_ge(four2, nf + 1)
                    for b in range(2):
                        A(b_high[:, 2 * b:2 * b + 2, :].rearrange("p a t -> p (a t)"), M[:, b, :], ACT.Copy).then_inc(z_ready, 1)

                def squares():
                    evacuated(act, p + "kv")
                    A(t2[:, ch, :], qk[:, ch, :], ACT.Square).then_inc(qk_sq, 1)

                def roots():
                    act.wait_ge(qk_ms, num + 1)
                    A(t2[:, ch, :], t2[:, ch, :], ACT.Sqrt).then_inc(qk_root, 1)

                def doubled_out():
                    act.wait_ge(kd_dup, num + 1)
                    A(kdup[:, :, kk:kk + T], M[:, 2, :].rearrange("p (h t) -> p h t", h=2), ACT.Copy).then_inc(kd_dupc, 1)

                if full:
                    out_to(p + "dq", dq, scale=HEAD ** -0.5,
                           beside={0: fourier_out, 1: squares})
                beside = {1: roots} if full else {}
                if s:
                    linear(p + "dk", lambda j, k, u: A(kdT[:, 2 * j:2 * j + 2, kk:kk + T],
                                                       L[:, k % 4, :].rearrange("p (a t) -> p a t", a=2), ACT.Copy), beside)
                else:
                    out_to(p + "dk", t1, beside=beside)
                linear(p + "dv", lambda j, k, u: A(vdrow[:, own:own + 2, j * T:(j + 1) * T],
                                                   L[:, k % 4, :].rearrange("p (a n) -> p a n", a=2), ACT.Copy))
                evacuated(act, p + "dv")
                if not full:
                    squares()
                    roots()
                    doubled_out()
                    continue

                def branch(i, gate_beside={}, proj_beside={}):
                    act.wait_ge(merged, 8 + 16 * nf + 4 * i)
                    out_to(p + f"gate{i}", gate, ACT.Sigmoid, beside=gate_beside)
                    linear(p + f"proj{i}", None, proj_beside)

                def conv_squares():
                    act.wait_ge(conv_n, 3 * nf + 1)
                    A(t2[:, 0:HC, :], acc, ACT.Square).then_inc(conv_st, 1)

                def conv_sqrt():
                    act.wait_ge(conv_n, 3 * nf + 2)
                    A(rstd[:, :], rstd[:, :], ACT.Sqrt).then_inc(conv_root, 1)

                def conv_silu():
                    act.wait_ge(conv_n, 3 * nf + 3)
                    multiplied(act, p + "proj0")
                    for c in range(HC):
                        A(acc[:, c, :], acc[:, c, :], ACT.Silu, bias=col("conv_ln_b_2", 4 * l + c)).then_inc(conv_sig, 1)
                    act.wait_ge(conv_sig, 4 * (nf + 1))
                    A(b_high[:, :, :], acc, ACT.Copy).then_inc(z_ready, 1)

                branch(0, proj_beside={0: conv_squares, 1: conv_sqrt})
                branch(1, gate_beside={0: conv_silu, 3: doubled_out})
                act.wait_ge(kd_dupc, num + 1)
                act.wait_ge(v_ready, num + 1)
                if rx is not None:
                    act.wait_ge(d_rot, 3 * rx + 3)
                attention(p + "gqa")
                act.wait_ge(o_ready, NHEADS[p + "gqa"])
                multiplied(act, p + "proj1")
                A(b_high[:, :, :], oT, ACT.Copy).then_inc(z_ready, 1)
                branch(2)
                attention(p + "diff")
                act.wait_ge(o_ready, NHEADS[p + "diff"])
                A(t1[:, 0:HC, :], oT, ACT.Square).then_inc(on_sq, 1)
                act.wait_ge(on_ms, nf + 1)
                A(t2[:, 0:HC, :], t2[:, 0:HC, :], ACT.Sqrt).then_inc(on_root, 1)
                act.wait_ge(on_ms, nf + 1)
                act.wait_ge(q_ready, nf + 1)
                multiplied(act, p + "proj2")
                A(b_high[:, :, :], oT, ACT.Copy).then_inc(z_ready, 1)
                branch(3)
                act.wait_ge(merged, 8 + 16 * (nf + 1))
                multiplied(act, p + "gate3")
                A(n_high[:, :, :], m[:, :, :], ACT.Copy).then_inc(n_high_ready, 1)
                linear(p + "out", None)
                feed_forward(p, NORM_OF[p] + 1, h, lambda c: mod[:, l, s * 48 + 24 + c:s * 48 + 25 + c])
            norm(12, hx, None, split=False)
            act.wait_ge(turned_out, 4 + 8 + 1 + 4)
            res = gate[:, :, :].rearrange("p a t -> p (a t)").rearrange("p (a n) -> p a n", a=2)
            act.dma_start(out[0].rearrange("(a p) n -> p a n", p=P), res).then_inc(stored, 16)
            act.wait_ge(stored, 16)

        @block.vector
        def _(dve):
            V = nc.vector
            n = [0]

            def link(ins):
                n[0] += 1
                ins.then_inc(dve_step, 1)
                dve.wait_ge(dve_step, n[0])

            def linear(name, one=None, beside={}):
                def step(u, j, k):
                    ahead_rest(dve, u, last_of(name))
                    if one is not None:
                        dve.wait_ge(unit_done, u.count(1))
                        one(j, k, u)
                    if isinstance(j, int) and j in beside:
                        beside[j]()
                each_unit(dve, name, step)

            def norm(k, h, gain, shift, split=True, dst=None):
                dve.wait_ge(sum_ready, k + 1)
                V.tensor_scalar(rstd[:, :], M[:, 0, 0:T], 1.0 / D, EPS, ALU.mult, ALU.add).then_inc(ms_ready, 1)
                dve.wait_ge(root_ready, k + 1)
                link(V.reciprocal(rstd[:, :], rstd[:, :]))
                for c in range(DC):
                    V.scalar_tensor_tensor(m[:, c, :] if dst is None else dst[:, c, :], h[:, c, :], gain(c), rstd[:, :],
                                           ALU.mult, ALU.mult).then_inc(scaled, 1)
                if split:
                    for c in range(DC):
                        dve.wait_ge(n_high_ready, NHIGH[k] + c + 1)
                        ins = V.scalar_tensor_tensor(n_rest[:, c, :], m[:, c, :], shift(c), n_high[:, c, :].bitcast(F32),
                                                     ALU.add, ALU.subtract)
                    ins.then_inc(n_ready, 1)

            def turn_out(h, base):
                for b in range(4):
                    dve.wait_ge(turned, base + b + 1)
                    ins = V.tensor_copy(h[:, 2 * b:2 * b + 2, :].rearrange("p a t -> p (a t)"), M[:, b, :])
                    n[0] += 1
                    ins.then_inc(dve_step, 1)
                dve.wait_ge(dve_step, n[0])
                dve.sem_inc(h_ready, 1)

            def n_split(src, count):
                dve.wait_ge(n_high_ready, count)
                V.tensor_tensor(n_rest[:, :, :], src, n_high[:, :, :].bitcast(F32), ALU.subtract).then_inc(m_split, 1)

            def add_to_h(name, h, gain):
                def one(j, k, u):
                    for o in range(2):
                        ins = V.scalar_tensor_tensor(h[:, 2 * j + o, :], L[:, k % 4, o * T:(o + 1) * T], gain(2 * j + o),
                                                     h[:, 2 * j + o, :], ALU.mult, ALU.add)
                    ins.then_inc(bank_free[k % 4], 1)
                linear(name, one)
                evacuated(dve, name)
                dve.sem_inc(h_ready, 1)

            def merge_rows(name, first, beside={}):
                linear(name, beside=beside)
                dve.wait_ge(unit_done, FIRST[name] + COUNT[name])
                for b in range(4):
                    g, mm_ = (x[:, 2 * b:2 * b + 2, :].rearrange("p a t -> p (a t)") for x in (gate, m))
                    if first:
                        V.tensor_tensor(mm_, g, L[:, b, :], ALU.mult).then_inc(bank_free[b], 1)
                    else:
                        V.tensor_tensor(g, g, L[:, b, :], ALU.mult).then_inc(bank_free[b], 1)
                evacuated(dve, name)
                for b in range(4):
                    g, mm_ = (x[:, 2 * b:2 * b + 2, :].rearrange("p a t -> p (a t)") for x in (gate, m))
                    if first:
                        dve.sem_inc(merged, 1)
                    else:
                        V.tensor_tensor(mm_, mm_, g, ALU.add).then_inc(merged, 1)

            def attention(key, out_of, negl=None):
                nk = keys_of(key)[1]
                exps, (th, tr) = store_of(key)
                tasks = TASKS[key]

                def negative_max(x):
                    dve.wait_ge(scores, x["g"] + 1)
                    V.tensor_reduce(soft[:, x["g"] % 4, 0:1], score_bank[x["g"] % 3][:, 0:nk], AX.X, ALU.max,
                                    negate=True).then_inc(neg_max, 1)

                def normalise(i, x):
                    s = x["g"] % 4
                    e = exps[i % 3][:, 0:nk]
                    dve.wait_ge(expd, x["g"] + 1)
                    link(V.reciprocal(soft[:, s, 3:4], soft[:, s, 2:3]))
                    if negl is None:
                        V.tensor_scalar(e, e, soft[:, s, 3:4], None, ALU.mult).then_inc(probs, 1)
                    elif x["map"] == 0:
                        link(V.tensor_scalar(e, e, soft[:, s, 3:4], None, ALU.mult))
                    else:
                        first = exps[(i - 1) % 3][:, 0:nk]
                        link(V.tensor_scalar(soft[:, s, 1:2], soft[:, s, 3:4], negl, None, ALU.mult))
                        V.scalar_tensor_tensor(first, e, soft[:, s, 1:2], first, ALU.mult, ALU.add).then_inc(probs, 1)

                def turned_rest(x):
                    dve.wait_ge(probs_T_high, x["group"] + 1)
                    at = slice(x["qt"] * P, (x["qt"] + 1) * P)
                    V.tensor_tensor(tr[:, 0:nk // P, at], turned_bank[x["group"] % 2][:, 0:nk].rearrange("p (c q) -> p c q", q=P),
                                    th[:, 0:nk // P, at].bitcast(F32), ALU.subtract).then_inc(probs_T_rest, 1)

                def head_out(x):
                    dve.wait_ge(attended, x["head"] + 1)
                    out_of(x["h"], head_bank[x["head"] % 2]).then_inc(o_ready, 1)
                negative_max(tasks[0])
                negative_max(tasks[1])
                for i, x in enumerate(tasks):
                    normalise(i, x)
                    if (key, i - 2) in END_OF:
                        head_out(tasks[i - 2])
                    if i + 2 < len(tasks):
                        negative_max(tasks[i + 2])
                    if i and tasks[i - 1]["whole"]:
                        turned_rest(tasks[i - 1])
                turned_rest(tasks[-1])
                head_out(tasks[-1])

            dve.wait_ge(consts_in, 16 * 6)
            dve.wait_ge(turned, 1)
            V.tensor_copy(cols[:, :], M[:, 0, 0:NVEC]).then_inc(turned_out, 1)
            V.tensor_copy(cols2[:, :], M[:, 0, P:P + 6]).then_inc(turned_out, 1)
            V.tensor_copy(tapc[:, :, :], M[:, 1, 0:2 * P].rearrange("p (l k) -> p l k", l=2)[:, :, 0:TAPS * HC]).then_inc(turned_out, 1)
            V.tensor_copy(b_ada[:, :, :], M[:, 1, 256:352].rearrange("p (l k) -> p l k", l=2)).then_inc(turned_out, 1)
            dve.wait_ge(lam_in, 16 * 4 * LAYERS)
            flat_m = m[:, :, :].rearrange("p a t -> p (a t)")
            for l in range(LAYERS):
                for i in range(2):
                    a, b = (flat_m[:, 512 + (4 * l + 2 * i + k) * HEAD:512 + (4 * l + 2 * i + k + 1) * HEAD] for k in range(2))
                    V.tensor_tensor_reduce(a, a, b, 1.0, 0.0, ALU.mult, ALU.add, lam[:, l, i:i + 1]).then_inc(lam_dot, 1)
            dve.wait_ge(lam_exp, 1)
            for l in range(LAYERS):
                link(V.tensor_tensor(lam[:, l, 4:5], lam[:, l, 3:4], lam[:, l, 2:3], ALU.subtract))
                link(V.tensor_scalar(lam[:, l, 5:6], lam[:, l, 4:5], -LAM_INIT[l], None, ALU.add))
                link(V.tensor_scalar(lam[:, l, 6:7], cols2[:, l:l + 1], 1.0 - LAM_INIT[l], None, ALU.mult))
                link(V.tensor_scalar(lam[:, l, 7:8], cols2[:, 2 + l:3 + l], HEAD ** -0.5, None, ALU.mult))
            turn_out(hc, 1)
            split_rest(dve, Unit(0))
            norm(0, hc, lambda c: col("mem_norm_g", c), lambda c: flat[:, 0:1])
            linear("mem_k")
            linear("mem_v")
            turn_out(hx, 5)
            norm(1, hx, lambda c: col("mix_norm_g", c), lambda c: flat[:, 0:1])
            linear("xa")
            evacuated(dve, "xa")
            V.tensor_copy(xaR, xaT[:, :, ::-1]).then_inc(xa_ready, 1)

            R = lambda i: rows[:, i, :]
            dve.wait_ge(s5_act, 1)
            for g in range(2):
                sl = slice(g * STATE, (g + 1) * STATE)
                for i in range(2):
                    link(V.tensor_scalar(rows[:, 3 + i, sl], rows[:, i, sl], rows[:, 2, g:g + 1], None, ALU.mult))
            big = 1.5 * 2.0 ** 23
            C1, C2 = 6.28125, 0.0019350051879882812
            C3 = float(2 * np.pi - C1 - C2)
            link(V.tensor_scalar(R(5), R(4), 1.0 / (2 * np.pi), big, ALU.mult, ALU.add))
            link(V.tensor_scalar(R(5), R(5), -big, None, ALU.add))
            link(V.scalar_tensor_tensor(R(6), R(5), -C1, R(4), ALU.mult, ALU.add))
            link(V.scalar_tensor_tensor(R(7), R(5), -C2, R(6), ALU.mult, ALU.add))
            link(V.scalar_tensor_tensor(R(6), R(5), -C3, R(7), ALU.mult, ALU.add))
            V.tensor_scalar(R(7), R(6), 3.1415925, -3.1415925, ALU.min, ALU.max).then_inc(s5_act_in, 1)
            dve.wait_ge(s5_act, 4)
            link(V.tensor_scalar(R(5), R(10), -1.0, 1.0, ALU.mult, ALU.add))
            link(V.reciprocal(R(5), R(5)))
            link(V.scalar_tensor_tensor(R(6), R(10), 2.0, R(5), ALU.mult, ALU.mult))
            link(V.tensor_scalar(R(11), R(6), 1.0, None, ALU.add))
            link(V.scalar_tensor_tensor(R(7), R(9), -2.0, R(9), ALU.mult, ALU.mult))
            link(V.tensor_scalar(R(12), R(7), 1.0, None, ALU.add))
            link(V.tensor_copy(R(13), R(8)))
            link(V.tensor_tensor(R(5), R(6), R(12), ALU.mult))
            link(V.tensor_tensor(R(5), R(5), R(7), ALU.add))
            link(V.tensor_tensor(R(6), R(11), R(13), ALU.mult))
            link(V.tensor_tensor(R(7), R(0), R(0), ALU.mult))
            link(V.tensor_tensor(R(9), R(1), R(1), ALU.mult))
            link(V.tensor_tensor(R(7), R(7), R(9), ALU.add))
            link(V.reciprocal(R(7), R(7)))
            link(V.tensor_tensor(R(9), R(5), R(0), ALU.mult))
            link(V.tensor_tensor(R(10), R(6), R(1), ALU.mult))
            link(V.tensor_tensor(R(9), R(9), R(10), ALU.add))
            link(V.tensor_tensor(R(14), R(9), R(7), ALU.mult))
            link(V.tensor_tensor(R(9), R(6), R(0), ALU.mult))
            link(V.tensor_tensor(R(10), R(5), R(1), ALU.mult))
            link(V.tensor_tensor(R(9), R(9), R(10), ALU.subtract))
            V.tensor_tensor(R(15), R(9), R(7), ALU.mult).then_inc(s5_coef_rows, 1)
            dve.wait_ge(s5_bt, 1)
            V.tensor_copy(s5c, M[:, 0, 0:5 * TILES].rearrange("p (i n) -> p i n", i=5)).then_inc(s5_coef, 1)
            dve.wait_ge(s5_coef, 1)
            cr, ci = (s5c[:, 3 + i, :].unsqueeze(2).to_broadcast((P, TILES, CH)) for i in range(2))
            for i, (x, y, op) in enumerate((((cr, 0), (ci, 1), ALU.subtract), ((cr, 1), (ci, 0), ALU.add))):
                link(V.tensor_tensor(bbar[:, i], braw[:, x[1]], x[0], ALU.mult))
                link(V.tensor_tensor(btmp, braw[:, y[1]], y[0], ALU.mult))
                link(V.tensor_tensor(bbar[:, i], bbar[:, i], btmp, op))
            dve.wait_ge(n_ready, 2)
            link(V.memset(bblk[0:STATE, :, :, 1, :], 0.0))
            link(V.memset(bblk[STATE:P, :, :, 0, :], 0.0))
            for i in range(2):
                V.tensor_copy(bblk[0:STATE, i, :, 0, :], bbar[0:STATE, i]).then_inc(s5_blk, 1)
                V.tensor_copy(bblk[STATE:P, i, :, 1, :], bbar[STATE:P, i]).then_inc(s5_blk, 1)
                for g in range(2):
                    V.tensor_scalar(cblk[:, i, :, g, :], craw[:, i, :, :], masks[:, 2 * i + g:2 * i + g + 1], None,
                                    ALU.mult).then_inc(s5_blk, 1)
            dve.wait_ge(turned_out, 4 + 8)

            def rotate_in(b):
                dve.wait_ge(s5_tab, b + 1)
                dve.wait_ge(s5_bu, b + 1)
                if b:
                    dve.wait_ge(s5_y, b)
                c_, s_ = tab_c[b % 2], tab_s[b % 2]
                re, im = M[:, :, 0:T], M[:, :, T:2 * T]
                V.tensor_tensor(z1, c_, re, ALU.mult).then_inc(dve_step, 1)
                V.tensor_tensor(z2, s_, im, ALU.mult).then_inc(dve_step, 1)
                V.tensor_tensor(z3, c_, im, ALU.mult).then_inc(dve_step, 1)
                V.tensor_tensor(z4, s_, re, ALU.mult).then_inc(dve_step, 1)
                n[0] += 4
                dve.wait_ge(dve_step, n[0])
                dve.sem_inc(s5_rot, 1)

            for b in range(8):
                d, c, tile = (1 if b < 4 else 0), b % 4, s5_tile(b)
                rotate_in(b)
                for half, (src, dst) in enumerate(((z1, z2), (z3, z4))):
                    dve.wait_ge(s5_sum, 2 * b + 2)
                    for r in range(4):
                        V.tensor_tensor_scan(dst[:, r, :], s5c[:, 0, tile + r:tile + r + 1].to_broadcast((P, T)), src[:, r, :],
                                             0.0, ALU.mult, ALU.add).then_inc(dve_step, 1)
                        n[0] += 1
                dve.wait_ge(dve_step, n[0])
                c_, s_ = tab_c[b % 2], tab_s[b % 2]
                V.tensor_tensor(z1, c_, z2, ALU.mult).then_inc(dve_step, 1)
                V.scalar_tensor_tensor(z3, s_, -1.0, z4, ALU.mult, ALU.mult).then_inc(dve_step, 1)
                V.tensor_tensor(z5, s_, z2, ALU.mult).then_inc(dve_step, 1)
                V.tensor_tensor(z6, c_, z4, ALU.mult).then_inc(dve_step, 1)
                n[0] += 4
                dve.wait_ge(dve_step, n[0])
                dve.sem_inc(s5_w, 1)
                dve.wait_ge(s5_y, b + 1)
                res = L[:, 2 + b % 2, 0:T]
                if d:
                    V.tensor_copy(yT[:, c, :], res[:, ::-1]).then_inc(s5_yout, 1)
                else:
                    link(V.tensor_tensor(yT[:, c, :], yT[:, c, :], res, ALU.add))
                    V.scalar_tensor_tensor(yT[:, c, :], xaT[:, c, :], col("s5_d", c), yT[:, c, :], ALU.mult,
                                           ALU.add).then_inc(s5_yout, 1)
            dve.wait_ge(turned, 1 + 8 + 8 + 1)
            for l in range(LAYERS):
                for s in range(2):
                    link(V.tensor_tensor(mod[:, l, s * 48:(s + 1) * 48], M[:, 0, l * P + s * 48:l * P + (s + 1) * 48], b_ada[:, l, :], ALU.add))
            for l in range(LAYERS):
                for s in range(2):
                    for i, (part, name) in enumerate(((1, "norm_mix_2"), (4, "norm_ffn_2"))):
                        at = s * 48 + part * 8
                        link(V.scalar_tensor_tensor(modg[:, l, s, i, :], mod[:, l, at:at + 8], 1.0, col(name, 8 * l, 8), ALU.add, ALU.mult))
            dve.sem_inc(mod_ready, 1)

            split_rest(dve, Unit(BEFORE_ADA))
            linear("zv")
            linear("zu")
            evacuated(dve, "zv")
            for a in range(2):
                link(V.tensor_reduce(stats[:, a, 0:1], zv[:, a, :], AX.X, ALU.add))
                link(V.tensor_scalar(stats[:, a, 1:2], stats[:, a, 0:1], -1.0 / D, None, ALU.mult))
                V.tensor_scalar(zv[:, a, :], zv[:, a, :], stats[:, a, 1:2], None, ALU.add).then_inc(ln_sum, 1)
            dve.wait_ge(ln_sq, 2)
            V.tensor_scalar(stats[:, :, 3], stats[:, :, 2], 1.0 / D, EPS, ALU.mult, ALU.add).then_inc(ln_sum, 1)
            dve.wait_ge(ln_root, 1)
            link(V.reciprocal(stats[:, :, 5], stats[:, :, 4]))
            dve.wait_ge(sgu_in, 16 * 4)
            lnv = m[:, :, :].rearrange("p a t -> p (a t)").rearrange("p (a n) -> p a n", a=2)
            for a in range(2):
                link(V.scalar_tensor_tensor(zv[:, a, :], zv[:, a, :], stats[:, a, 5:6], lnv[:, 0, :], ALU.mult, ALU.mult))
                V.tensor_tensor(zv[:, a, :], zv[:, a, :], lnv[:, 1, :], ALU.add).then_inc(ln_ready, 1)
            dve.wait_ge(sgu_mm, 1)
            evacuated(dve, "zu")
            for b in range(4):
                x = zu[:, 2 * b:2 * b + 2, :].rearrange("p a t -> p (a t)")
                V.tensor_tensor(x, x, M[:, b, :], ALU.mult).then_inc(sgu_out, 1)
            linear("gate_a")
            dve.wait_ge(glu_sig, 1)
            V.tensor_tensor(b_rest[:, :, :], yT, b_high[:, :, :].bitcast(F32), ALU.subtract).then_inc(branch_ready, 1)
            linear("glu")
            evacuated(dve, "glu")
            V.tensor_tensor(yT, yT, work[:, 5760:6784].rearrange("p (c t) -> p c t", c=HC), ALU.mult).then_inc(glu_sig, 1)
            dve.wait_ge(glu_sig, 3)
            V.tensor_tensor(b_rest[:, :, :], yT, b_high[:, :, :].bitcast(F32), ALU.subtract).then_inc(branch_ready, 1)
            dve.wait_ge(ln_ready, 2)
            evacuated(dve, "gate_a")
            merge_rows("proj_a", True)
            linear("gate_b")
            n_split(zu, NHIGH_EVENTS["yb"])

            def proj_b_out(j, k, u):
                g, mm_ = (x[:, 2 * j:2 * j + 2, :].rearrange("p a t -> p (a t)") for x in (gate, m))
                if j == 0:
                    evacuated(dve, "gate_b")
                V.tensor_tensor(g, g, L[:, k, :], ALU.mult).then_inc(bank_free[k], 1)
                dve.wait_ge(bank_free[k], after("proj_b", k))
                V.tensor_tensor(mm_, mm_, g, ALU.add).then_inc(merged, 1)
            linear("proj_b", proj_b_out)
            n_split(m[:, :, :], NHIGH_EVENTS["merged"])
            one = lambda c: flat[:, 1:2]
            zero = lambda c: flat[:, 0:1]
            add_to_h("out", hx, one)
            norm(2, hx, lambda c: col("xattn_norm_g", c), zero)
            linear("mem_q")
            attention("mem", lambda h, bank: V.tensor_copy(o_mem[:, 2 * h:2 * h + 2, :].rearrange("p a t -> p (a t)"), bank))
            n_split(o_mem, NHIGH_EVENTS["o_mem"])
            add_to_h("mem_o", hx, one)

            def feed_forward(pre, k, h, gain, shift, out_gain):
                norm(k, h, gain, shift)
                first, cnt = FIRST[pre + "ffn_up"], COUNT[pre + "ffn_up"]
                base = FC // 2 * HID_OF[pre]
                steps = n[0]

                def pair(i, k2, gates, done):
                    sg = gate[:, 2 * k2 - 2:2 * k2, :].rearrange("p a t -> p (a t)")
                    hh = gate[:, 2 * k2:2 * k2 + 2, :].rearrange("p a t -> p (a t)")
                    at = 4 * i + (k2 - 1)
                    if isinstance(at, int):
                        hi_, re_ = (x[:, at:at + 2, :].rearrange("p a t -> p (a t)") for x in (hid_high, hid_rest))
                    else:
                        hi_, re_ = (x[:, bass.ds(at, 2), :].rearrange("p a t -> p (a t)") for x in (hid_high, hid_rest))
                    dve.wait_ge(up_act, gates)
                    V.tensor_tensor(hh, sg, L[:, k2, :], ALU.mult).then_inc(dve_step, 1)
                    dve.wait_ge(dve_step, done + 1)
                    V.tensor_copy(hi_, hh).then_inc(dve_step, 1)
                    dve.wait_ge(dve_step, done + 2)
                    V.tensor_tensor(re_, hh, hi_.bitcast(F32), ALU.subtract).then_inc(hid_ready, 1)
                    dve.sem_inc(bank_free[k2 - 1], 1)
                    dve.sem_inc(bank_free[k2], 1)

                def turn(i):
                    for k2 in range(4):
                        u = Unit(first + k2, i)
                        ahead_rest(dve, u, UNITS)
                        if k2 % 2:
                            dve.wait_ge(unit_done, u.count(1))
                            pair(i, k2, base + 2 * i + k2 // 2 + 1, steps + 4 * i + 2 * (k2 // 2))
                turns = cnt // 4
                with dve.Fori(0, turns) as i:
                    turn(i)
                n[0] += 4 * turns
                for k2 in range(cnt - 4 * turns):
                    u = Unit(first + 4 * turns + k2)
                    ahead_rest(dve, u, UNITS)
                    if k2 % 2:
                        dve.wait_ge(unit_done, u.count(1))
                        pair(turns, k2, base + 2 * turns + k2 // 2 + 1, n[0])
                        n[0] += 2
                name = pre + "ffn_down"
                linear(name)
                dve.wait_ge(unit_done, FIRST[name] + COUNT[name])
                for b in range(4):
                    for o in range(2):
                        ins = V.scalar_tensor_tensor(h[:, 2 * b + o, :], L[:, b, o * T:(o + 1) * T], out_gain(2 * b + o),
                                                     h[:, 2 * b + o, :], ALU.mult, ALU.add)
                    ins.then_inc(bank_free[b], 1)
                evacuated(dve, name)
                dve.sem_inc(h_ready, 1)

            feed_forward("", 3, hx, lambda c: col("ffn_norm_g", c), zero, one)
            norm(4, hx, lambda c: col("final_norm_g", c), None, split=False, dst=hx)
            dve.wait_ge(scaled, SCALED[4] + DC)
            dve.sem_inc(h_ready, 1)
            turn_out(hc, 1 + 8 + 8 + 1 + 1)
            for num, (p, l, s) in enumerate(PASSES):
                h = hc if s else hx
                own, kk = (2, T) if s else (0, 0)
                full, nf, rx = p != "c1", FULL_OF.get(p), ROPE_OF.get(p)
                norm(NORM_OF[p], h, lambda c: modg[:, l, s, 0, c:c + 1], lambda c: mod[:, l, s * 48 + c:s * 48 + c + 1])

                def b_split(src):
                    V.tensor_tensor(b_rest[:, :, :], src, b_high[:, :, :].bitcast(F32), ALU.subtract).then_inc(branch_ready, 1)
                def v_out():
                    dve.wait_ge(k_ready, num + 1)
                    V.tensor_copy(vrow[:, own:own + 2, :], M[:, 3, 0:T].rearrange("p (a n) -> p a n", a=2)).then_inc(v_ready, 1)

                banks = ((0, 0, 2), (1, 2, 2), (2, 4, 1)) if full else ((2, 4, 1),)

                def mean_squares():
                    dve.wait_ge(qk_sum, num + 1)
                    for b, c0, w in banks:
                        link(V.tensor_scalar(t2[:, c0:c0 + w, :].rearrange("p a t -> p (a t)"), M[:, b, 0:w * T], 1.0 / HEAD, EPS, ALU.mult, ALU.add))
                    dve.sem_inc(qk_ms, 1)

                def normed(c):
                    dve.wait_ge(qk_root, num + 1)
                    link(V.reciprocal(t2[:, c, :], t2[:, c, :]))
                    g = lam[:, l, 7:8] if c < HC else cols2[:, 4 + l:5 + l]
                    link(V.scalar_tensor_tensor(qk[:, c, :], qk[:, c, :], g, t2[:, c, :], ALU.mult, ALU.mult))

                if not full:
                    linear(p + "kv")
                    v_out()
                    linear(p + "dk")
                    linear(p + "dv")
                    mean_squares()
                    normed(HC)
                    dve.sem_inc(qk_n, 1)
                    continue

                def taps(k0, n_):
                    with dve.Fori(k0, k0 + n_) as k:
                        for c in range(DVE_CHUNKS):
                            dve.wait_ge(conv_step, CONV_STEPS * nf + HC + DVE_CHUNKS * (k - 2) + c + 1)
                            V.scalar_tensor_tensor(acc[:, c, :], conv_in[:, c, bass.ds(k, T)], tapc[:, l, bass.ds(4 * k + c, 1)], acc[:, c, :],
                                                   ALU.mult, ALU.add).then_inc(conv_step, 1)

                def last_norm():
                    normed(3)
                    dve.sem_inc(qk_n, 1)

                def last_taps():
                    taps(28, 3)
                    dve.wait_ge(conv_step, CONV_STEPS * (nf + 1))
                    dve.sem_inc(conv_st, 1)

                def fourier_split():
                    dve.wait_ge(z_ready, 5 * nf + 2)
                    b_split(M[:, 0:2, :].rearrange("p b (c t) -> p (b c) t", c=2))

                def bc(i, w):
                    return rope[:, i, :].unsqueeze(1).to_broadcast((P, w, T))

                def rotate_q():
                    dve.wait_ge(consts_in, 16 * 7)
                    dve.wait_ge(qk_rot, 3 * rx + 1)
                    for b, c0, w in banks:
                        link(V.tensor_tensor(t2[:, c0:c0 + w, :], M[:, b, 0:w * T].rearrange("p (a t) -> p a t", a=w), bc(1, w), ALU.mult))
                    link(V.tensor_tensor(qk, qk, bc(0, 5), ALU.mult))

                def rotated_q():
                    V.tensor_tensor(qk, qk, t2, ALU.add).then_inc(d_rot, 1)

                def rotate_d(i, src, dst):
                    dve.wait_ge(qk_rot, 3 * rx + 2 + i)
                    dve.wait_ge(d_rot, 3 * rx + 1 + i)
                    rot = M[:, 2 * i:2 * i + 2, :].rearrange("p b (c t) -> p (b c) t", c=2)
                    link(V.tensor_tensor(t2[:, 0:HC, :], rot, bc(1, HC), ALU.mult))
                    link(V.tensor_tensor(src, src, bc(0, HC), ALU.mult))
                    V.tensor_tensor(dst, src, t2[:, 0:HC, :], ALU.add).then_inc(d_rot, 1)

                def conv_centre():
                    dve.wait_ge(conv_stc, 2 * nf + 1)
                    link(V.tensor_scalar(rstd[:, :], M[:, 3, 0:T], -1.0 / HALF, None, ALU.mult))
                    link(V.tensor_tensor(acc, acc, rstd[:, :].unsqueeze(1).to_broadcast((P, HC, T)), ALU.add))
                    dve.sem_inc(conv_n, 1)

                def conv_mean_square():
                    dve.wait_ge(conv_stc, 2 * nf + 2)
                    V.tensor_scalar(rstd[:, :], M[:, 3, T:2 * T], 1.0 / HALF, LN_EPS, ALU.mult, ALU.add).then_inc(conv_n, 1)

                def conv_scale():
                    dve.wait_ge(conv_root, nf + 1)
                    link(V.reciprocal(rstd[:, :], rstd[:, :]))
                    for c in range(HC):
                        link(V.scalar_tensor_tensor(acc[:, c, :], acc[:, c, :], col("conv_ln_g_2", 4 * l + c), rstd[:, :], ALU.mult, ALU.mult))
                    dve.sem_inc(conv_n, 1)

                def conv_split():
                    dve.wait_ge(z_ready, 5 * nf + 3)
                    b_split(acc)

                link(V.memset(conv_in[:, :, 0:PAD], 0.0))
                V.memset(conv_in[:, :, PAD + T:2 * PAD + T], 0.0).then_inc(conv_a, 1)
                linear(p + "conv_u")
                linear(p + "conv_g")
                evacuated(dve, p + "conv_g")
                mid = conv_in[:, :, PAD:PAD + T]
                V.tensor_tensor(mid, mid, t1[:, 0:HC, :], ALU.mult).then_inc(conv_a, 1)
                dve.wait_ge(conv_a, 2 * nf + 2)
                for c in range(HC):
                    V.tensor_scalar(acc[:, c, :], conv_in[:, c, 0:T], tapc[:, l, c:c + 1], col("conv_b_2", 4 * l + c),
                                    ALU.mult, ALU.add).then_inc(conv_step, 1)
                linear(p + "four", beside={0: lambda: taps(1, 3), 1: lambda: taps(4, 3)})
                linear(p + "q", beside={0: lambda: taps(7, 3), 1: lambda: taps(10, 3)})
                linear(p + "kv", beside={0: lambda: taps(13, 4)})
                linear(p + "dq", beside={0: lambda: taps(17, 4), 1: lambda: (v_out(), taps(21, 4))})
                linear(p + "dk", beside={0: lambda: (fourier_split(), taps(25, 3)), 1: mean_squares})
                linear(p + "dv", beside={0: lambda: normed(HC), 1: lambda: normed(0)})
                evacuated(dve, p + "dv")

                def gl(i, gate_beside={}, proj_beside={}):
                    linear(p + f"gate{i}", beside=gate_beside)
                    evacuated(dve, p + f"gate{i}")
                    merge_rows(p + f"proj{i}", i == 0, proj_beside)
                gl(0, {0: lambda: normed(1), 1: lambda: normed(2), 2: last_norm, 3: last_taps},
                   {0: conv_centre, 1: conv_mean_square})
                if rx is None:
                    gl(1, {0: conv_scale, 2: conv_split})
                else:
                    gl(1, {0: conv_scale, 1: rotate_q, 2: lambda: (rotated_q(), conv_split()), 3: lambda: rotate_d(0, dq, dq)},
                       {1: lambda: rotate_d(1, t1[:, 0:HC, :], kdT[:, :, 0:T])})

                def gqa_out(h_, bank):
                    a = HEAD * (h_ % 2)
                    return V.tensor_copy(oT[a:a + HEAD, h_ // 2, :], bank[0:HEAD, 0:T])
                attention(p + "gqa", gqa_out)
                dve.wait_ge(z_ready, 5 * nf + 4)
                b_split(oT)
                gl(2)
                attention(p + "diff", lambda h_, bank: V.tensor_copy(oT[:, h_, :], bank[:, 0:T]), negl=lam[:, l, 5:6])
                dve.wait_ge(on_sum, nf + 1)
                for b in range(2):
                    link(V.tensor_scalar(t2[:, 2 * b:2 * b + 2, :].rearrange("p a t -> p (a t)"), M[:, b, :], 1.0 / P, EPS, ALU.mult, ALU.add))
                dve.sem_inc(on_ms, 1)
                dve.wait_ge(on_root, nf + 1)
                link(V.reciprocal(t2[:, 0:HC, :], t2[:, 0:HC, :]))
                link(V.scalar_tensor_tensor(oT, oT, lam[:, l, 6:7], t2[:, 0:HC, :], ALU.mult, ALU.mult))
                dve.sem_inc(q_ready, 1)
                dve.wait_ge(z_ready, 5 * nf + 5)
                b_split(oT)
                gl(3)
                n_split(m[:, :, :], NHIGH_EVENTS[p])
                add_to_h(p + "out", h, lambda c: mod[:, l, s * 48 + 16 + c:s * 48 + 17 + c])
                feed_forward(p, NORM_OF[p] + 1, h, lambda c: modg[:, l, s, 1, c:c + 1],
                             lambda c: mod[:, l, s * 48 + 24 + c:s * 48 + 25 + c],
                             lambda c: mod[:, l, s * 48 + 40 + c:s * 48 + 41 + c])
            norm(12, hx, lambda c: col("final_norm_2", c), None, split=False)
            for b in range(4):
                dve.wait_ge(turned, 1 + 8 + 8 + 1 + 1 + 4 + b + 1)
                V.tensor_copy(gate[:, 2 * b:2 * b + 2, :].rearrange("p a t -> p (a t)"), M[:, b, :]).then_inc(turned_out, 1)


_INS = [
    "x", "mem", "mix_norm_g", "w_in", "s5_lam_re", "s5_lam_im", "s5_log_step", "s5_b_re", "s5_b_im", "s5_c_re",
    "s5_c_im", "s5_d", "s5_w_glu", "sgu_ln_g", "sgu_ln_b", "sgu_w", "sgu_bias", "w_proj_a", "w_proj_b", "w_out",
    "xattn_norm_g", "mem_norm_g", "w_q", "w_k", "w_v", "w_xo", "ffn_norm_g", "w_gate", "w_up", "w_down",
    "final_norm_g", "c_2", "ctx_2", "c_ctx_2", "w_ada_2", "b_ada_2", "norm_mix_2", "w_in_2", "w_four_2", "conv_w_2",
    "conv_b_2", "conv_ln_g_2", "conv_ln_b_2", "w_conv_2", "q_norm_2", "k_norm_2", "w_gqa_2", "lam_q1_2",
    "lam_k1_2", "lam_q2_2", "lam_k2_2", "diff_norm_2", "w_diff_2", "w_out_2", "norm_ffn_2", "w_ffn1_2",
    "w_ffn3_2", "w_ffn2_2", "final_norm_2",
]


def shape_constants():
    f = np.float32
    i, j = np.arange(P)[:, None], np.arange(P)[None, :]
    same64 = i // HEAD == j // HEAD
    ang64 = 2 * np.pi * ((i % HEAD) * (j % HEAD) % HEAD) / HEAD
    dft64 = np.concatenate([np.where(same64, np.cos(ang64), 0), np.where(same64, -np.sin(ang64), 0)], 1) / 8
    l, k = np.arange(T)[:, None], np.arange(T)[None, :]
    ang = 2 * np.pi * (l * k % T) / T
    dft256 = np.stack([np.cos(ang), np.sin(ang)]) / 16
    dft256 = dft256.reshape(2, 2, P, T).transpose(2, 0, 1, 3).reshape(P, -1)
    half = HEAD // 2
    inv = (f(10000.0) ** (-np.arange(0, half, 2, dtype=f) / f(half))).astype(f)
    tok = np.arange(T)
    angles = np.concatenate([(tok // 64).astype(f)[:, None] * inv, (tok % 64).astype(f)[:, None] * inv], 1).astype(f)
    angles = angles.astype(np.float64)[:, np.arange(P) % half].T
    rope = np.concatenate([np.cos(angles), np.sin(angles)], 1)
    a, b = np.arange(P) % HEAD, np.arange(P)
    swap = np.zeros((P, P))
    for c in range(P):
        swap[c + half if a[c] < half else c - half, c] = -1 if a[c] < half else 1
    dup = np.concatenate([(i == j % HEAD) * 1.0, (i == HEAD + j % HEAD) * 1.0], 1)
    even = (np.arange(P) // CH) % 2 == 0
    masks = np.stack([even * 1.0, ~even * 1.0, even * -1.0, ~even * -1.0], 1)
    out = dict(ident=np.eye(P), dft64=dft64, dft256=dft256, rope=rope, swap=swap, dup=dup, pair_ones=same64 * 1.0, masks=masks)
    return {k: np.ascontiguousarray(v).astype(f) for k, v in out.items()}


def kernel(**inputs):
    import concourse.bacc as _bacc
    from concourse.bass_utils import run_bass_kernel_spmd as _run

    nc = _bacc.Bacc("TRN2", target_bir_lowering=False, num_devices=1)
    arrays, t, consts = {}, {}, {}
    for name in _INS:
        a = np.ascontiguousarray(inputs[name])
        arrays[f"in_{name}"] = a
        t[name] = nc.dram_tensor(f"in_{name}", a.shape, mybir.dt.from_np(a.dtype), kind="ExternalInput").ap()
    for name, a in shape_constants().items():
        arrays[f"const_{name}"] = a
        consts[name] = nc.dram_tensor(f"const_{name}", a.shape, mybir.dt.from_np(a.dtype), kind="ExternalInput").ap()
    out = nc.dram_tensor("out_0", (1, T, D), F32, kind="ExternalOutput").ap()
    build(nc, t, out, consts)
    r = _run(nc, [arrays], core_ids=[0])
    return r.results[0]["out_0"]
```

```python
from contextlib import ExitStack

import concourse.bass as bass
from concourse import mybir
import numpy as np

F32 = mybir.dt.float32
F32R = mybir.dt.float32r
ALU = mybir.AluOpType
ACT = mybir.ActivationFunctionType
AX = mybir.AxisListType

P = 128
T = 256
D = 1024
DC = D // P
HALF = 512
HC = HALF // P
F = 2816
FC = F // P
GROUPS, STATE, CH = 32, 64, 16
TILES = 2 * GROUPS // 2
SGU_HEADS = 8
CHUNK = 128
MEM_HEADS = 4
TAPS = 31
PAD = TAPS // 2
HEAD = 64
DIFF_HEADS = 4
LAYERS = 2
EPS = 1e-6
LN_EPS = 1e-5
UNIT = 2048
RAW = 4
REST = 2
LAM_INIT = [0.8 - 0.6 * float(np.exp(-0.3 * l)) for l in range(LAYERS)]
ADA_GROUPS = 6

COLS = {}


def _place_columns():
    at = 0
    for name, rows in (("mix_norm_g", 8), ("mem_norm_g", 8), ("xattn_norm_g", 8), ("ffn_norm_g", 8),
                       ("final_norm_g", 8), ("norm_mix_2", 16), ("norm_ffn_2", 16), ("final_norm_2", 8),
                       ("c_2", 8), ("c_ctx_2", 8), ("s5_d", 4), ("conv_b_2", 8), ("conv_ln_g_2", 8),
                       ("conv_ln_b_2", 8)):
        COLS[name] = at
        at += rows
    return at


NVEC = _place_columns()


def schedule():
    s = [("mem_k", 4), ("mem_v", 4), ("xa", 2), ("ADA", 0),
         ("zv", 4), ("zu", 4), ("gate_a", 4), ("glu", 1), ("proj_a", 2), ("gate_b", 4), ("proj_b", 4),
         ("out", 4), ("mem_q", 4), ("mem_o", 4), ("ffn_up", 22), ("ffn_down", 11)]
    for p in ("c0", "x0", "c1", "x1"):
        if p == "c1":
            s += [(p + k, n) for k, n in (("kv", 1), ("dk", 2), ("dv", 2))]
        else:
            s += [(p + k, n) for k, n in (
                ("conv_u", 2), ("conv_g", 2), ("four", 2), ("q", 2), ("kv", 1), ("dq", 2), ("dk", 2), ("dv", 2),
                ("gate0", 4), ("proj0", 2), ("gate1", 4), ("proj1", 2), ("gate2", 4), ("proj2", 2),
                ("gate3", 4), ("proj3", 2), ("out", 4), ("ffn_up", 22), ("ffn_down", 11))]
    return s


ROW_KIND = ("proj_a", "proj0", "proj1", "proj2", "proj3", "ffn_down")


def row_kind(name):
    return name in ROW_KIND or name[2:] in ROW_KIND


FIRST, COUNT, BANK_USES = {}, {}, {}


def _number_units():
    at, uses = 0, [0] * 4
    for name, n in schedule():
        if name == "ADA":
            continue
        FIRST[name], COUNT[name], BANK_USES[name] = at, n, list(uses)
        at += n
        if row_kind(name):
            uses = [x + 1 for x in uses]
        elif name == "glu":
            uses = [uses[0] + 1, uses[1] + 1, uses[2], uses[3]]
        else:
            uses = [x + (n - b + 3) // 4 for b, x in enumerate(uses)]
    return at


UNITS = _number_units()
BEFORE_ADA = FIRST["zv"]
ADA_UNITS = LAYERS * 3 * DC


class Unit:

    def __init__(self, first, turn=0):
        self.first, self.turn = first, turn

    def plus(self, k):
        return Unit(self.first + k, self.turn)

    def count(self, k=0):
        return self.first + 4 * self.turn + k

    def quarter(self):
        at = self.first + (ADA_UNITS if self.first >= BEFORE_ADA else 0)
        return at // 4 + 1 + self.turn


def build(nc, t, out, consts):
    ctx = ExitStack()
    with ctx:
        def sb(name, shape, dt=F32):
            return ctx.enter_context(nc.sbuf_tensor(name, shape, dt))

        def sem(name):
            return ctx.enter_context(nc.semaphore(name))

        raw = sb("raw", [P, RAW, UNIT])
        w_high = sb("w_high", [P, RAW, UNIT], F32R)
        over = ExitStack()
        with over:
            s5z = over.enter_context(nc.sbuf_tensor("s5z", [P, 4096], F32))
        w_rest = sb("w_rest", [P, REST, UNIT], F32R)
        n_high = sb("n_high", [P, DC, T], F32R)
        n_rest = sb("n_rest", [P, DC, T], F32R)
        hx = sb("hx", [P, DC, T])
        hc = sb("hc", [P, DC, T])
        kv = sb("kv", [P, 5632])
        ident = sb("ident", [P, P])
        dft64 = sb("dft64", [P, 2 * P])
        rope = sb("rope", [P, 2, T])
        ada_rows = sb("ada_rows", [96, LAYERS, P])
        b_ada = sb("b_ada", [P, LAYERS, 48])
        swap = sb("swap", [P, P])
        dup = sb("dup", [P, 2, P])
        pair_ones = sb("pair_ones", [P, P])
        ones = sb("ones", [P, P])
        one_row = sb("one_row", [1, P])
        masks = sb("masks", [P, 4])
        cols = sb("cols", [P, NVEC])
        cols2 = sb("cols2", [P, 6])
        tapc = sb("tapc", [P, LAYERS, TAPS * HC])
        mod = sb("mod", [P, LAYERS, 96])
        modg = sb("modg", [P, LAYERS, 2, 2, DC])
        silu_c = sb("silu_c", [P, DC, 2])
        flat = sb("flat", [P, 2])
        lam = sb("lam", [P, LAYERS, 8])
        stats = sb("stats", [P, 2, 8])
        soft = sb("soft", [P, 4, 4])
        rstd = sb("rstd", [P, T])
        m = sb("m", [P, DC, T])
        gate = sb("gate", [P, DC, T])

        over = ExitStack()
        with over:
            hid_high = over.enter_context(nc.sbuf_tensor("hid_high", [P, FC, T], F32R))
            hid_rest = over.enter_context(nc.sbuf_tensor("hid_rest", [P, FC, T], F32R))
        over = ExitStack()
        with over:
            b_high = over.enter_context(nc.sbuf_tensor("b_high", [P, HC, T], F32R))
            b_rest = over.enter_context(nc.sbuf_tensor("b_rest", [P, HC, T], F32R))
            again = ExitStack()
            with again:
                work = again.enter_context(nc.sbuf_tensor("work", [P, 9216], F32))
            work_r = over.enter_context(nc.sbuf_tensor("work_r", [P, 9216], F32R))
        over = ExitStack()
        with over:
            s5w = over.enter_context(nc.sbuf_tensor("s5w", [P, 11264], F32))

        dft256 = work[:, 0:1024].rearrange("p (s l k) -> p s l k", s=2, l=2)
        conv_in = work[:, 1024:1024 + HC * (T + 2 * PAD)].rearrange("p (c t) -> p c t", c=HC)
        acc = work[:, 2176:3200].rearrange("p (c t) -> p c t", c=HC)
        qk = work[:, 3200:4480].rearrange("p (c t) -> p c t", c=HC + 1)
        dq = work[:, 4480:5504].rearrange("p (c t) -> p c t", c=HC)
        t1 = work[:, 5504:6784].rearrange("p (c t) -> p c t", c=HC + 1)
        t2 = work[:, 6784:8064].rearrange("p (c t) -> p c t", c=HC + 1)
        oT = work[:, 8064:9088].rearrange("p (c t) -> p c t", c=HC)
        zu = work[:, 0:2048].rearrange("p (c t) -> p c t", c=DC)
        zv = work[:, 2048:4096].rearrange("p (a n) -> p a n", a=2)
        o_mem = work[:, 2048:4096].rearrange("p (c t) -> p c t", c=DC)
        sgu_wt = work[:, 7040:8064].rearrange("p (h t) -> p h t", h=SGU_HEADS)
        sgu_raw = work[:, 4480:5504].rearrange("p (h t) -> p h t", h=SGU_HEADS)
        sgu_b = work[0:1, 8064:9088]
        mem_kT = kv[:, 0:2048].rearrange("p (c t) -> p c t", c=DC)
        mem_v = kv[:, 2048:4096].rearrange("p (a n) -> p a n", a=2)
        kdup = kv[:, 0:1024].rearrange("p (h t) -> p h t", h=2)
        vrow = kv[:, 1024:1536].rearrange("p (a n) -> p a n", a=4)
        kdT = kv[:, 1536:3584].rearrange("p (h t) -> p h t", h=HC)
        vdrow = kv[:, 3584:5632].rearrange("p (a n) -> p a n", a=4)
        STORE = {"mem": dict(k=4096, v=5120, q=6144, turned=7168, turned_rest=7680, exp=8192, step=256),
                 "gqa": dict(k=0, v=1024, q=1536, turned_rest=2048, exp=5504, turned=7040, step=512),
                 "diff": dict(k=0, v=2048, q=3072, turned_rest=3328, exp=5504, turned=7040, step=512)}
        SHARE = {"mem": dict(k=1, q=1, v=1), "gqa": dict(k=4, q=2, v=4), "diff": dict(k=1, q=1, v=1)}
        BUFFERS = {"mem": dict(k=1, q=2, v=1), "gqa": dict(k=1, q=2, v=1), "diff": dict(k=2, q=1, v=1)}
        WORDS = {"mem": dict(k=512, q=512, v=512), "gqa": dict(k=512, q=256, v=256), "diff": dict(k=512, q=256, v=512)}

        def kind_of(key):
            return key if key == "mem" else key[2:]

        def store_of(key):
            at = STORE[kind_of(key)]
            exps = [work[:, at["exp"] + i * at["step"]:at["exp"] + (i + 1) * at["step"]] for i in range(3)]
            n = 2 * at["step"]
            return exps, [work_r[:, at[x]:at[x] + n].rearrange("p (c q) -> p c q", q=T) for x in ("turned", "turned_rest")]

        def s5a(i):
            return s5w[:, 1024 * i:1024 * (i + 1)]
        q4 = "p (r t) -> p r t"
        tab_c = [s5a(0).rearrange(q4, r=4), s5a(2).rearrange(q4, r=4)]
        tab_s = [s5a(1).rearrange(q4, r=4), s5a(3).rearrange(q4, r=4)]
        zset = [(m[:, 0:4, :], gate[:, 0:4, :], s5a(4).rearrange(q4, r=4), s5a(5).rearrange(q4, r=4)),
                [s5z[:, 1024 * i:1024 * (i + 1)].rearrange(q4, r=4) for i in range(4)]]
        z_re, z_im = m[:, 4:8, :], gate[:, 4:8, :]
        BT = s5w[:, 6144:8192].rearrange("p (i n k) -> p i n k", i=2, n=8)
        CT = s5w[:, 8192:10240].rearrange("p (i n k) -> p i n k", i=2, n=8)
        hi_c = s5w[:, 10240:10752].rearrange("p (n k) -> p n k", n=TILES)
        hi_s = s5w[:, 10752:11264].rearrange("p (n k) -> p n k", n=TILES)
        lo_c = kv[:, 4096:4608].rearrange("p (n k) -> p n k", n=TILES)
        lo_s = kv[:, 4608:5120].rearrange("p (n k) -> p n k", n=TILES)
        s5c = kv[:, 5120:5280].rearrange("p (i n) -> p i n", i=5)
        pw = kv[:, 5280:5472].rearrange("p (i n) -> p i n", i=6)
        xaT, xaR, yT = hc[:, 0:4, :], hc[:, 4:8, :], hc[:, 4:8, :]
        braw = s5w[:, 0:1024].rearrange("p (i n c) -> p i n c", i=2, n=TILES)
        bbar = s5w[:, 1024:2048].rearrange("p (i n c) -> p i n c", i=2, n=TILES)
        btmp = s5w[:, 2048:2560].rearrange("p (n c) -> p n c", n=TILES)
        craw = s5w[:, 3072:4096].rearrange("p (i n k) -> p i n k", i=2, n=8)
        bblk = m[:, :, :].rearrange("p a t -> p (a t)").rearrange("p (i n g c) -> p i n g c", i=2, n=TILES, g=2)
        cblk = hx[:, :, :].rearrange("p a t -> p (a t)").rearrange("p (i n g k) -> p i n g k", i=2, n=8, g=2)
        rows = s5w[0:TILES, 4096:4096 + 16 * P].rearrange("p (i k) -> p i k", i=16)

        L = ctx.enter_context(nc.psum_tensor("L", [P, 4, 512], F32))
        M = ctx.enter_context(nc.psum_tensor("M", [P, 4, 512], F32))

        score_bank = (M[:, 0, :], M[:, 1, :])
        turned_bank = (M[:, 2, :], L[:, 3, :])
        head_bank = M[:, 3, :]

        landed = [sem(f"landed{i}") for i in range(RAW)]
        high_ready, rest_ready, unit_done, ada_done = sem("high_ready"), sem("rest_ready"), sem("unit_done"), sem("ada_done")
        bank_free = [sem(f"bank_free{i}") for i in range(4)]
        consts_in, params_in, s5_in, tokens_in = sem("consts_in"), sem("params_in"), sem("s5_in"), sem("tokens_in")
        sgu_in, dft_in, lam_in = sem("sgu_in"), sem("dft_in"), sem("lam_in")
        flats_set, dve_step, act_step, pool_step = sem("flats_set"), sem("dve_step"), sem("act_step"), sem("pool_step")
        turned, turned_out = sem("turned"), sem("turned_out")
        sq_ready, sum_ready, ms_ready, root_ready, scaled, n_high_ready, n_ready = [
            sem(x) for x in ("sq_ready", "sum_ready", "ms_ready", "root_ready", "scaled", "n_high_ready", "n_ready")]
        ada_row, ada_rows_in, mod_ready = sem("ada_row"), sem("ada_rows_in"), sem("mod_ready")
        silu_ready = sem("silu_ready")
        s5_act_in, s5_act, s5_coef_rows, s5_coef, s5_blk, s5_tab = [
            sem(x) for x in ("s5_act_in", "s5_act", "s5_coef_rows", "s5_coef", "s5_blk", "s5_tab")]
        s5_bt, s5_bu, s5_rot, s5_scan, s5_w, s5_y, s5_yout, xa_ready = [
            sem(x) for x in ("s5_bt", "s5_bu", "s5_rot", "s5_scan", "s5_w", "s5_y", "s5_yout", "xa_ready")]
        gelu_y, branch_ready, glu_sig, gate_ready, merged = [
            sem(x) for x in ("gelu_y", "branch_ready", "glu_sig", "gate_ready", "merged")]
        ln_sum, ln_sq, ln_root, ln_ready, sgu_mm, sgu_out, m_split = [
            sem(x) for x in ("ln_sum", "ln_sq", "ln_root", "ln_ready", "sgu_mm", "sgu_out", "m_split")]
        h_ready, q_ready, k_ready, v_ready, scores, neg_max, expd, probs, probs_T, probs_T_high, attended, o_ready = [
            sem(x) for x in ("h_ready", "q_ready", "k_ready", "v_ready", "scores", "neg_max", "expd", "probs",
                             "probs_T", "probs_T_high", "attended", "o_ready")]
        probs_T_rest, op_high, op_rest = sem("probs_T_rest"), sem("op_high"), sem("op_rest")
        up_act, hid_ready = sem("up_act"), sem("hid_ready")
        z_ready, four1, four1c, four2 = sem("z_ready"), sem("four1"), sem("four1c"), sem("four2")
        conv_a, conv_sig, conv_step, conv_st, conv_stc, conv_root, conv_n, conv_pool = [
            sem(x) for x in ("conv_a", "conv_sig", "conv_step", "conv_st", "conv_stc", "conv_root", "conv_n", "conv_pool")]
        qk_sq, qk_sum, qk_ms, qk_root, qk_n, qk_rot, d_rot, kd_dup, kd_dupc = [
            sem(x) for x in ("qk_sq", "qk_sum", "qk_ms", "qk_root", "qk_n", "qk_rot", "d_rot",
                             "kd_dup", "kd_dupc")]
        on_sq, on_sum, on_ms, on_root = sem("on_sq"), sem("on_sum"), sem("on_ms"), sem("on_root")
        lam_dot, lam_exp = sem("lam_dot"), sem("lam_exp")
        stored = sem("stored")

        block = ctx.enter_context(nc.Block())

        def col(name, c, n=1):
            return cols[:, COLS[name] + c:COLS[name] + c + n]

        def each_unit(eng, name, body, start=0):
            first, n = FIRST[name] + start, COUNT[name] - start
            turns = n // 4
            if turns > 1:
                with eng.Fori(0, turns) as i:
                    for k in range(4):
                        body(Unit(first + k, i), start + 4 * i + k, k)
            else:
                turns = 0
            for k in range(4 * turns, n):
                body(Unit(first + k), start + k, start + k)

        def uses(name, k, turn=0):
            return BANK_USES[name][k % 4] + k // 4 + turn

        def split_high(act, u):
            act.wait_ge(landed[u.first % 4 if u.first < BEFORE_ADA else (u.first + ADA_UNITS) % 4], 16 * u.quarter())
            if u.first >= 4:
                act.wait_ge(unit_done, u.count(-3))
            nc.scalar.activation(w_high[:, u.first % 4, :], raw[:, u.first % 4, :], ACT.Copy).then_inc(high_ready, 1)

        def split_rest(dve, u):
            dve.wait_ge(high_ready, u.count(1))
            if u.first >= 2:
                dve.wait_ge(unit_done, u.count(-1))
            nc.vector.tensor_tensor(w_rest[:, u.first % 2, :], raw[:, u.first % 4, :],
                                    w_high[:, u.first % 4, :].bitcast(F32), ALU.subtract).then_inc(rest_ready, 1)

        def ahead_high(act, u, last):
            if u.first + 3 < last:
                split_high(act, u.plus(3))

        def ahead_rest(dve, u, last):
            if u.first + 1 < last:
                split_rest(dve, u.plus(1))

        def last_of(name):
            return BEFORE_ADA if FIRST[name] < BEFORE_ADA else UNITS


        @block.sync
        def _(sp):
            for k, (name, dst) in enumerate((("ident", ident), ("dft64", dft64), ("swap", swap),
                                             ("pair_ones", pair_ones), ("masks", masks))):
                sp.dma_start(dst[:, :], consts[name]).then_inc(consts_in, 16)
            sp.dma_start(gate[:, :, :].rearrange("p a t -> p (a t)").rearrange("p (a n) -> p a n", a=2),
                         t["mem"][0].rearrange("(a p) n -> p a n", p=P)).then_inc(tokens_in, 16)

            def rows_of(ap):
                return ap.rearrange("l (r k) -> (l r) k", k=P) if len(ap.shape) == 2 else ap.rearrange("(r k) -> r k", k=P)
            at = 0
            flat_m = m[:, :, :].rearrange("p a t -> p (a t)")
            for name in COLS:
                src = rows_of(t[name])
                sp.dma_start(flat_m[at:at + src.shape[0], 0:P], src).then_inc(params_in, 16)
                at += src.shape[0]
            sp.dma_start(flat_m[0:2, P:2 * P], t["diff_norm_2"]).then_inc(params_in, 16)
            for k, name in enumerate(("q_norm_2", "k_norm_2")):
                for h in range(2):
                    sp.dma_start(flat_m[2 + 2 * k:4 + 2 * k, P + h * HEAD:P + (h + 1) * HEAD], t[name]).then_inc(params_in, 16)
            for l in range(LAYERS):
                sp.dma_start(flat_m[0:TAPS * HC, (2 + l) * P:(3 + l) * P],
                             t["conv_w_2"][l].rearrange("k (c n) -> (k c) n", n=P)).then_inc(params_in, 16)
                sp.dma_start(flat_m[0:48, 1024 + l * P:1024 + (l + 1) * P],
                             t["b_ada_2"][l].rearrange("(r k) -> r k", k=P)).then_inc(params_in, 16)
            for k, name in enumerate(("lam_q1_2", "lam_k1_2", "lam_q2_2", "lam_k2_2")):
                for l in range(LAYERS):
                    sp.dma_start(flat_m[:, 512 + (4 * l + k) * HEAD:512 + (4 * l + k + 1) * HEAD],
                                 t[name][l:l + 1, :].partition_broadcast(P)).then_inc(lam_in, 16)

            def load(u, src, dst=None):
                slot = u.first % 4
                if u.first >= 4:
                    if BEFORE_ADA <= u.first < BEFORE_ADA + 4:
                        sp.wait_ge(ada_done, ADA_UNITS - 4 + u.first - BEFORE_ADA + 1)
                    else:
                        sp.wait_ge(rest_ready, u.count(-3))
                sp.dma_start(raw[:, slot, :] if dst is None else dst, src).then_inc(landed[slot], 16)

            def load_cols(name, w, at, step=256):
                wv = w.rearrange("(k p) n -> p k n", p=P)
                k = wv.shape[1]
                each_unit(sp, name, lambda u, j, _: load(
                    u, wv[:, :, bass.ds(at + step * j, step)],
                    raw[:, u.first % 4, :].rearrange("p (k n) -> p k n", k=k)))

            def load_rows(name, w):
                wv = w.rearrange("(k p) n -> p k n", p=P)
                each_unit(sp, name, lambda u, j, _: load(
                    u, wv[:, bass.ds(2 * j, 2), :], raw[:, u.first % 4, :].rearrange("p (k n) -> p k n", k=2)), start=0)

            def load_ffn(name, gate_w, up_w, down_w):
                gv, uv = (w.rearrange("(k p) n -> p k n", p=P) for w in (gate_w, up_w))

                def one(u, j, k):
                    half = (j - (k % 2)) * 128 if isinstance(j, int) else (u.turn * 512 + (k // 2) * 256)
                    load(u, (gv if k % 2 == 0 else uv)[:, :, bass.ds(half, 256)],
                         raw[:, u.first % 4, :].rearrange("p (k n) -> p k n", k=DC))
                each_unit(sp, name + "up", one)
                load_rows(name + "down", down_w)

            load_cols("mem_k", t["w_k"][0], 0)
            load_cols("mem_v", t["w_v"][0], 0)
            w_in = t["w_in"][0]
            load_cols("xa", w_in, 0)
            sp.wait_ge(h_ready, 1)
            sp.dma_start(gate[:, :, :].rearrange("p a t -> p (a t)").rearrange("p (a n) -> p a n", a=2),
                         t["x"][0].rearrange("(a p) n -> p a n", p=P)).then_inc(tokens_in, 16)
            for a in range(ADA_UNITS):
                v = BEFORE_ADA + a
                if a < 4:
                    sp.wait_ge(rest_ready, v - 3)
                else:
                    sp.wait_ge(ada_done, a - 3)
                l, g, k = a // 24, a // 8 % 3, a % 8
                sp.dma_start(raw[:, v % 4, :], t["w_ada_2"][l, k * P:(k + 1) * P, g * UNIT:(g + 1) * UNIT]).then_inc(landed[v % 4], 16)

            load_cols("zv", w_in, HALF + D)
            load_cols("zu", w_in, HALF)
            load_cols("gate_a", w_in, HALF + 2 * D)
            load(Unit(FIRST["glu"]), t["s5_w_glu"][0].rearrange("(k p) n -> p k n", p=P),
                 raw[:, FIRST["glu"] % 4, :].rearrange("p (k n) -> p k n", k=HC))
            load_rows("proj_a", t["w_proj_a"][0])
            load_cols("gate_b", w_in, HALF + 3 * D)
            load_cols("proj_b", t["w_proj_b"][0], 0)
            load_cols("out", t["w_out"][0], 0)
            load_cols("mem_q", t["w_q"][0], 0)
            load_cols("mem_o", t["w_xo"][0], 0)
            load_ffn("ffn_", t["w_gate"][0], t["w_up"][0], t["w_down"][0])
            for p, l in (("c0", 0), ("x0", 0), ("c1", 1), ("x1", 1)):
                w = t["w_in_2"][l]
                if p != "c1":
                    load_cols(p + "conv_u", w, 512)
                    load_cols(p + "conv_g", w, 1024)
                    load_cols(p + "four", w, 0)
                    load_cols(p + "q", w, 1536)
                load_cols(p + "kv", w, 2048)
                if p != "c1":
                    load_cols(p + "dq", w, 2304)
                load_cols(p + "dk", w, 2816)
                load_cols(p + "dv", w, 3328)
                if p == "c1":
                    continue
                for b, wb in enumerate(("w_four_2", "w_conv_2", "w_gqa_2", "w_diff_2")):
                    load_cols(p + f"gate{b}", w, 3840 + b * D)
                    load_rows(p + f"proj{b}", t[wb][l])
                load_cols(p + "out", t["w_out_2"][l], 0)
                load_ffn(p + "ffn_", t["w_ffn1_2"][l], t["w_ffn3_2"][l], t["w_ffn2_2"][l])

        PASSES = (("c0", 0, 1), ("x0", 0, 0), ("c1", 1, 1), ("x1", 1, 0))
        NORM_H = [1, 2, 3, 4, 5, 6, 8, 7, 10, 9, 11, 12, 13]
        NORM_OF = {"c0": 4, "x0": 7, "c1": 9, "x1": 10}
        FFN_NORM = {"": 3, "c0": 6, "x0": 8, "x1": 11}
        BEFORE_NORM = {2: "out", 3: "mem_o", 5: "ffn_down", 6: "c0out", 8: "x0out", 10: "x0ffn_down", 11: "x1out",
                       12: "x1ffn_down"}
        NEXT_NORM = {"": 4, "c0": 7, "x0": 9}
        FULL_OF = {"c0": 0, "x0": 1, "x1": 2}
        ROPE_OF = {"x0": 0, "x1": 1}
        HID_OF = {"": 0, "c0": 1, "x0": 2, "x1": 3}
        DVE_CHUNKS = 2
        CONV_STEPS = HC + DVE_CHUNKS * (TAPS - 1)
        SCALED = [DC * k for k in range(13)]
        NREADY = {k: DC * i for i, k in enumerate((0, 1, 2, 3, 4, 6, 7, 8, 9, 10, 11))}
        NHIGH, NHIGH_EVENTS = {}, {}
        count = 0
        for x in (0, 1, "yb", "merged", 2, "o_mem", 3, 4, "c0", 6, 7, "x0", 8, 9, 10, "x1", 11):
            if isinstance(x, int):
                NHIGH[x] = count
                count += DC
            else:
                NHIGH_EVENTS[x] = count
                count += 4
        y1 = work[:, 5504:7552].rearrange("p (c a k) -> p c a k", c=HC, a=2)

        def after(name, b):
            n = COUNT[name]
            if row_kind(name):
                return BANK_USES[name][b] + 1
            if name == "glu":
                return BANK_USES[name][b] + (b < 2)
            return BANK_USES[name][b] + (n - b + 3) // 4

        def evacuated(eng, name):
            for b in range(4):
                eng.wait_ge(bank_free[b], after(name, b))

        def multiplied(eng, name):
            eng.wait_ge(unit_done, FIRST[name] + COUNT[name])

        BESIDE = {"gqa": ("gate2", 3), "diff": ("gate3", 2)}

        def beside_of(key):
            if key == "mem":
                return None, 0
            name, n = BESIDE[key[2:]]
            return key[:2] + name, n

        TASKS = {}

        def _tasks():
            g = group = head = 0
            for key, heads, maps in [("mem", MEM_HEADS, 1)] + [(p + k, h, n) for p in ("c0", "x0", "x1")
                                                              for k, h, n in (("gqa", 8, 1), ("diff", DIFF_HEADS, 2))]:
                tasks = []
                for h in range(heads):
                    for qt in range(2):
                        for mp in range(maps):
                            tasks.append(dict(g=g, group=group, head=head, h=h, qt=qt, map=mp,
                                              whole=mp == maps - 1, end=mp == maps - 1 and qt == 1))
                            g += 1
                        group += 1
                    head += 1
                TASKS[key] = tasks
        _tasks()
        NHEADS = {k: v[-1]["head"] + 1 for k, v in TASKS.items()}
        END_OF = {}
        for key_, v_ in TASKS.items():
            for i_, x_ in enumerate(v_):
                if x_["end"]:
                    END_OF[key_, i_] = x_

        def keys_of(key):
            return (0, T) if key == "mem" else (T, T) if key[0] == "c" else (0, 2 * T)

        def operand(key, what, h):
            k0, nk = keys_of(key)
            kc = slice(k0 // P, (k0 + nk) // P)
            if key == "mem":
                return {"k": mem_kT[:, 2 * h:2 * h + 2, :], "q": zu[:, 2 * h:2 * h + 2, :],
                        "v": mem_v[:, :, 2 * h * P:2 * (h + 1) * P]}[what]
            if kind_of(key) == "gqa":
                return {"k": kdup[:, h // 4, k0:k0 + nk], "q": qk[:, h // 2, :],
                        "v": vrow[:, kc, h // 4 * HEAD:(h // 4 + 1) * HEAD]}[what]
            return {"k": kdT[:, h, k0:k0 + nk], "q": dq[:, h, :], "v": vdrow[:, kc, h * P:(h + 1) * P]}[what]

        def shaped(buf, like):
            if len(like.shape) == 2:
                return buf[:, 0:like.shape[1]]
            return buf[:, 0:like.shape[1] * like.shape[2]].rearrange("p (a n) -> p a n", a=like.shape[1])

        Q_AT = {"mem": (0, 512), "gqa": (3200, 256), "diff": (4480, 256)}

        def split_of(key, what, h):
            kind, like = kind_of(key), operand(key, what, h)
            n, w, at = h // SHARE[kind][what], WORDS[kind][what], STORE[kind][what]
            slot = n % BUFFERS[kind][what]
            if what == "q":
                q0, qw = Q_AT[kind]
                return shaped(work_r[:, at + slot * w:at + (slot + 1) * w], like), shaped(work_r[:, q0 + n * qw:q0 + (n + 1) * qw], like)
            return [shaped(work_r[:, at + (2 * slot + i) * w:at + (2 * slot + i + 1) * w], like) for i in range(2)]

        SPLITS, NEED = {}, {}

        def _splits():
            done = 0
            for key, tasks in TASKS.items():
                firsts = {x["h"]: i for i, x in reversed(list(enumerate(tasks)))}
                kind = kind_of(key)
                for at in range(-1, len(tasks)):
                    events = []
                    for what in "kqv":
                        share, held = SHARE[kind][what], BUFFERS[kind][what]
                        for h in range(0, len(firsts), share):
                            free = h - (held - 1) * share
                            when = firsts[free] + (1 if what == "v" else -2) if free > 0 else -1
                            if when == at:
                                done += 1
                                events.append((what, h, tasks[firsts[max(free, 0)]], done))
                                for i in range(share):
                                    NEED[key, what, h + i] = done
                    SPLITS[key, at] = events
        _splits()

        def s5_tile(b):
            return 4 * (b % 4) + (16 if b < 4 else 0)

        @block.gpsimd
        def _(pool):
            n = [0]

            def link(ins):
                n[0] += 1
                ins.then_inc(pool_step, 1)
                pool.wait_ge(pool_step, n[0])

            def s5rows(name):
                return t[name].rearrange("o d (n g) p -> (o d n) (g p)", g=2)
            nc.gpsimd.memset(ones[:, :], 1.0).then_inc(flats_set, 1)
            nc.gpsimd.memset(one_row[:, :], 1.0).then_inc(flats_set, 1)
            nc.gpsimd.memset(flat[:, 0:1], 0.0).then_inc(flats_set, 1)
            nc.gpsimd.memset(flat[:, 1:2], 1.0).then_inc(flats_set, 1)
            pool.dma_start(rows[:, 0, :], s5rows("s5_lam_re")).then_inc(s5_in, 16)
            pool.dma_start(rows[:, 1, :], s5rows("s5_lam_im")).then_inc(s5_in, 16)
            pool.dma_start(rows[:, 2, 0:2], t["s5_log_step"].rearrange("o d (n g) -> (o d n) g", g=2)).then_inc(s5_in, 16)
            for i, (b, c) in enumerate((("s5_b_re", "s5_c_re"), ("s5_b_im", "s5_c_im"))):
                pool.dma_start(braw[:, i, :, :], t[b].rearrange("o d (n g) p c -> (g p) (o d n) c", g=2)).then_inc(s5_in, 16)
                pool.dma_start(craw[:, i, :, :], t[c].rearrange("o d (n g) c p -> (g c) (o d n) p", g=8)).then_inc(s5_in, 16)
            pool.wait_ge(s5_coef, 1)
            link(nc.gpsimd.tensor_copy(pw[:, 0, :], s5c[:, 1, :]))
            link(nc.gpsimd.tensor_copy(pw[:, 1, :], s5c[:, 2, :]))
            scr = s5w[:, 4096:5120]
            for tc_, ts_ in ((lo_c, lo_s), (hi_c, hi_s)):
                link(nc.gpsimd.memset(tc_[:, :, 0:1], 1.0))
                link(nc.gpsimd.memset(ts_[:, :, 0:1], 0.0))
                for k in range(4):
                    w = 1 << k
                    pc = pw[:, 0, :].unsqueeze(2).to_broadcast((P, TILES, w))
                    ps = pw[:, 1, :].unsqueeze(2).to_broadcast((P, TILES, w))
                    s1 = scr[:, 0:TILES * w].rearrange("p (n k) -> p n k", n=TILES)
                    s2 = scr[:, 512:512 + TILES * w].rearrange("p (n k) -> p n k", n=TILES)
                    link(nc.gpsimd.tensor_tensor(s1, tc_[:, :, 0:w], pc, ALU.mult))
                    link(nc.gpsimd.tensor_tensor(s2, ts_[:, :, 0:w], ps, ALU.mult))
                    link(nc.gpsimd.tensor_tensor(tc_[:, :, w:2 * w], s1, s2, ALU.subtract))
                    link(nc.gpsimd.tensor_tensor(s1, tc_[:, :, 0:w], ps, ALU.mult))
                    link(nc.gpsimd.tensor_tensor(s2, ts_[:, :, 0:w], pc, ALU.mult))
                    link(nc.gpsimd.tensor_tensor(ts_[:, :, w:2 * w], s1, s2, ALU.add))
                    link(nc.gpsimd.tensor_tensor(pw[:, 2, :], pw[:, 0, :], pw[:, 1, :], ALU.add))
                    link(nc.gpsimd.tensor_tensor(pw[:, 3, :], pw[:, 0, :], pw[:, 1, :], ALU.subtract))
                    link(nc.gpsimd.tensor_tensor(pw[:, 4, :], pw[:, 0, :], pw[:, 1, :], ALU.mult))
                    link(nc.gpsimd.tensor_tensor(pw[:, 0, :], pw[:, 2, :], pw[:, 3, :], ALU.mult))
                    link(nc.gpsimd.tensor_tensor(pw[:, 1, :], pw[:, 4, :], pw[:, 4, :], ALU.add))
            pool.wait_ge(s5_blk, 8)

            def make_table(b):
                if b >= 2:
                    pool.wait_ge(s5_w, 4 * (b - 1))
                tile = s5_tile(b)
                hc_, hs_, lc_, ls_ = (x[:, tile:tile + 4, :] for x in (hi_c, hi_s, lo_c, lo_s))

                def up(x):
                    return x.unsqueeze(3).to_broadcast((P, 4, 16, 16))

                def low(x):
                    return x.unsqueeze(2).to_broadcast((P, 4, 16, 16))
                c4, s4 = (x[b % 2].rearrange("p r (a t) -> p r a t", a=16) for x in (tab_c, tab_s))
                one = dup[:, :, :].rearrange("p a (b t) -> p (a b) t", t=16)
                link(nc.gpsimd.tensor_tensor(c4, up(hc_), low(lc_), ALU.mult))
                link(nc.gpsimd.tensor_tensor(s4, up(hs_), low(ls_), ALU.mult))
                link(nc.gpsimd.tensor_tensor(c4, c4, s4, ALU.subtract))
                link(nc.gpsimd.tensor_tensor(s4, up(hs_), low(lc_), ALU.mult))
                for r in range(4):
                    link(nc.gpsimd.tensor_tensor(one, hc_[:, r, :].unsqueeze(2).to_broadcast((P, 16, 16)),
                                                 ls_[:, r, :].unsqueeze(1).to_broadcast((P, 16, 16)), ALU.mult))
                    link(nc.gpsimd.tensor_tensor(s4[:, r], s4[:, r], one, ALU.add))
                pool.sem_inc(s5_tab, 1)

            for b in range(8):
                make_table(b)

            def taps(nf, l):
                mine, tmp = HC - DVE_CHUNKS, rstd[:, :]
                base = nf * (TAPS - 1) * mine * 2 + 1
                pool.wait_ge(conv_step, CONV_STEPS * nf + HC)
                if nf == 0:
                    pool.sem_inc(conv_pool, 1)
                with pool.Fori(1, TAPS) as k:
                    for i in range(mine):
                        c, at = DVE_CHUNKS + i, base + (k - 1) * mine * 2 + 2 * i
                        pool.wait_ge(conv_pool, at)
                        nc.gpsimd.tensor_tensor(tmp, conv_in[:, c, bass.ds(k, T)],
                                                tapc[:, l, bass.ds(4 * k + c, 1)].to_broadcast((P, T)), ALU.mult).then_inc(conv_pool, 1)
                        pool.wait_ge(conv_pool, at + 1)
                        nc.gpsimd.tensor_tensor(acc[:, c, :], acc[:, c, :], tmp, ALU.add).then_inc(conv_pool, 1)

            for key in TASKS:
                if kind_of(key) == "gqa":
                    taps(FULL_OF[key[:2]], 0 if key[1] == "0" else 1)
                for at in range(-1, len(TASKS[key])):
                    for what, h, _, done in SPLITS[key, at]:
                        src = operand(key, what, h)
                        high, rest = split_of(key, what, h)
                        pool.wait_ge(op_high, done)
                        nc.gpsimd.tensor_tensor(rest, src, high.bitcast(F32), ALU.subtract).then_inc(op_rest, 1)

        @block.tensor
        def _(pe):
            mm = nc.tensor.matmul

            def begin(u, banks):
                pe.wait_ge(rest_ready, u.count(1))
                for b, n in banks:
                    if not isinstance(n, int) or n > 0:
                        pe.wait_ge(bank_free[b], n)

            def parts(u, shape):
                return [w[:, u.first % n, :].rearrange("p (k n) -> p k n", k=shape)
                        for w, n in ((w_high, RAW), (w_rest, REST))]

            def product(dst, wh, wr, xh, xr, first, last, skip=False, weights_move=False):
                ops = ((wh, xh), (wh, xr), (wr, xh)) if not weights_move else ((wh, xh), (wr, xh), (wh, xr))
                for i, (w, x) in enumerate(ops):
                    a, b = (x, w) if weights_move else (w, x)
                    ins = mm(dst, a, b, start=first and i == 0, stop=last and i == 2, skip_group_check=skip)
                return ins

            def first_unit(u, k, name, chunk):
                begin(u, [(k % 4, uses(name, k, u.turn))])
                wh, wr = parts(u, DC)
                for c in range(DC):
                    chunk(c)
                    for o in range(2):
                        ins = product(L[:, k % 4, o * T:(o + 1) * T], wh[:, c, o * P:(o + 1) * P], wr[:, c, o * P:(o + 1) * P],
                                      n_high[:, c, :], n_rest[:, c, :], c == 0 and o == 0, c == DC - 1, skip=True)
                ins.then_inc(unit_done, 1)

            def normed_chunk(k):
                return lambda c: pe.wait_ge(n_ready, NREADY[k] + c + 1)

            def split_chunk(event):
                return lambda c: pe.wait_ge(m_split, 4 * event + c // 2 + 1)

            def cols_unit(u, k, name, xh, xr, kc=DC):
                begin(u, [(k % 4, uses(name, k, u.turn))])
                wh, wr = parts(u, kc)
                for o in range(2):
                    for c in range(kc):
                        ins = product(L[:, k % 4, o * T:(o + 1) * T], wh[:, c, o * P:(o + 1) * P], wr[:, c, o * P:(o + 1) * P],
                                      xh[:, c, :], xr[:, c, :], c == 0, c == kc - 1)
                ins.then_inc(unit_done, 1)

            def quarter_unit(name, k, q):
                u = Unit(FIRST[name] + k)
                if q == 0:
                    begin(u, [(k, uses(name, k))])
                wh, wr = parts(u, DC)
                o, c0 = q // 2, q % 2 * 4
                for c in range(c0, c0 + 4):
                    ins = product(L[:, k, o * T:(o + 1) * T], wh[:, c, o * P:(o + 1) * P], wr[:, c, o * P:(o + 1) * P],
                                  n_high[:, c, :], n_rest[:, c, :], c == 0, c == DC - 1)
                if q == 3:
                    ins.then_inc(unit_done, 1)

            def cols_linear(name, before={}, chunk=None, start=0):
                def one(u, j, k):
                    if isinstance(j, int) and j in before:
                        before[j]()
                    if chunk is not None and u.first == FIRST[name]:
                        first_unit(u, k, name, chunk)
                    else:
                        cols_unit(u, k, name, n_high, n_rest)
                each_unit(pe, name, one, start)

            def rows_linear(name, before={}):
                def one(u, j, k):
                    if j in before:
                        before[j]()
                    begin(u, [(k % 4, uses(name, k, u.turn))])
                    wh, wr = parts(u, DC)
                    for a in range(2):
                        for c in range(DC):
                            ins = product(L[:, k % 4, a * T:(a + 1) * T], wh[:, c, :], wr[:, c, :],
                                          n_high[:, c, a * P:(a + 1) * P], n_rest[:, c, a * P:(a + 1) * P],
                                          c == 0, c == DC - 1, weights_move=True)
                    ins.then_inc(unit_done, 1)
                each_unit(pe, name, one)

            def acc_unit(u, xh, xr, at, first, last):
                wh, wr = parts(u, 2)
                for c in range(2):
                    for o in range(DC):
                        ins = product(L[:, o // 2, o % 2 * T:(o % 2 + 1) * T], wh[:, c, o * P:(o + 1) * P],
                                      wr[:, c, o * P:(o + 1) * P], xh[:, at + c, :] if isinstance(at, int) else xh[:, bass.ds(at + c, 1), :].rearrange("p a t -> p (a t)"),
                                      xr[:, at + c, :] if isinstance(at, int) else xr[:, bass.ds(at + c, 1), :].rearrange("p a t -> p (a t)"),
                                      first and c == 0 and o % 2 == 0, last and c == 1, skip=True)
                ins.then_inc(unit_done, 1)

            def acc_linear(name, xh, xr, before={}):
                first, n = FIRST[name], COUNT[name]
                if 0 in before:
                    before[0]()
                begin(Unit(first), [(b, BANK_USES[name][b]) for b in range(4)])
                acc_unit(Unit(first), xh, xr, 0, True, n == 1)

                turns = (n - 2) // 4
                if turns > 1:
                    with pe.Fori(0, turns) as i:
                        for k in range(1, 5):
                            u = Unit(first + k, i)
                            begin(u, [])
                            acc_unit(u, xh, xr, 8 * i + 2 * k, False, False)
                else:
                    turns = 0
                for k in range(1 + 4 * turns, n):
                    if k in before:
                        before[k]()
                    begin(Unit(first + k), [])
                    acc_unit(Unit(first + k), xh, xr, 2 * k, False, k == n - 1)

            def turn_tokens(k, rows_ap):
                pe.wait_ge(tokens_in, 16 * (k + 1))
                for b in range(4):
                    for c in range(2):
                        for a in range(2):
                            ins = nc.tensor.transpose(M[:, b, c * T + a * P:c * T + (a + 1) * P],
                                                      rows_ap[:, a, (2 * b + c) * P:(2 * b + c + 1) * P], ident[:, :])
                    ins.then_inc(turned, 1)

            rows2 = gate[:, :, :].rearrange("p a t -> p (a t)").rearrange("p (a n) -> p a n", a=2)

            def norm(k):
                for c in range(DC):
                    pe.wait_ge(sq_ready, 4 * k + c // 2 + 1)
                    ins = mm(M[:, 0, 0:T], ones[:, :], m[:, c, :], start=c == 0, stop=c == DC - 1)
                ins.then_inc(sum_ready, 1)

            def attention(key, before, parts_of, values_of):
                tasks = TASKS[key]
                nk = keys_of(key)[1]
                exps, (th, tr) = store_of(key)
                beside, n_beside = beside_of(key)

                def score(x):
                    if x["g"] >= 2:
                        pe.wait_ge(expd, x["g"] - 1)
                    pe.wait_ge(op_rest, max(NEED[key, "k", x["h"]], NEED[key, "q", x["h"]]))
                    pairs = parts_of(x["h"], x["map"], x["qt"])
                    (kh, kr), (qh, qr) = (split_of(key, what, x["h"]) for what in "kq")
                    for i, (q, kk) in enumerate(pairs):
                        ins = product(score_bank[x["g"] % 2][:, 0:nk], qh[q], qr[q], kh[kk], kr[kk], i == 0, i == len(pairs) - 1)
                    ins.then_inc(scores, 1)

                def turn(i, x):
                    pe.wait_ge(probs, x["group"] + 1)
                    if x["group"] >= 2:
                        pe.wait_ge(probs_T_rest, x["group"] - 1)
                    if i < 4:
                        pe.wait_ge(bank_free[3], after(before, 3))
                    for c in range(nk // P):
                        ins = nc.tensor.transpose(turned_bank[x["group"] % 2][:, c * P:(c + 1) * P],
                                                  exps[(i - x["map"]) % 3][:, c * P:(c + 1) * P], ident[:, :])
                    ins.then_inc(probs_T, 1)

                def values(x):
                    pe.wait_ge(probs_T_rest, x["group"] + 1)
                    pe.wait_ge(op_rest, NEED[key, "v", x["h"]])
                    if x["head"]:
                        pe.wait_ge(o_ready, x["head"])
                    vh, vr = split_of(key, "v", x["h"])
                    for dst, sl in values_of(x["h"], head_bank):
                        for c in range(nk // P):
                            ins = product(dst, vh[:, c, sl], vr[:, c, sl], th[:, c, :], tr[:, c, :], c == 0, c == nk // P - 1)
                    ins.then_inc(attended, 1)
                score(tasks[0])
                score(tasks[1])
                for i, x in enumerate(tasks):
                    if x["whole"]:
                        turn(i, x)
                    if i + 2 < len(tasks):
                        score(tasks[i + 2])
                    if (key, i - 1) in END_OF:
                        values(tasks[i - 1])
                    if i // 4 < n_beside:
                        quarter_unit(beside, i // 4, i % 4)
                values(tasks[-1])

            pe.wait_ge(consts_in, 16 * 5)
            pe.wait_ge(params_in, 16 * (len(COLS) + 1 + 4 + 2 * LAYERS))
            flat_m = m[:, :, :].rearrange("p a t -> p (a t)")
            nc.tensor.transpose(M[:, 0, 0:NVEC], flat_m[0:NVEC, 0:P], ident[0:NVEC, 0:NVEC])
            nc.tensor.transpose(M[:, 0, P:P + 6], flat_m[0:6, P:2 * P], ident[0:6, 0:6])
            for l in range(LAYERS):
                nc.tensor.transpose(M[:, 1, l * P:l * P + TAPS * HC], flat_m[0:TAPS * HC, (2 + l) * P:(3 + l) * P],
                                    ident[0:TAPS * HC, 0:TAPS * HC])
                ins = nc.tensor.transpose(M[:, 1, 256 + l * 48:256 + (l + 1) * 48], flat_m[0:48, 1024 + l * P:1024 + (l + 1) * P],
                                          ident[0:48, 0:48])
            ins.then_inc(turned, 1)
            pe.wait_ge(turned_out, 4)
            turn_tokens(0, rows2)
            norm(0)

            def coefficients_back():
                for i in range(5):
                    ins = nc.tensor.transpose(M[:, 0, i * TILES:(i + 1) * TILES], rows[:, 11 + i, :], ident[0:TILES, 0:TILES])
                ins.then_inc(s5_bt, 1)

            def turn_blocks(q0):
                pe.wait_ge(s5_blk, 8)
                for q in range(q0, q0 + 4):
                    if q >= 4:
                        pe.wait_ge(turned_out, 4 + q - 4 + 1)
                    else:
                        pe.wait_ge(s5_coef, 1)
                    for k in range(4):
                        i, nblk = (4 * q + k) % 16 // 8, (4 * q + k) % 8
                        if q < 4:
                            src = bblk[:, i, 4 * nblk:4 * nblk + 4, :, :].rearrange("p n g c -> p (n g c)")
                        else:
                            src = cblk[:, i, nblk, :, :].rearrange("p g k -> p (g k)")
                        ins = nc.tensor.transpose(M[:, q % 4, k * P:(k + 1) * P], src, ident[:, :])
                    ins.then_inc(turned, 1)

            pe.wait_ge(s5_coef_rows, 1)
            pe.wait_ge(ms_ready, 1)
            coefficients_back()
            cols_linear("mem_k", chunk=normed_chunk(0))
            rows_linear("mem_v", before={1: lambda: turn_blocks(0), 3: lambda: turn_blocks(4)})
            pe.wait_ge(turned_out, 4 + 8)
            turn_tokens(1, rows2)
            norm(1)
            cols_linear("xa", chunk=normed_chunk(1))

            def modulation(half):
                grp = half // 2
                if half == 0:
                    pe.wait_ge(silu_ready, 1)
                    pe.wait_ge(bank_free[0], after("xa", 0))
                    pe.wait_ge(bank_free[1], after("xa", 1))
                if half % 2 == 0 and grp >= 2:
                    pe.wait_ge(ada_row, grp - 1)
                for a in range(4 * half, 4 * half + 4):
                    v, kc = BEFORE_ADA + a, a % 8
                    pe.wait_ge(landed[v % 4], 16 * (v // 4 + 1))
                    for q in range(4):
                        ins = mm(L[32 * q:32 * q + 2, grp % 2, :], silu_c[:, kc, :], raw[:, v % 4, q * 512:(q + 1) * 512],
                                 start=kc == 0, stop=kc == 7, skip_group_check=True)
                    ins.then_inc(ada_done, 1)

            def s5_in_product(b):
                d, c = (1 if b < 4 else 0), b % 4
                pe.wait_ge(xa_ready, 1)
                if b == 0:
                    pe.wait_ge(turned_out, 4 + 8)
                else:
                    pe.wait_ge(s5_rot, 4 * b)
                for r in range(4):
                    x = (xaR if d else xaT)[32 * r:32 * r + 32, c, :]
                    for i in range(2):
                        ins = mm(M[:, r, i * T:(i + 1) * T], BT[32 * r:32 * r + 32, i, 4 * d + c, :], x, start=True, stop=True)
                ins.then_inc(s5_bu, 1)

            def s5_out_product(b):
                d, c = (1 if b < 4 else 0), b % 4
                pe.wait_ge(s5_w, 4 * (b + 1))
                if b == 0:
                    evacuated(pe, "xa")
                if b >= 2:
                    pe.wait_ge(s5_yout, b - 1)
                for r in range(4):
                    for k, (i, z) in enumerate(zip((0, 0, 1, 1), zset[b % 2])):
                        ins = mm(L[32 * r:32 * r + 32, 2 + b % 2, 0:T], CT[:, i, 4 * d + c, 32 * r:32 * r + 32], z[:, r, :],
                                 start=k == 0, stop=k == 3, skip_group_check=True)
                ins.then_inc(s5_y, 1)

            s5_in_product(0)
            half = 0
            for b, upto in enumerate((2, 3, 5, 7, 8, 10, 12, 12)):
                if b < 7:
                    s5_in_product(b + 1)
                while half < upto:
                    modulation(half)
                    half += 1
                s5_out_product(b)
            pe.wait_ge(ada_rows_in, 16 * 8 * ADA_GROUPS)
            for l in range(LAYERS):
                ins = nc.tensor.transpose(M[:, 0, l * P:l * P + 96], ada_rows[:, l, :], ident[0:96, 0:96])
            ins.then_inc(turned, 1)

            pe.wait_ge(s5_yout, 8)
            pe.wait_ge(ada_row, ADA_GROUPS)
            rows_linear("zv")
            cols_linear("zu")
            pe.wait_ge(sgu_in, 16 * 4)
            pe.wait_ge(mod_ready, 1)
            for h in range(SGU_HEADS):
                ins = nc.tensor.transpose(M[:, 2 + h // 4, h % 4 * P:(h % 4 + 1) * P], sgu_raw[:, h, :], ident[:, :])
            ins.then_inc(turned, 1)
            pe.wait_ge(ln_ready, 2)
            pe.wait_ge(turned_out, 4 + 8 + 1)
            for h in range(SGU_HEADS):
                for a in range(2):
                    dst = M[:, h // 2, h % 2 * T + a * P:h % 2 * T + (a + 1) * P]
                    mm(dst, zv[:, a, h * P:(h + 1) * P], sgu_wt[:, h, :], start=True, stop=False)
                    ins = mm(dst, one_row[0:1, :], sgu_b[0:1, h * P:(h + 1) * P], start=False, stop=True)
            ins.then_inc(sgu_mm, 1)
            cols_linear("gate_a")

            name = "glu"
            pe.wait_ge(branch_ready, 1)
            u = Unit(FIRST[name])
            begin(u, [(0, BANK_USES[name][0]), (1, BANK_USES[name][1])])
            wh, wr = parts(u, HC)
            for o in range(HC):
                for c in range(HC):
                    ins = product(L[:, o // 2, o % 2 * T:(o % 2 + 1) * T], wh[:, c, o * P:(o + 1) * P], wr[:, c, o * P:(o + 1) * P],
                                  b_high[:, c, :], b_rest[:, c, :], c == 0, c == HC - 1)
            ins.then_inc(unit_done, 1)
            pe.wait_ge(branch_ready, 2)
            acc_linear("proj_a", b_high, b_rest)
            cols_linear("gate_b")
            cols_linear("proj_b", chunk=split_chunk(0))
            cols_linear("out", chunk=split_chunk(1))
            norm(2)
            cols_linear("mem_q", chunk=normed_chunk(2))
            evacuated(pe, "mem_q")

            attention("mem", "mem_q",
                      lambda h, mp, qt: [((slice(None), c, slice(qt * P, (qt + 1) * P)), (slice(None), c)) for c in range(2)],
                      lambda h, bank: [(bank[:, d * T:(d + 1) * T], slice(d * P, (d + 1) * P)) for d in range(2)])
            cols_linear("mem_o", chunk=split_chunk(2))

            rows_m = m[:, :, :].rearrange("p a t -> p (a t)").rearrange("p (a n) -> p a n", a=2)

            def feed_forward(pre):
                k, next_ = FFN_NORM[pre], NEXT_NORM.get(pre)
                norm(k)
                cols_linear(pre + "ffn_up", chunk=normed_chunk(k))
                if pre == "":
                    turn_tokens(2, rows_m)
                pe.wait_ge(hid_ready, FC // 2 * (HID_OF[pre] + 1))
                acc_linear(pre + "ffn_down", hid_high, hid_rest, before={9: lambda: norm(next_)} if next_ else {})

            feed_forward("")
            for num, (p, l, s) in enumerate(PASSES):
                own = 0 if s == 0 else 2
                full = p != "c1"
                nf = FULL_OF.get(p)
                rx = ROPE_OF.get(p)
                first_chunk = normed_chunk(NORM_OF[p])

                def fourier_heads():
                    evacuated(pe, p + "four")
                    pe.wait_ge(ms_ready, NORM_OF[p] + (2 if p == "c0" else 1))
                    if nf:
                        pe.wait_ge(kd_dupc, num)
                    for c in range(HC):
                        for a in range(2):
                            ins = mm(M[:, c, a * T:(a + 1) * T], oT[:, c, a * P:(a + 1) * P], dft64[:, :], start=True, stop=True)
                    ins.then_inc(four1, 1)

                def fourier_tokens():
                    pe.wait_ge(dft_in, 16 * (nf + 1))
                    pe.wait_ge(four1c, 4 * (nf + 1))
                    for c in range(HC):
                        for i, (a, k) in enumerate(((0, 0), (0, 1), (1, 0), (1, 1))):
                            ins = mm(M[:, c // 2, c % 2 * T:(c % 2 + 1) * T], y1[:, c, a, k * P:(k + 1) * P], dft256[:, k, a, :],
                                     start=i == 0, stop=i == 3)
                    ins.then_inc(four2, 1)

                def turn_v():
                    evacuated(pe, p + "kv")
                    for a in range(2):
                        ins = nc.tensor.transpose(M[:, 3, a * P:(a + 1) * P], oT[:, 0, a * P:(a + 1) * P], ident[:, :])
                    ins.then_inc(k_ready, 1)

                def square_sums():
                    if full:
                        pe.wait_ge(branch_ready, 2 + 4 * nf + 1)
                    pe.wait_ge(qk_sq, num + 1)
                    for c in (range(HC + 1) if full else (HC,)):
                        ins = mm(M[:, c // 2, c % 2 * T:(c % 2 + 1) * T], pair_ones[:, :], t2[:, c, :], start=True, stop=True)
                    ins.then_inc(qk_sum, 1)

                def swap_halves(src, n, bank):
                    for c in range(n):
                        ins = mm(M[:, bank + c // 2, c % 2 * T:(c % 2 + 1) * T], swap[:, :], src[:, c, :], start=True, stop=True)
                    ins.then_inc(qk_rot, 1)

                def double_k(num):
                    if num % 2:
                        pe.wait_ge(d_rot, 3 * (num // 2) + 1)
                    pe.wait_ge(qk_n, num + 1)
                    pe.wait_ge(consts_in, 16 * 7)
                    for h in range(2):
                        ins = mm(M[:, 2, h * T:(h + 1) * T], dup[:, h, :], qk[:, HC, :], start=True, stop=True)
                    ins.then_inc(kd_dup, 1)

                def swap_qk():
                    pe.wait_ge(qk_n, num + 1)
                    swap_halves(qk, HC + 1, 0)

                def swap_dq():
                    evacuated(pe, p + "dq")
                    pe.wait_ge(d_rot, 3 * rx + 1)
                    swap_halves(dq, HC, 0)

                def swap_dk():
                    evacuated(pe, p + "dk")
                    pe.wait_ge(kd_dupc, num + 1)
                    swap_halves(t1, HC, 2)

                if full:
                    cols_linear(p + "conv_u", chunk=first_chunk)
                    if p == "c0":
                        norm(5)
                    if p == "x1":
                        double_k(num - 1)
                    cols_linear(p + "conv_g")
                    cols_linear(p + "four")
                    cols_linear(p + "q")
                    fourier_heads()
                    cols_linear(p + "kv")
                    fourier_tokens()
                    cols_linear(p + "dq", before={1: turn_v})
                    cols_linear(p + "dk", before={1: square_sums})
                    rows_linear(p + "dv")
                else:
                    cols_linear(p + "kv", chunk=first_chunk)
                    cols_linear(p + "dk", before={0: lambda: norm(10), 1: turn_v})
                    rows_linear(p + "dv", before={1: square_sums})
                    continue

                def conv_sums(k, src, at):
                    pe.wait_ge(conv_st, 2 * nf + k)
                    for c in range(HC):
                        ins = mm(M[:, 3, at:at + T], ones[:, :], src[:, c, :], start=c == 0, stop=c == HC - 1)
                    ins.then_inc(conv_stc, 1)

                def sum_acc():
                    pe.wait_ge(conv_pool, (nf + 1) * (TAPS - 1) * (HC - DVE_CHUNKS) * 2 + 1)
                    pe.wait_ge(v_ready, num + 1)
                    conv_sums(1, acc, 0)

                def branch(i, gate_before={}, proj_before={}, start=0):
                    cols_linear(p + f"gate{i}", before=gate_before, start=start)
                    pe.wait_ge(branch_ready, 2 + 4 * nf + i + 1)
                    acc_linear(p + f"proj{i}", b_high, b_rest, before=proj_before)

                branch(0, proj_before={0: sum_acc, 1: lambda: conv_sums(2, t2, T)})
                if rx is not None:
                    branch(1, gate_before={0: swap_qk, 3: lambda: (double_k(num), swap_dq())}, proj_before={1: swap_dk})
                    pe.wait_ge(d_rot, 3 * rx + 3)
                else:
                    branch(1, gate_before={3: lambda: double_k(num)})
                pe.wait_ge(kd_dupc, num + 1)

                def head_parts(a, qt):
                    return [((slice(a, a + HEAD), slice(qt * P, (qt + 1) * P)), (slice(a, a + HEAD), slice(None)))]
                attention(p + "gqa", p + "proj1", lambda h, mp, qt: head_parts(HEAD * (h % 2), qt),
                          lambda h, bank: [(bank[0:HEAD, 0:T], slice(0, HEAD))])
                branch(2, start=BESIDE["gqa"][1])
                attention(p + "diff", p + "proj2", lambda h, mp, qt: head_parts(HEAD * mp, qt),
                          lambda h, bank: [(bank[:, 0:T], slice(0, P))])
                pe.wait_ge(on_sq, nf + 1)
                for c in range(HC):
                    ins = mm(M[:, c // 2, c % 2 * T:(c % 2 + 1) * T], ones[:, :], t1[:, c, :], start=True, stop=True)
                ins.then_inc(on_sum, 1)
                branch(3, start=BESIDE["diff"][1])
                cols_linear(p + "out", chunk=split_chunk(3 + nf))
                feed_forward(p)
            norm(12)
            for b in range(4):
                half, a = b // 2, b % 2
                pe.wait_ge(scaled, SCALED[12] + 4 * half + 4)
                pe.wait_ge(ms_ready, 13)
                for c in range(4):
                    ins = nc.tensor.transpose(M[:, b, c * P:(c + 1) * P], m[:, 4 * half + c, a * P:(a + 1) * P], ident[:, :])
                ins.then_inc(turned, 1)

        @block.scalar
        def _(act):
            A = nc.scalar.activation
            rows2 = gate[:, :, :].rearrange("p a t -> p (a t)").rearrange("p (a n) -> p a n", a=2)

            def start_units(first):
                for k in range(3):
                    split_high(act, Unit(first + k))

            def linear(name, one, beside={}, start=0):
                def step(u, j, k):
                    ahead_high(act, u, last_of(name))
                    if one is not None:
                        act.wait_ge(unit_done, u.count(1))
                        ins = one(j, k, u)
                        if ins is not None:
                            ins.then_inc(bank_free[k % 4], 1)
                    if isinstance(j, int) and j in beside:
                        beside[j]()
                each_unit(act, name, step, start)

            def out_to(name, dst, func=ACT.Copy, scale=1.0, beside={}, start=0):
                linear(name, lambda j, k, u: A(dst[:, 2 * j:2 * j + 2, :].rearrange("p a t -> p (a t)"), L[:, k % 4, :], func,
                                               scale=scale), beside, start)

            def rows_to(name, dst, func=ACT.Copy, beside={}):
                linear(name, lambda j, k, u: A(dst[:, :, j * T:(j + 1) * T], L[:, k % 4, :].rearrange("p (a n) -> p a n", a=2), func),
                       beside)

            def squares_of(k, h):
                if k not in BEFORE_NORM:
                    act.wait_ge(h_ready, NORM_H[k])
                for b in range(4):
                    if k in BEFORE_NORM:
                        act.wait_ge(bank_free[b], after(BEFORE_NORM[k], b))
                    A(m[:, 2 * b:2 * b + 2, :], h[:, 2 * b:2 * b + 2, :], ACT.Square).then_inc(sq_ready, 1)

            def root_of(k):
                act.wait_ge(ms_ready, k + 1)
                A(rstd[:, :], rstd[:, :], ACT.Sqrt).then_inc(root_ready, 1)

            def highs_of(k, shift):
                if k >= 4:
                    act.wait_ge(mod_ready, 1)
                for c in range(DC):
                    act.wait_ge(scaled, SCALED[k] + c + 1)
                    A(n_high[:, c, :], m[:, c, :], ACT.Identity, bias=shift(c)).then_inc(n_high_ready, 1)

            def norm(k, h, shift, split=True):
                squares_of(k, h)
                root_of(k)
                if split:
                    highs_of(k, shift)

            def split_high_of(src, sem_, base):
                for b in range(4):
                    act.wait_ge(sem_, base + b + 1)
                    A(n_high[:, 2 * b:2 * b + 2, :], src[:, 2 * b:2 * b + 2, :], ACT.Copy).then_inc(n_high_ready, 1)

            def attention(key, gate_free=0):
                nk = keys_of(key)[1]
                exps, (th, tr) = store_of(key)
                tasks = TASKS[key]

                def split(at):
                    for what, h, x, _ in SPLITS[key, at]:
                        if what != "v" and x["g"]:
                            act.wait_ge(scores, x["g"])
                        if what == "v" and x["head"]:
                            act.wait_ge(attended, x["head"])
                        src = operand(key, what, h)
                        A(split_of(key, what, h)[0], src, ACT.Copy).then_inc(op_high, 1)

                def exponentials(i, x):
                    act.wait_ge(neg_max, x["g"] + 1)
                    if i >= 3:
                        act.wait_ge(probs_T, tasks[i - 3]["group"] + 1)
                    A(exps[i % 3][:, 0:nk], score_bank[x["g"] % 2][:, 0:nk], ACT.Exp, bias=soft[:, x["g"] % 4, 0:1],
                      accum_out=soft[:, x["g"] % 4, 2:3]).then_inc(expd, 1)

                def turned_high(x):
                    act.wait_ge(probs_T, x["group"] + 1)
                    if x["qt"] == 0 and x["head"]:
                        act.wait_ge(attended, x["head"])
                    A(th[:, 0:nk // P, x["qt"] * P:(x["qt"] + 1) * P],
                      turned_bank[x["group"] % 2][:, 0:nk].rearrange("p (c q) -> p c q", q=P), ACT.Copy).then_inc(probs_T_high, 1)
                beside, n_beside = beside_of(key)

                def out_beside(k):
                    act.wait_ge(merged, gate_free)
                    act.wait_ge(unit_done, FIRST[beside] + k + 1)
                    A(gate[:, 2 * k:2 * k + 2, :].rearrange("p a t -> p (a t)"), L[:, k, :], ACT.Copy).then_inc(bank_free[k], 1)
                split(-1)
                exponentials(0, tasks[0])
                for i, x in enumerate(tasks):
                    split(i)
                    if i + 1 < len(tasks):
                        exponentials(i + 1, tasks[i + 1])
                    if i and tasks[i - 1]["whole"]:
                        turned_high(tasks[i - 1])
                    if i % 4 == 1:
                        if i // 4 < n_beside:
                            ahead_high(act, Unit(FIRST[beside] + i // 4), UNITS)
                        if 0 < i // 4 <= n_beside:
                            out_beside(i // 4 - 1)
                turned_high(tasks[-1])

            act.wait_ge(flats_set, 4)
            act.wait_ge(turned_out, 4)
            for i, name in enumerate(("c_2", "c_ctx_2")):
                ins = A(silu_c[:, :, i], col(name, 0, DC), ACT.Silu)
            ins.then_inc(silu_ready, 1)
            act.wait_ge(lam_dot, 2 * LAYERS)
            for l in range(LAYERS):
                ins = A(lam[:, l, 2:4], lam[:, l, 0:2], ACT.Exp)
            ins.then_inc(lam_exp, 1)
            act.wait_ge(s5_in, 16 * 7)
            A(rows[:, 2, 0:2], rows[:, 2, 0:2], ACT.Exp).then_inc(s5_act, 1)
            act.wait_ge(s5_act_in, 1)
            A(rows[:, 8, :], rows[:, 7, :], ACT.Sin).then_inc(s5_act, 1)
            A(rows[:, 9, :], rows[:, 7, :], ACT.Sin, scale=0.5).then_inc(s5_act, 1)
            A(rows[:, 10, :], rows[:, 3, :], ACT.Tanh, scale=0.5).then_inc(s5_act, 1)
            start_units(0)
            norm(0, hc, lambda c: flat[:, 0:1])
            out_to("mem_k", mem_kT)
            flatB = s5w[:, 6144:10240].rearrange("p (q k) -> p q k", q=8)

            def turned_blocks(q0):
                for q in range(q0, q0 + 4):
                    act.wait_ge(turned, 1 + 4 + q + 1)
                    A(flatB[:, q, :], M[:, q % 4, :], ACT.Copy).then_inc(turned_out, 1)
            rows_to("mem_v", mem_v, beside={1: lambda: turned_blocks(0), 3: lambda: turned_blocks(4)})
            norm(1, hx, lambda c: flat[:, 0:1])
            out_to("xa", xaT)
            def ada_out(grp):
                l, g = grp // 3, grp % 3
                act.wait_ge(ada_done, 8 * (grp + 1))
                if grp:
                    act.wait_ge(ada_rows_in, 16 * 8 * grp)
                flat_rope = rope[:, :, :].rearrange("p a t -> p (a t)")
                for q in range(4):
                    ins = A(flat_rope[32 * q:32 * q + 2, :], L[32 * q:32 * q + 2, grp % 2, :], ACT.Copy)
                    ins.then_inc(act_step, 1)
                act.wait_ge(act_step, 4 * (grp + 1))
                act.sem_inc(ada_row, 1)
                for q in range(4):
                    for s in range(2):
                        at = s * 48 + g * 16 + q * 4
                        act.dma_start(ada_rows[at:at + 4, l, :], flat_rope[32 * q + s:32 * q + s + 1, :]).then_inc(ada_rows_in, 16)
            for grp in range(ADA_GROUPS):
                ada_out(grp)
            act.wait_ge(ada_rows_in, 16 * 8 * ADA_GROUPS)
            act.dma_start(rope[:, :, :], consts["rope"].rearrange("p (a t) -> p a t", a=2)).then_inc(consts_in, 16)
            act.wait_ge(s5_tab, 8)
            act.dma_start(dup[:, :, :], consts["dup"].rearrange("p (a k) -> p a k", a=2)).then_inc(consts_in, 16)
            start_units(BEFORE_ADA)
            act.wait_ge(s5_yout, 8)
            act.dma_start(sgu_raw, t["sgu_w"][0].rearrange("h t s -> t h s")).then_inc(sgu_in, 16)
            act.dma_start(sgu_b, t["sgu_bias"][0].rearrange("(o h) t -> o (h t)", o=1)).then_inc(sgu_in, 16)
            lnv = m[:, :, :].rearrange("p a t -> p (a t)").rearrange("p (a n) -> p a n", a=2)
            act.dma_start(lnv[:, 0, :], t["sgu_ln_g"].partition_broadcast(P)).then_inc(sgu_in, 16)
            act.dma_start(lnv[:, 1, :], t["sgu_ln_b"].partition_broadcast(P)).then_inc(sgu_in, 16)
            act.wait_ge(s5_yout, 8)
            A(yT, yT, ACT.Gelu_apprx_tanh).then_inc(gelu_y, 1)
            rows_to("zv", zv, ACT.Gelu_apprx_tanh)
            out_to("zu", zu, ACT.Gelu_apprx_tanh)
            act.wait_ge(turned, 1 + 4 * 2 + 8 + 1 + 1)
            A(sgu_wt.rearrange("p h t -> p (h t)"), M[:, 2:4, :].rearrange("p a n -> p (a n)"), ACT.Copy).then_inc(turned_out, 1)
            for a in range(2):
                act.wait_ge(ln_sum, a + 1)
                A(work[:, 5760:6784], zv[:, a, :], ACT.Square, accum_out=stats[:, a, 2:3]).then_inc(ln_sq, 1)
                act.wait_ge(ln_sq, a + 1)
            act.wait_ge(ln_sum, 3)
            A(stats[:, :, 4], stats[:, :, 3], ACT.Sqrt).then_inc(ln_root, 1)
            out_to("gate_a", gate, ACT.Sigmoid)
            act.wait_ge(gelu_y, 1)
            A(b_high[:, :, :], yT, ACT.Copy).then_inc(glu_sig, 1)

            def glu_out(j, k, u):
                for b in range(2):
                    A(work[:, 5760 + 512 * b:5760 + 512 * (b + 1)], L[:, b, :], ACT.Sigmoid).then_inc(bank_free[b], 1)
            linear("glu", glu_out)
            act.wait_ge(glu_sig, 2)
            A(b_high[:, :, :], yT, ACT.Copy).then_inc(glu_sig, 1)
            linear("proj_a", None)
            act.wait_ge(merged, 4)
            out_to("gate_b", gate, ACT.Sigmoid)
            multiplied(act, "gate_b")
            split_high_of(zu, sgu_out, 0)
            linear("proj_b", None)
            multiplied(act, "proj_b")
            split_high_of(m, merged, 4)
            linear("out", None)
            norm(2, hx, lambda c: flat[:, 0:1])
            out_to("mem_q", zu, scale=float(D // MEM_HEADS) ** -0.5)
            evacuated(act, "mem_q")
            attention("mem")
            multiplied(act, "mem_q")
            split_high_of(o_mem, o_ready, 0)
            linear("mem_o", None)

            def feed_forward(pre, h, shift):
                norm(FFN_NORM[pre], h, shift)
                if pre == "":
                    act.wait_ge(n_ready, NREADY[3] + DC)
                    act.dma_start(rows_m, t["ctx_2"][0].rearrange("(a p) n -> p a n", p=P)).then_inc(tokens_in, 16)
                base = FC // 2 * HID_OF[pre]

                def one(j, k2, u):
                    if k2 % 2:
                        return None
                    pair = u.turn * 2 + k2 // 2 if not isinstance(u.turn, int) else j // 2
                    buf = (k2 // 2) % 2
                    if isinstance(pair, int):
                        if pair >= 2:
                            act.wait_ge(hid_ready, base + pair - 1)
                    else:
                        act.wait_ge(hid_ready, base + pair - 1)
                    A(gate[:, 4 * buf:4 * buf + 2, :].rearrange("p a t -> p (a t)"), L[:, k2 % 4, :], ACT.Silu).then_inc(up_act, 1)
                    return None
                first, n = FIRST[pre + "ffn_up"], COUNT[pre + "ffn_up"]

                def step(u, j, k2):
                    ahead_high(act, u, UNITS)
                    if k2 % 2 == 0:
                        act.wait_ge(unit_done, u.count(1))
                        one(j, k2, u)
                for j in range(4):
                    step(Unit(first + j), j, j)
                with act.Fori(0, n // 4 - 1) as i:
                    for k2 in range(4):
                        ahead_high(act, Unit(first + 4 + k2, i), UNITS)
                        if k2 % 2 == 0:
                            act.wait_ge(unit_done, Unit(first + 4 + k2, i).count(1))
                            act.wait_ge(hid_ready, base + 2 * i + 2 + k2 // 2 - 1)
                            A(gate[:, 2 * k2:2 * k2 + 2, :].rearrange("p a t -> p (a t)"), L[:, k2, :],
                              ACT.Silu).then_inc(up_act, 1)
                for j in range(n // 4 * 4, n):
                    step(Unit(first + j), j, j % 4)
                k = NEXT_NORM.get(pre)
                if k is None:
                    linear(pre + "ffn_down", None)
                else:
                    linear(pre + "ffn_down", None, {8: lambda: squares_of(k, hx if pre == "c0" else hc), 9: lambda: root_of(k),
                                                    10: lambda: highs_of(k, shift_of[k])})

            rows_m = m[:, :, :].rearrange("p a t -> p (a t)").rearrange("p (a n) -> p a n", a=2)
            shift_of = {NORM_OF[p]: (lambda c, l=l, s=s: mod[:, l, s * 48 + c:s * 48 + c + 1]) for p, l, s in PASSES}
            feed_forward("", hx, lambda c: flat[:, 0:1])
            for num, (p, l, s) in enumerate(PASSES):
                h = hc if s else hx
                own = 2 if s else 0
                full, nf, rx = p != "c1", FULL_OF.get(p), ROPE_OF.get(p)
                kk = T if s else 0
                ch = slice(0, HC + 1) if full else slice(HC, HC + 1)

                def doubled_out(num):
                    at = T * PASSES[num][2]
                    act.wait_ge(kd_dup, num + 1)
                    A(kdup[:, :, at:at + T], M[:, 2, :].rearrange("p (h t) -> p h t", h=2), ACT.Copy).then_inc(kd_dupc, 1)

                if full:
                    act.dma_start(dft256, consts["dft256"].rearrange("p (s l k) -> p s l k", s=2, l=2)).then_inc(dft_in, 16)
                    conv_mid = conv_in[:, :, PAD:PAD + T]
                    act.wait_ge(conv_a, 2 * nf + 1)
                    beside = {0: lambda: squares_of(5, hx), 1: lambda: root_of(5)} if p == "c0" else {}
                    linear(p + "conv_u", lambda j, k, u: A(conv_mid[:, 2 * j:2 * j + 2, :],
                                                           L[:, k % 4, :].rearrange("p (a t) -> p a t", a=2), ACT.Copy), beside)
                    out_to(p + "conv_g", t1, ACT.Sigmoid, beside={0: lambda: doubled_out(num - 1)} if p == "x1" else {})
                    out_to(p + "four", oT)
                    out_to(p + "q", qk)
                    act.wait_ge(four1, nf + 1)
                    act.wait_ge(conv_a, 2 * nf + 2)
                    for c in range(HC):
                        A(y1[:, c, :, :].rearrange("p a k -> p (a k)"), M[:, c, :], ACT.Copy).then_inc(four1c, 1)

                def kv_out(j, k, u):
                    A(qk[:, HC, :], L[:, k, 0:T], ACT.Copy)
                    return A(oT[:, 0, :], L[:, k, T:2 * T], ACT.Copy)
                linear(p + "kv", kv_out, {} if full else {0: lambda: squares_of(10, hx)})

                def fourier_out():
                    act.wait_ge(four2, nf + 1)
                    for b in range(2):
                        A(b_high[:, 2 * b:2 * b + 2, :].rearrange("p a t -> p (a t)"), M[:, b, :], ACT.Copy).then_inc(z_ready, 1)

                def squares():
                    evacuated(act, p + "kv")
                    A(t2[:, ch, :], qk[:, ch, :], ACT.Square).then_inc(qk_sq, 1)

                def roots():
                    act.wait_ge(qk_ms, num + 1)
                    A(t2[:, ch, :], t2[:, ch, :], ACT.Sqrt).then_inc(qk_root, 1)

                if full:
                    out_to(p + "dq", dq, scale=HEAD ** -0.5,
                           beside={0: fourier_out, 1: squares})
                beside = {1: roots} if full else {0: lambda: root_of(10), 1: squares}
                if s:
                    linear(p + "dk", lambda j, k, u: A(kdT[:, 2 * j:2 * j + 2, kk:kk + T],
                                                       L[:, k % 4, :].rearrange("p (a t) -> p a t", a=2), ACT.Copy), beside)
                else:
                    out_to(p + "dk", t1, beside=beside)
                linear(p + "dv", lambda j, k, u: A(vdrow[:, own:own + 2, j * T:(j + 1) * T],
                                                   L[:, k % 4, :].rearrange("p (a n) -> p a n", a=2), ACT.Copy),
                       {} if full else {1: roots})
                evacuated(act, p + "dv")
                if not full:
                    multiplied(act, p + "dv")
                    highs_of(10, shift_of[10])
                    continue

                def branch(i, gate_beside={}, proj_beside={}, start=0):
                    act.wait_ge(merged, 8 + 16 * nf + 4 * i)
                    if start:
                        for k in range(start):
                            act.wait_ge(bank_free[k], after(p + f"gate{i}", k))
                        A(gate[:, 0:2 * start, :], gate[:, 0:2 * start, :], ACT.Sigmoid).then_inc(gate_ready, 1)
                    out_to(p + f"gate{i}", gate, ACT.Sigmoid, beside=gate_beside, start=start)
                    linear(p + f"proj{i}", None, proj_beside)

                def conv_squares():
                    act.wait_ge(conv_n, 3 * nf + 1)
                    A(t2[:, 0:HC, :], acc, ACT.Square).then_inc(conv_st, 1)

                def conv_sqrt():
                    act.wait_ge(conv_n, 3 * nf + 2)
                    A(rstd[:, :], rstd[:, :], ACT.Sqrt).then_inc(conv_root, 1)

                def conv_silu():
                    act.wait_ge(conv_n, 3 * nf + 3)
                    multiplied(act, p + "proj0")
                    for c in range(HC):
                        A(acc[:, c, :], acc[:, c, :], ACT.Silu, bias=col("conv_ln_b_2", 4 * l + c)).then_inc(conv_sig, 1)
                    act.wait_ge(conv_sig, 4 * (nf + 1))
                    A(b_high[:, :, :], acc, ACT.Copy).then_inc(z_ready, 1)

                branch(0, proj_beside={0: conv_squares, 1: conv_sqrt})
                branch(1, gate_beside={0: conv_silu, 3: lambda: doubled_out(num)})
                act.wait_ge(kd_dupc, num + 1)
                act.wait_ge(v_ready, num + 1)
                if rx is not None:
                    act.wait_ge(d_rot, 3 * rx + 3)
                attention(p + "gqa", 8 + 16 * nf + 8)
                act.wait_ge(o_ready, NHEADS[p + "gqa"])
                multiplied(act, p + "proj1")
                A(b_high[:, :, :], oT, ACT.Copy).then_inc(z_ready, 1)
                branch(2, start=BESIDE["gqa"][1])
                attention(p + "diff", 8 + 16 * nf + 12)
                act.wait_ge(o_ready, NHEADS[p + "diff"])
                A(t1[:, 0:HC, :], oT, ACT.Square).then_inc(on_sq, 1)
                act.wait_ge(on_ms, nf + 1)
                A(t2[:, 0:HC, :], t2[:, 0:HC, :], ACT.Sqrt).then_inc(on_root, 1)
                act.wait_ge(on_ms, nf + 1)
                act.wait_ge(q_ready, nf + 1)
                multiplied(act, p + "proj2")
                A(b_high[:, :, :], oT, ACT.Copy).then_inc(z_ready, 1)
                branch(3, start=BESIDE["diff"][1])
                multiplied(act, p + "gate3")
                split_high_of(m, merged, 8 + 16 * nf + 12)
                linear(p + "out", None)
                feed_forward(p, h, lambda c: mod[:, l, s * 48 + 24 + c:s * 48 + 25 + c])
            norm(12, hx, None, split=False)
            for b in range(4):
                half, a = b // 2, b % 2
                act.wait_ge(turned_out, 4 + 8 + 1 + b + 1)
                act.dma_start(out[0, a * P:(a + 1) * P, half * HALF:(half + 1) * HALF],
                              gate[:, 2 * b:2 * b + 2, :].rearrange("p a t -> p (a t)")).then_inc(stored, 16)
            act.wait_ge(stored, 16 * 4)

        @block.vector
        def _(dve):
            V = nc.vector
            n = [0]

            def link(ins):
                n[0] += 1
                ins.then_inc(dve_step, 1)
                dve.wait_ge(dve_step, n[0])

            def linear(name, one=None, beside={}, start=0):
                def step(u, j, k):
                    ahead_rest(dve, u, last_of(name))
                    if one is not None:
                        dve.wait_ge(unit_done, u.count(1))
                        one(j, k, u)
                    if isinstance(j, int) and j in beside:
                        beside[j]()
                each_unit(dve, name, step, start)

            def mean_of(k):
                dve.wait_ge(sum_ready, k + 1)
                V.tensor_scalar(rstd[:, :], M[:, 0, 0:T], 1.0 / D, EPS, ALU.mult, ALU.add).then_inc(ms_ready, 1)

            def inverse_root(k):
                dve.wait_ge(root_ready, k + 1)
                link(V.reciprocal(rstd[:, :], rstd[:, :]))

            def scale_chunk(h, gain, c, dst=None):
                V.scalar_tensor_tensor((m if dst is None else dst)[:, c, :], h[:, c, :], gain(c), rstd[:, :],
                                       ALU.mult, ALU.mult).then_inc(scaled, 1)

            def scale_chunks(h, gain, c0=0, c1=DC, dst=None):
                for c in range(c0, c1):
                    scale_chunk(h, gain, c, dst)

            def rest_chunk(k, shift, c):
                dve.wait_ge(n_high_ready, NHIGH[k] + c + 1)
                V.scalar_tensor_tensor(n_rest[:, c, :], m[:, c, :], shift(c), n_high[:, c, :].bitcast(F32),
                                       ALU.add, ALU.subtract).then_inc(n_ready, 1)

            def rest_chunks(k, shift):
                for c in range(DC):
                    rest_chunk(k, shift, c)

            def norm(k, h, gain, shift, split=True, dst=None):
                mean_of(k)
                inverse_root(k)
                if not split:
                    scale_chunks(h, gain, dst=dst)
                    return
                for c in range(DC + 2):
                    if c < DC:
                        scale_chunk(h, gain, c)
                    if c >= 2:
                        rest_chunk(k, shift, c - 2)

            def turn_out(h, base):
                for b in range(4):
                    dve.wait_ge(turned, base + b + 1)
                    ins = V.tensor_copy(h[:, 2 * b:2 * b + 2, :].rearrange("p a t -> p (a t)"), M[:, b, :])
                    n[0] += 1
                    ins.then_inc(dve_step, 1)
                dve.wait_ge(dve_step, n[0])
                dve.sem_inc(h_ready, 1)

            def n_split(src, count):
                for b in range(4):
                    dve.wait_ge(n_high_ready, count + b + 1)
                    V.tensor_tensor(n_rest[:, 2 * b:2 * b + 2, :], src[:, 2 * b:2 * b + 2, :],
                                    n_high[:, 2 * b:2 * b + 2, :].bitcast(F32), ALU.subtract).then_inc(m_split, 1)

            def add_to_h(name, h, gain):
                def one(j, k, u):
                    for o in range(2):
                        ins = V.scalar_tensor_tensor(h[:, 2 * j + o, :], L[:, k % 4, o * T:(o + 1) * T], gain(2 * j + o),
                                                     h[:, 2 * j + o, :], ALU.mult, ALU.add)
                    ins.then_inc(bank_free[k % 4], 1)
                linear(name, one)
                evacuated(dve, name)
                dve.sem_inc(h_ready, 1)

            def merge_rows(name, first, beside={}):
                linear(name, beside=beside)
                dve.wait_ge(unit_done, FIRST[name] + COUNT[name])
                def pair(x, b):
                    return x[:, 2 * b:2 * b + 2, :].rearrange("p a t -> p (a t)")
                for b in range(5):
                    if b < 4:
                        V.tensor_tensor(pair(m if first else gate, b), pair(gate, b), L[:, b, :], ALU.mult).then_inc(bank_free[b], 1)
                    if b:
                        dve.wait_ge(bank_free[b - 1], after(name, b - 1))
                        if first:
                            dve.sem_inc(merged, 1)
                        else:
                            V.tensor_tensor(pair(m, b - 1), pair(m, b - 1), pair(gate, b - 1), ALU.add).then_inc(merged, 1)

            def attention(key, out_of, negl=None):
                nk = keys_of(key)[1]
                exps, (th, tr) = store_of(key)
                tasks = TASKS[key]

                def negative_max(x):
                    dve.wait_ge(scores, x["g"] + 1)
                    V.tensor_reduce(soft[:, x["g"] % 4, 0:1], score_bank[x["g"] % 2][:, 0:nk], AX.X, ALU.max,
                                    negate=True).then_inc(neg_max, 1)

                def normalise(i, x):
                    s = x["g"] % 4
                    e = exps[i % 3][:, 0:nk]
                    dve.wait_ge(expd, x["g"] + 1)
                    link(V.reciprocal(soft[:, s, 3:4], soft[:, s, 2:3]))
                    if negl is None:
                        V.tensor_scalar(e, e, soft[:, s, 3:4], None, ALU.mult).then_inc(probs, 1)
                    elif x["map"] == 0:
                        link(V.tensor_scalar(e, e, soft[:, s, 3:4], None, ALU.mult))
                    else:
                        first = exps[(i - 1) % 3][:, 0:nk]
                        link(V.tensor_scalar(soft[:, s, 1:2], soft[:, s, 3:4], negl, None, ALU.mult))
                        V.scalar_tensor_tensor(first, e, soft[:, s, 1:2], first, ALU.mult, ALU.add).then_inc(probs, 1)

                def turned_rest(x):
                    dve.wait_ge(probs_T_high, x["group"] + 1)
                    at = slice(x["qt"] * P, (x["qt"] + 1) * P)
                    V.tensor_tensor(tr[:, 0:nk // P, at], turned_bank[x["group"] % 2][:, 0:nk].rearrange("p (c q) -> p c q", q=P),
                                    th[:, 0:nk // P, at].bitcast(F32), ALU.subtract).then_inc(probs_T_rest, 1)

                def head_out(x):
                    dve.wait_ge(attended, x["head"] + 1)
                    out_of(x["h"], head_bank).then_inc(o_ready, 1)
                beside, n_beside = beside_of(key)
                negative_max(tasks[0])
                negative_max(tasks[1])
                for i, x in enumerate(tasks):
                    normalise(i, x)
                    if (key, i - 2) in END_OF:
                        head_out(tasks[i - 2])
                    if i and tasks[i - 1]["whole"]:
                        turned_rest(tasks[i - 1])
                    if i + 2 < len(tasks):
                        negative_max(tasks[i + 2])
                    if i % 4 == 1 and i // 4 < n_beside:
                        ahead_rest(dve, Unit(FIRST[beside] + i // 4), UNITS)
                turned_rest(tasks[-1])
                head_out(tasks[-1])

            dve.wait_ge(consts_in, 16 * 5)
            dve.wait_ge(turned, 1)
            V.tensor_copy(cols[:, :], M[:, 0, 0:NVEC]).then_inc(turned_out, 1)
            V.tensor_copy(cols2[:, :], M[:, 0, P:P + 6]).then_inc(turned_out, 1)
            V.tensor_copy(tapc[:, :, :], M[:, 1, 0:2 * P].rearrange("p (l k) -> p l k", l=2)[:, :, 0:TAPS * HC]).then_inc(turned_out, 1)
            V.tensor_copy(b_ada[:, :, :], M[:, 1, 256:352].rearrange("p (l k) -> p l k", l=2)).then_inc(turned_out, 1)
            dve.wait_ge(lam_in, 16 * 4 * LAYERS)
            flat_m = m[:, :, :].rearrange("p a t -> p (a t)")
            for l in range(LAYERS):
                for i in range(2):
                    a, b = (flat_m[:, 512 + (4 * l + 2 * i + k) * HEAD:512 + (4 * l + 2 * i + k + 1) * HEAD] for k in range(2))
                    V.tensor_tensor_reduce(a, a, b, 1.0, 0.0, ALU.mult, ALU.add, lam[:, l, i:i + 1]).then_inc(lam_dot, 1)
            dve.wait_ge(lam_exp, 1)
            for l in range(LAYERS):
                link(V.tensor_tensor(lam[:, l, 4:5], lam[:, l, 3:4], lam[:, l, 2:3], ALU.subtract))
                link(V.tensor_scalar(lam[:, l, 5:6], lam[:, l, 4:5], -LAM_INIT[l], None, ALU.add))
                link(V.tensor_scalar(lam[:, l, 6:7], cols2[:, l:l + 1], 1.0 - LAM_INIT[l], None, ALU.mult))
                link(V.tensor_scalar(lam[:, l, 7:8], cols2[:, 2 + l:3 + l], HEAD ** -0.5, None, ALU.mult))
            R = lambda i: rows[:, i, :]
            dve.wait_ge(s5_act, 1)
            for g in range(2):
                sl = slice(g * STATE, (g + 1) * STATE)
                for i in range(2):
                    link(V.tensor_scalar(rows[:, 3 + i, sl], rows[:, i, sl], rows[:, 2, g:g + 1], None, ALU.mult))
            big = 1.5 * 2.0 ** 23
            C1, C2 = 6.28125, 0.0019350051879882812
            C3 = float(2 * np.pi - C1 - C2)
            link(V.tensor_scalar(R(5), R(4), 1.0 / (2 * np.pi), big, ALU.mult, ALU.add))
            link(V.tensor_scalar(R(5), R(5), -big, None, ALU.add))
            link(V.scalar_tensor_tensor(R(6), R(5), -C1, R(4), ALU.mult, ALU.add))
            link(V.scalar_tensor_tensor(R(7), R(5), -C2, R(6), ALU.mult, ALU.add))
            link(V.scalar_tensor_tensor(R(6), R(5), -C3, R(7), ALU.mult, ALU.add))
            V.tensor_scalar(R(7), R(6), 3.1415925, -3.1415925, ALU.min, ALU.max).then_inc(s5_act_in, 1)
            turn_out(hc, 1)
            split_rest(dve, Unit(0))
            dve.wait_ge(s5_act, 4)
            link(V.tensor_scalar(R(5), R(10), -1.0, 1.0, ALU.mult, ALU.add))
            link(V.reciprocal(R(5), R(5)))
            link(V.scalar_tensor_tensor(R(6), R(10), 2.0, R(5), ALU.mult, ALU.mult))
            link(V.tensor_scalar(R(11), R(6), 1.0, None, ALU.add))
            link(V.scalar_tensor_tensor(R(7), R(9), -2.0, R(9), ALU.mult, ALU.mult))
            link(V.tensor_scalar(R(12), R(7), 1.0, None, ALU.add))
            link(V.tensor_copy(R(13), R(8)))
            link(V.tensor_tensor(R(5), R(6), R(12), ALU.mult))
            link(V.tensor_tensor(R(5), R(5), R(7), ALU.add))
            link(V.tensor_tensor(R(6), R(11), R(13), ALU.mult))
            link(V.tensor_tensor(R(7), R(0), R(0), ALU.mult))
            link(V.tensor_tensor(R(9), R(1), R(1), ALU.mult))
            link(V.tensor_tensor(R(7), R(7), R(9), ALU.add))
            link(V.reciprocal(R(7), R(7)))
            link(V.tensor_tensor(R(9), R(5), R(0), ALU.mult))
            link(V.tensor_tensor(R(10), R(6), R(1), ALU.mult))
            link(V.tensor_tensor(R(9), R(9), R(10), ALU.add))
            link(V.tensor_tensor(R(14), R(9), R(7), ALU.mult))
            link(V.tensor_tensor(R(9), R(6), R(0), ALU.mult))
            link(V.tensor_tensor(R(10), R(5), R(1), ALU.mult))
            link(V.tensor_tensor(R(9), R(9), R(10), ALU.subtract))
            V.tensor_tensor(R(15), R(9), R(7), ALU.mult).then_inc(s5_coef_rows, 1)
            norm(0, hc, lambda c: col("mem_norm_g", c), lambda c: flat[:, 0:1])
            dve.wait_ge(s5_bt, 1)
            V.tensor_copy(s5c, M[:, 0, 0:5 * TILES].rearrange("p (i n) -> p i n", i=5)).then_inc(s5_coef, 1)
            dve.wait_ge(s5_coef, 1)
            cr, ci = (s5c[:, 3 + i, :].unsqueeze(2).to_broadcast((P, TILES, CH)) for i in range(2))

            def bbar_part(i):
                x, y, op = (((cr, 0), (ci, 1), ALU.subtract), ((cr, 1), (ci, 0), ALU.add))[i]
                link(V.tensor_tensor(bbar[:, i], braw[:, x[1]], x[0], ALU.mult))
                link(V.tensor_tensor(btmp, braw[:, y[1]], y[0], ALU.mult))
                link(V.tensor_tensor(bbar[:, i], bbar[:, i], btmp, op))

            def zero_blocks():
                dve.wait_ge(n_ready, DC)
                link(V.memset(bblk[0:STATE, :, :, 1, :], 0.0))
                link(V.memset(bblk[STATE:P, :, :, 0, :], 0.0))

            def fill_blocks():
                for i in range(2):
                    V.tensor_copy(bblk[0:STATE, i, :, 0, :], bbar[0:STATE, i]).then_inc(s5_blk, 1)
                    V.tensor_copy(bblk[STATE:P, i, :, 1, :], bbar[STATE:P, i]).then_inc(s5_blk, 1)
                    for g in range(2):
                        V.tensor_scalar(cblk[:, i, :, g, :], craw[:, i, :, :], masks[:, 2 * i + g:2 * i + g + 1], None,
                                        ALU.mult).then_inc(s5_blk, 1)

            linear("mem_k", beside={0: lambda: bbar_part(0), 1: lambda: bbar_part(1), 2: zero_blocks, 3: fill_blocks})
            linear("mem_v")
            turn_out(hx, 5 + 8)
            norm(1, hx, lambda c: col("mix_norm_g", c), lambda c: flat[:, 0:1])
            linear("xa")
            evacuated(dve, "xa")
            V.tensor_copy(xaR, xaT[:, :, ::-1]).then_inc(xa_ready, 1)

            dve.wait_ge(turned_out, 4 + 8)

            def s5_result(b):
                d, c = (1 if b < 4 else 0), b % 4
                dve.wait_ge(s5_y, b + 1)
                res = L[:, 2 + b % 2, 0:T]
                if d:
                    V.tensor_copy(yT[:, c, :], res[:, ::-1]).then_inc(s5_yout, 1)
                else:
                    link(V.tensor_tensor(yT[:, c, :], yT[:, c, :], res, ALU.add))
                    V.scalar_tensor_tensor(yT[:, c, :], xaT[:, c, :], col("s5_d", c), yT[:, c, :], ALU.mult,
                                           ALU.add).then_inc(s5_yout, 1)

            for b in range(8):
                tile = s5_tile(b)
                a0, a1, a2, a3 = zset[b % 2]
                dve.wait_ge(s5_tab, b + 1)
                dve.wait_ge(s5_bu, b + 1)
                c_, s_ = tab_c[b % 2], tab_s[b % 2]
                re, im = M[:, :, 0:T], M[:, :, T:2 * T]
                V.tensor_tensor(a0, c_, re, ALU.mult).then_inc(s5_rot, 1)
                V.tensor_tensor(z_re, s_, im, ALU.mult).then_inc(s5_rot, 1)
                V.tensor_tensor(a1, c_, im, ALU.mult).then_inc(s5_rot, 1)
                V.tensor_tensor(z_im, s_, re, ALU.mult).then_inc(s5_rot, 1)
                for x, z, op in ((a0, z_re, ALU.add), (a1, z_im, ALU.subtract)):
                    dve.wait_ge(s5_rot, 4 * b + 4)
                    V.tensor_tensor(x, x, z, op).then_inc(dve_step, 1)
                n[0] += 2
                for i, (src, dst) in enumerate(((a0, z_re), (a1, z_im))):
                    dve.wait_ge(dve_step, n[0])
                    for r in range(4):
                        V.tensor_tensor_scan(dst[:, r, :], s5c[:, 0, tile + r:tile + r + 1].to_broadcast((P, T)), src[:, r, :],
                                             0.0, ALU.mult, ALU.add).then_inc(s5_scan, 1)
                dve.wait_ge(s5_scan, 8 * b + 8)
                V.tensor_tensor(a0, c_, z_re, ALU.mult).then_inc(s5_w, 1)
                V.scalar_tensor_tensor(a1, s_, -1.0, z_im, ALU.mult, ALU.mult).then_inc(s5_w, 1)
                V.tensor_tensor(a2, s_, z_re, ALU.mult).then_inc(s5_w, 1)
                V.tensor_tensor(a3, c_, z_im, ALU.mult).then_inc(s5_w, 1)
                if b:
                    s5_result(b - 1)
                dve.wait_ge(s5_w, 4 * b + 4)
            s5_result(7)
            dve.wait_ge(turned, 1 + 8 + 8 + 1)
            for l in range(LAYERS):
                for s in range(2):
                    link(V.tensor_tensor(mod[:, l, s * 48:(s + 1) * 48], M[:, 0, l * P + s * 48:l * P + (s + 1) * 48], b_ada[:, l, :], ALU.add))
            for l in range(LAYERS):
                for s in range(2):
                    for i, (part, name) in enumerate(((1, "norm_mix_2"), (4, "norm_ffn_2"))):
                        at = s * 48 + part * 8
                        link(V.scalar_tensor_tensor(modg[:, l, s, i, :], mod[:, l, at:at + 8], 1.0, col(name, 8 * l, 8), ALU.add, ALU.mult))
            dve.sem_inc(mod_ready, 1)

            split_rest(dve, Unit(BEFORE_ADA))
            linear("zv")
            linear("zu")
            evacuated(dve, "zv")
            for a in range(2):
                link(V.tensor_reduce(stats[:, a, 0:1], zv[:, a, :], AX.X, ALU.add))
                link(V.tensor_scalar(stats[:, a, 1:2], stats[:, a, 0:1], -1.0 / D, None, ALU.mult))
                V.tensor_scalar(zv[:, a, :], zv[:, a, :], stats[:, a, 1:2], None, ALU.add).then_inc(ln_sum, 1)
            dve.wait_ge(ln_sq, 2)
            V.tensor_scalar(stats[:, :, 3], stats[:, :, 2], 1.0 / D, EPS, ALU.mult, ALU.add).then_inc(ln_sum, 1)
            dve.wait_ge(ln_root, 1)
            link(V.reciprocal(stats[:, :, 5], stats[:, :, 4]))
            dve.wait_ge(sgu_in, 16 * 4)
            lnv = m[:, :, :].rearrange("p a t -> p (a t)").rearrange("p (a n) -> p a n", a=2)
            for a in range(2):
                link(V.scalar_tensor_tensor(zv[:, a, :], zv[:, a, :], stats[:, a, 5:6], lnv[:, 0, :], ALU.mult, ALU.mult))
                V.tensor_tensor(zv[:, a, :], zv[:, a, :], lnv[:, 1, :], ALU.add).then_inc(ln_ready, 1)
            dve.wait_ge(sgu_mm, 1)
            evacuated(dve, "zu")
            for b in range(4):
                x = zu[:, 2 * b:2 * b + 2, :].rearrange("p a t -> p (a t)")
                V.tensor_tensor(x, x, M[:, b, :], ALU.mult).then_inc(sgu_out, 1)
            linear("gate_a")
            dve.wait_ge(glu_sig, 1)
            V.tensor_tensor(b_rest[:, :, :], yT, b_high[:, :, :].bitcast(F32), ALU.subtract).then_inc(branch_ready, 1)
            linear("glu")
            evacuated(dve, "glu")
            V.tensor_tensor(yT, yT, work[:, 5760:6784].rearrange("p (c t) -> p c t", c=HC), ALU.mult).then_inc(glu_sig, 1)
            dve.wait_ge(glu_sig, 3)
            V.tensor_tensor(b_rest[:, :, :], yT, b_high[:, :, :].bitcast(F32), ALU.subtract).then_inc(branch_ready, 1)
            dve.wait_ge(ln_ready, 2)
            evacuated(dve, "gate_a")
            merge_rows("proj_a", True)
            linear("gate_b")
            n_split(zu, NHIGH_EVENTS["yb"])

            def proj_b_out(j, k, u):
                g, mm_ = (x[:, 2 * j:2 * j + 2, :].rearrange("p a t -> p (a t)") for x in (gate, m))
                if j == 0:
                    evacuated(dve, "gate_b")
                V.tensor_tensor(g, g, L[:, k, :], ALU.mult).then_inc(bank_free[k], 1)
                dve.wait_ge(bank_free[k], after("proj_b", k))
                V.tensor_tensor(mm_, mm_, g, ALU.add).then_inc(merged, 1)
            linear("proj_b", proj_b_out)
            n_split(m[:, :, :], NHIGH_EVENTS["merged"])
            one = lambda c: flat[:, 1:2]
            zero = lambda c: flat[:, 0:1]
            add_to_h("out", hx, one)
            norm(2, hx, lambda c: col("xattn_norm_g", c), zero)
            linear("mem_q")
            attention("mem", lambda h, bank: V.tensor_copy(o_mem[:, 2 * h:2 * h + 2, :].rearrange("p a t -> p (a t)"), bank))
            n_split(o_mem, NHIGH_EVENTS["o_mem"])
            add_to_h("mem_o", hx, one)

            def feed_forward(pre, h, gain, shift, out_gain):
                norm(FFN_NORM[pre], h, gain, shift)
                first, cnt = FIRST[pre + "ffn_up"], COUNT[pre + "ffn_up"]
                base = FC // 2 * HID_OF[pre]
                steps = n[0]

                def pair(i, k2, gates, done):
                    sg = gate[:, 2 * k2 - 2:2 * k2, :].rearrange("p a t -> p (a t)")
                    hh = gate[:, 2 * k2:2 * k2 + 2, :].rearrange("p a t -> p (a t)")
                    at = 4 * i + (k2 - 1)
                    if isinstance(at, int):
                        hi_, re_ = (x[:, at:at + 2, :].rearrange("p a t -> p (a t)") for x in (hid_high, hid_rest))
                    else:
                        hi_, re_ = (x[:, bass.ds(at, 2), :].rearrange("p a t -> p (a t)") for x in (hid_high, hid_rest))
                    dve.wait_ge(up_act, gates)
                    V.tensor_tensor(hh, sg, L[:, k2, :], ALU.mult).then_inc(dve_step, 1)
                    dve.wait_ge(dve_step, done + 1)
                    V.tensor_copy(hi_, hh).then_inc(dve_step, 1)
                    dve.wait_ge(dve_step, done + 2)
                    V.tensor_tensor(re_, hh, hi_.bitcast(F32), ALU.subtract).then_inc(hid_ready, 1)
                    dve.sem_inc(bank_free[k2 - 1], 1)
                    dve.sem_inc(bank_free[k2], 1)

                def turn(i):
                    for k2 in range(4):
                        u = Unit(first + k2, i)
                        ahead_rest(dve, u, UNITS)
                        if k2 % 2:
                            dve.wait_ge(unit_done, u.count(1))
                            pair(i, k2, base + 2 * i + k2 // 2 + 1, steps + 4 * i + 2 * (k2 // 2))
                turns = cnt // 4
                with dve.Fori(0, turns) as i:
                    turn(i)
                n[0] += 4 * turns
                for k2 in range(cnt - 4 * turns):
                    u = Unit(first + 4 * turns + k2)
                    ahead_rest(dve, u, UNITS)
                    if k2 % 2:
                        dve.wait_ge(unit_done, u.count(1))
                        pair(turns, k2, base + 2 * turns + k2 // 2 + 1, n[0])
                        n[0] += 2
                name = pre + "ffn_down"
                if pre == "":
                    turn_out(hc, 1 + 8 + 8 + 1 + 1)
                next_ = NEXT_NORM.get(pre)
                if next_ is None:
                    linear(name)
                else:
                    p_ = [x for x in PASSES if NORM_OF[x[0]] == next_][0]
                    g_, s_ = mix_gain(*p_[1:]), mix_shift(*p_[1:])
                    linear(name, beside={8: lambda: (mean_of(next_), inverse_root(next_)),
                                         9: lambda: scale_chunks(hc if p_[2] else hx, g_),
                                         10: lambda: rest_chunks(next_, s_)})
                dve.wait_ge(unit_done, FIRST[name] + COUNT[name])
                for b in range(4):
                    for o in range(2):
                        ins = V.scalar_tensor_tensor(h[:, 2 * b + o, :], L[:, b, o * T:(o + 1) * T], out_gain(2 * b + o),
                                                     h[:, 2 * b + o, :], ALU.mult, ALU.add)
                    ins.then_inc(bank_free[b], 1)
                evacuated(dve, name)
                dve.sem_inc(h_ready, 1)

            def mix_gain(l, s):
                return lambda c: modg[:, l, s, 0, c:c + 1]

            def mix_shift(l, s):
                return lambda c: mod[:, l, s * 48 + c:s * 48 + c + 1]

            def last_gain(c):
                return col("final_norm_g", c)

            feed_forward("", hx, lambda c: col("ffn_norm_g", c), zero, one)
            for num, (p, l, s) in enumerate(PASSES):
                h = hc if s else hx
                own, kk = (2, T) if s else (0, 0)
                full, nf, rx = p != "c1", FULL_OF.get(p), ROPE_OF.get(p)
                def b_split(src):
                    V.tensor_tensor(b_rest[:, :, :], src, b_high[:, :, :].bitcast(F32), ALU.subtract).then_inc(branch_ready, 1)
                def v_out():
                    dve.wait_ge(k_ready, num + 1)
                    V.tensor_copy(vrow[:, own:own + 2, :], M[:, 3, 0:T].rearrange("p (a n) -> p a n", a=2)).then_inc(v_ready, 1)

                banks = ((0, 0, 2), (1, 2, 2), (2, 4, 1)) if full else ((2, 4, 1),)

                def mean_squares():
                    dve.wait_ge(qk_sum, num + 1)
                    for b, c0, w in banks:
                        link(V.tensor_scalar(t2[:, c0:c0 + w, :].rearrange("p a t -> p (a t)"), M[:, b, 0:w * T], 1.0 / HEAD, EPS, ALU.mult, ALU.add))
                    dve.sem_inc(qk_ms, 1)

                def normed(c):
                    dve.wait_ge(qk_root, num + 1)
                    link(V.reciprocal(t2[:, c, :], t2[:, c, :]))
                    g = lam[:, l, 7:8] if c < HC else cols2[:, 4 + l:5 + l]
                    link(V.scalar_tensor_tensor(qk[:, c, :], qk[:, c, :], g, t2[:, c, :], ALU.mult, ALU.mult))

                def k_normed():
                    normed(HC)
                    dve.sem_inc(qk_n, 1)

                if not full:
                    linear(p + "kv")
                    linear(p + "dk", beside={0: lambda: mean_of(10), 1: lambda: (v_out(), inverse_root(10))})
                    linear(p + "dv", beside={0: lambda: scale_chunks(hx, mix_gain(1, 0)), 1: mean_squares})
                    rest_chunks(10, mix_shift(1, 0))
                    k_normed()
                    continue

                def taps(k0, n_):
                    with dve.Fori(k0, k0 + n_) as k:
                        for c in range(DVE_CHUNKS):
                            dve.wait_ge(conv_step, CONV_STEPS * nf + HC + DVE_CHUNKS * (k - 2) + c + 1)
                            V.scalar_tensor_tensor(acc[:, c, :], conv_in[:, c, bass.ds(k, T)], tapc[:, l, bass.ds(4 * k + c, 1)], acc[:, c, :],
                                                   ALU.mult, ALU.add).then_inc(conv_step, 1)

                def last_norm():
                    normed(3)
                    dve.sem_inc(qk_n, 1)

                def last_taps():
                    taps(28, 3)
                    dve.wait_ge(conv_step, CONV_STEPS * (nf + 1))
                    dve.sem_inc(conv_st, 1)

                def fourier_split():
                    dve.wait_ge(z_ready, 5 * nf + 2)
                    b_split(M[:, 0:2, :].rearrange("p b (c t) -> p (b c) t", c=2))

                def bc(i, w):
                    return rope[:, i, :].unsqueeze(1).to_broadcast((P, w, T))

                def rotate_q():
                    dve.wait_ge(consts_in, 16 * 7)
                    dve.wait_ge(qk_rot, 3 * rx + 1)
                    for b, c0, w in banks:
                        link(V.tensor_tensor(t2[:, c0:c0 + w, :], M[:, b, 0:w * T].rearrange("p (a t) -> p a t", a=w), bc(1, w), ALU.mult))
                    link(V.tensor_tensor(qk, qk, bc(0, 5), ALU.mult))

                def rotated_q():
                    V.tensor_tensor(qk, qk, t2, ALU.add).then_inc(d_rot, 1)

                def rotate_d(i, src, dst):
                    dve.wait_ge(qk_rot, 3 * rx + 2 + i)
                    dve.wait_ge(d_rot, 3 * rx + 1 + i)
                    rot = M[:, 2 * i:2 * i + 2, :].rearrange("p b (c t) -> p (b c) t", c=2)
                    link(V.tensor_tensor(t2[:, 0:HC, :], rot, bc(1, HC), ALU.mult))
                    link(V.tensor_tensor(src, src, bc(0, HC), ALU.mult))
                    V.tensor_tensor(dst, src, t2[:, 0:HC, :], ALU.add).then_inc(d_rot, 1)

                def conv_centre():
                    dve.wait_ge(conv_stc, 2 * nf + 1)
                    link(V.tensor_scalar(rstd[:, :], M[:, 3, 0:T], -1.0 / HALF, None, ALU.mult))
                    link(V.tensor_tensor(acc, acc, rstd[:, :].unsqueeze(1).to_broadcast((P, HC, T)), ALU.add))
                    dve.sem_inc(conv_n, 1)

                def conv_mean_square():
                    dve.wait_ge(conv_stc, 2 * nf + 2)
                    V.tensor_scalar(rstd[:, :], M[:, 3, T:2 * T], 1.0 / HALF, LN_EPS, ALU.mult, ALU.add).then_inc(conv_n, 1)

                def conv_scale():
                    dve.wait_ge(conv_root, nf + 1)
                    link(V.reciprocal(rstd[:, :], rstd[:, :]))
                    for c in range(HC):
                        link(V.scalar_tensor_tensor(acc[:, c, :], acc[:, c, :], col("conv_ln_g_2", 4 * l + c), rstd[:, :], ALU.mult, ALU.mult))
                    dve.sem_inc(conv_n, 1)

                def conv_split():
                    dve.wait_ge(z_ready, 5 * nf + 3)
                    b_split(acc)

                link(V.memset(conv_in[:, :, 0:PAD], 0.0))
                V.memset(conv_in[:, :, PAD + T:2 * PAD + T], 0.0).then_inc(conv_a, 1)
                if p == "c0":
                    linear(p + "conv_u", beside={1: lambda: mean_of(5)})
                    linear(p + "conv_g", beside={0: lambda: (inverse_root(5), scale_chunks(hx, last_gain, 0, 3, hx)),
                                                 1: lambda: scale_chunks(hx, last_gain, 3, DC, hx)})
                    dve.wait_ge(scaled, SCALED[5] + DC)
                    dve.sem_inc(h_ready, 1)
                else:
                    linear(p + "conv_u")
                    linear(p + "conv_g")
                evacuated(dve, p + "conv_g")
                mid = conv_in[:, :, PAD:PAD + T]
                V.tensor_tensor(mid, mid, t1[:, 0:HC, :], ALU.mult).then_inc(conv_a, 1)
                dve.wait_ge(conv_a, 2 * nf + 2)
                for c in range(HC):
                    V.tensor_scalar(acc[:, c, :], conv_in[:, c, 0:T], tapc[:, l, c:c + 1], col("conv_b_2", 4 * l + c),
                                    ALU.mult, ALU.add).then_inc(conv_step, 1)
                linear(p + "four", beside={0: lambda: taps(1, 3), 1: lambda: taps(4, 3)})
                linear(p + "q", beside={0: lambda: taps(7, 3), 1: lambda: taps(10, 3)})
                linear(p + "kv", beside={0: lambda: taps(13, 4)})
                linear(p + "dq", beside={0: lambda: taps(17, 4), 1: lambda: (v_out(), taps(21, 4))})
                linear(p + "dk", beside={0: lambda: (fourier_split(), taps(25, 3)), 1: mean_squares})
                linear(p + "dv", beside={0: lambda: normed(HC), 1: lambda: normed(0)})
                evacuated(dve, p + "dv")

                def gl(i, gate_beside={}, proj_beside={}, start=0):
                    linear(p + f"gate{i}", beside=gate_beside, start=start)
                    evacuated(dve, p + f"gate{i}")
                    if start:
                        dve.wait_ge(gate_ready, 2 * nf + i - 1)
                    merge_rows(p + f"proj{i}", i == 0, proj_beside)
                gl(0, {0: lambda: normed(1), 1: lambda: normed(2), 2: last_norm, 3: last_taps},
                   {0: conv_centre, 1: conv_mean_square})
                if rx is None:
                    gl(1, {0: conv_scale, 2: conv_split})
                else:
                    gl(1, {0: conv_scale, 1: rotate_q, 2: lambda: (rotated_q(), conv_split()), 3: lambda: rotate_d(0, dq, dq)},
                       {1: lambda: rotate_d(1, t1[:, 0:HC, :], kdT[:, :, 0:T])})

                def gqa_out(h_, bank):
                    a = HEAD * (h_ % 2)
                    return V.tensor_copy(oT[a:a + HEAD, h_ // 2, :], bank[0:HEAD, 0:T])
                attention(p + "gqa", gqa_out)
                dve.wait_ge(z_ready, 5 * nf + 4)
                b_split(oT)
                gl(2, start=BESIDE["gqa"][1])
                attention(p + "diff", lambda h_, bank: V.tensor_copy(oT[:, h_, :], bank[:, 0:T]), negl=lam[:, l, 5:6])
                dve.wait_ge(on_sum, nf + 1)
                for b in range(2):
                    link(V.tensor_scalar(t2[:, 2 * b:2 * b + 2, :].rearrange("p a t -> p (a t)"), M[:, b, :], 1.0 / P, EPS, ALU.mult, ALU.add))
                dve.sem_inc(on_ms, 1)

                def head_normed(c):
                    dve.wait_ge(on_root, nf + 1)
                    link(V.reciprocal(t2[:, c:c + 2, :], t2[:, c:c + 2, :]))
                    link(V.scalar_tensor_tensor(oT[:, c:c + 2, :], oT[:, c:c + 2, :], lam[:, l, 6:7], t2[:, c:c + 2, :], ALU.mult, ALU.mult))

                def heads_split():
                    head_normed(2)
                    dve.sem_inc(q_ready, 1)
                    dve.wait_ge(z_ready, 5 * nf + 5)
                    b_split(oT)
                gl(3, {2: lambda: head_normed(0), 3: heads_split}, start=BESIDE["diff"][1])
                n_split(m[:, :, :], NHIGH_EVENTS[p])
                add_to_h(p + "out", h, lambda c: mod[:, l, s * 48 + 16 + c:s * 48 + 17 + c])
                feed_forward(p, h, lambda c: modg[:, l, s, 1, c:c + 1],
                             lambda c: mod[:, l, s * 48 + 24 + c:s * 48 + 25 + c],
                             lambda c: mod[:, l, s * 48 + 40 + c:s * 48 + 41 + c])
            norm(12, hx, lambda c: col("final_norm_2", c), None, split=False)
            for b in range(4):
                dve.wait_ge(turned, 1 + 8 + 8 + 1 + 1 + 4 + b + 1)
                V.tensor_copy(gate[:, 2 * b:2 * b + 2, :].rearrange("p a t -> p (a t)"), M[:, b, :]).then_inc(turned_out, 1)


_INS = [
    "x", "mem", "mix_norm_g", "w_in", "s5_lam_re", "s5_lam_im", "s5_log_step", "s5_b_re", "s5_b_im", "s5_c_re",
    "s5_c_im", "s5_d", "s5_w_glu", "sgu_ln_g", "sgu_ln_b", "sgu_w", "sgu_bias", "w_proj_a", "w_proj_b", "w_out",
    "xattn_norm_g", "mem_norm_g", "w_q", "w_k", "w_v", "w_xo", "ffn_norm_g", "w_gate", "w_up", "w_down",
    "final_norm_g", "c_2", "ctx_2", "c_ctx_2", "w_ada_2", "b_ada_2", "norm_mix_2", "w_in_2", "w_four_2", "conv_w_2",
    "conv_b_2", "conv_ln_g_2", "conv_ln_b_2", "w_conv_2", "q_norm_2", "k_norm_2", "w_gqa_2", "lam_q1_2",
    "lam_k1_2", "lam_q2_2", "lam_k2_2", "diff_norm_2", "w_diff_2", "w_out_2", "norm_ffn_2", "w_ffn1_2",
    "w_ffn3_2", "w_ffn2_2", "final_norm_2",
]


def shape_constants():
    f = np.float32
    i, j = np.arange(P)[:, None], np.arange(P)[None, :]
    same64 = i // HEAD == j // HEAD
    ang64 = 2 * np.pi * ((i % HEAD) * (j % HEAD) % HEAD) / HEAD
    dft64 = np.concatenate([np.where(same64, np.cos(ang64), 0), np.where(same64, -np.sin(ang64), 0)], 1) / 8
    l, k = np.arange(T)[:, None], np.arange(T)[None, :]
    ang = 2 * np.pi * (l * k % T) / T
    dft256 = np.stack([np.cos(ang), np.sin(ang)]) / 16
    dft256 = dft256.reshape(2, 2, P, T).transpose(2, 0, 1, 3).reshape(P, -1)
    half = HEAD // 2
    inv = (f(10000.0) ** (-np.arange(0, half, 2, dtype=f) / f(half))).astype(f)
    tok = np.arange(T)
    angles = np.concatenate([(tok // 64).astype(f)[:, None] * inv, (tok % 64).astype(f)[:, None] * inv], 1).astype(f)
    angles = angles.astype(np.float64)[:, np.arange(P) % half].T
    rope = np.concatenate([np.cos(angles), np.sin(angles)], 1)
    a, b = np.arange(P) % HEAD, np.arange(P)
    swap = np.zeros((P, P))
    for c in range(P):
        swap[c + half if a[c] < half else c - half, c] = -1 if a[c] < half else 1
    dup = np.concatenate([(i == j % HEAD) * 1.0, (i == HEAD + j % HEAD) * 1.0], 1)
    even = (np.arange(P) // CH) % 2 == 0
    masks = np.stack([even * 1.0, ~even * 1.0, even * -1.0, ~even * -1.0], 1)
    out = dict(ident=np.eye(P), dft64=dft64, dft256=dft256, rope=rope, swap=swap, dup=dup, pair_ones=same64 * 1.0, masks=masks)
    return {k: np.ascontiguousarray(v).astype(f) for k, v in out.items()}


def kernel(**inputs):
    import concourse.bacc as _bacc
    from concourse.bass_utils import run_bass_kernel_spmd as _run

    nc = _bacc.Bacc("TRN2", target_bir_lowering=False, num_devices=1)
    arrays, t, consts = {}, {}, {}
    for name in _INS:
        a = np.ascontiguousarray(inputs[name])
        arrays[f"in_{name}"] = a
        t[name] = nc.dram_tensor(f"in_{name}", a.shape, mybir.dt.from_np(a.dtype), kind="ExternalInput").ap()
    for name, a in shape_constants().items():
        arrays[f"const_{name}"] = a
        consts[name] = nc.dram_tensor(f"const_{name}", a.shape, mybir.dt.from_np(a.dtype), kind="ExternalInput").ap()
    out = nc.dram_tensor("out_0", (1, T, D), F32, kind="ExternalOutput").ap()
    build(nc, t, out, consts)
    r = _run(nc, [arrays], core_ids=[0])
    return r.results[0]["out_0"]
```
